# Optimizing a Trainium2 kernel written in Bass

```python
import math
import jax
import jax.numpy as jnp
from jax import lax
import numpy as np

D_MODEL = 1024
BATCH = 1
SEQ = 1024
DEPTH = 1
DEC_BATCH = 8
DEC_SEQ = 16
PAST_LEN = 256

CHUNK = 64
N_META = 16
Q_BLOCK = 128
RWKV_HEAD_DIM = 64
RWKV_WIDTH = D_MODEL // 2
RWKV_HEADS = RWKV_WIDTH // RWKV_HEAD_DIM
DECAY_LORA = 64
AAA_LORA = 64
GATE_LORA = 128
DECAY_SCALE = 0.6065306597126334
V_HEAD = 64
MLA_WIDTH = D_MODEL - RWKV_WIDTH
MLA_HEADS = MLA_WIDTH // V_HEAD
Q_LORA = 384
KV_LORA = 256
QK_NOPE = 64
QK_ROPE = 32
ATTN_SCALE = (QK_NOPE + QK_ROPE) ** -0.5
ROPE_THETA = 10000.0
MIX_WIDTH = RWKV_WIDTH + MLA_WIDTH
C_RWKV = 3 * RWKV_WIDTH + DECAY_LORA + AAA_LORA + GATE_LORA
C_MLA = Q_LORA + KV_LORA + QK_ROPE
C_IN = C_RWKV + C_MLA
D_FF = 4 * D_MODEL
LN_EPS = 1e-5
RMS_EPS = 1e-6
GN_EPS = 64e-5
DEEPNORM_ALPHA = (2.0 * DEPTH) ** 0.25
DEEPNORM_BETA = (8.0 * DEPTH) ** -0.25
NEG_INF = -1e30

kernel_name = 'hymba_rwkv7_mla_streaming_encoder_step'

def _layernorm(x, g, b):
    xf = x.astype(jnp.float32)
    mu = jnp.mean(xf, -1, keepdims=True)
    var = jnp.mean(jnp.square(xf - mu), -1, keepdims=True)
    return ((xf - mu) * lax.rsqrt(var + LN_EPS) * g + b).astype(x.dtype)

def _rmsnorm(x, g):
    xf = x.astype(jnp.float32)
    return (xf * lax.rsqrt(jnp.mean(xf * xf, -1, keepdims=True) + RMS_EPS) * g).astype(x.dtype)

def _rope_tables(pos):
    inv = ROPE_THETA ** (-jnp.arange(0, QK_ROPE, 2, dtype=jnp.float32) / QK_ROPE)
    ang = pos.astype(jnp.float32)[:, None] * inv[None, :]
    return jnp.cos(ang), jnp.sin(ang)

def _rope(x, cos, sin):
    half = QK_ROPE // 2
    x1, x2 = x[..., :half], x[..., half:]
    return jnp.concatenate([x1 * cos - x2 * sin, x1 * sin + x2 * cos], axis=-1).astype(x.dtype)

def _project(xn, shift_prev, w_in, mu_shift):
    p = jnp.einsum('bld,dc->blc', xn, w_in)
    pr, pm = p[..., :C_RWKV], p[..., C_RWKV:]
    prev = jnp.concatenate([shift_prev.astype(pr.dtype), pr[:, :-1]], axis=1)
    return pr + mu_shift * (prev - pr), pm, pr[:, -1:]

def _rwkv7(pr_s, s0, w_decay_up, decay_base, w_aaa_up, aaa_base, w_gate_up, k_k, k_a, r_k, gn_g, gn_b):
    f32 = jnp.float32
    p = pr_s.astype(f32)
    b, l, _ = p.shape
    W = RWKV_WIDTH
    o_ad = 3 * W + DECAY_LORA
    o_gd = o_ad + AAA_LORA
    r, k, v = p[..., :W], p[..., W:2 * W], p[..., 2 * W:3 * W]
    wd, ad, gd = p[..., 3 * W:o_ad], p[..., o_ad:o_gd], p[..., o_gd:]
    w = jnp.exp(-DECAY_SCALE * jax.nn.sigmoid(decay_base + jnp.tanh(wd) @ w_decay_up))
    a = jax.nn.sigmoid(aaa_base + ad @ w_aaa_up)
    g = jax.nn.sigmoid(gd) @ w_gate_up
    heads = lambda t: t.reshape(b, l, RWKV_HEADS, RWKV_HEAD_DIM)
    kk = heads(k * k_k)
    kk = kk / jnp.maximum(jnp.sqrt(jnp.sum(kk * kk, -1, keepdims=True)), 1e-12)
    kt = k * (1.0 + (a - 1.0) * k_a)
    tm = lambda t: jnp.moveaxis(t, 1, 0)
    xs = (tm(heads(r)), tm(heads(w)), tm(heads(kt)), tm(heads(v)), tm(kk), tm(heads(a)))

    def step(S, inp):
        r_t, w_t, k_t, v_t, kk_t, a_t = inp
        sa = jnp.einsum('bhij,bhj->bhi', S, -kk_t)
        S = S * w_t[..., None, :] + sa[..., :, None] * (kk_t * a_t)[..., None, :] + v_t[..., :, None] * k_t[..., None, :]
        return S, jnp.einsum('bhij,bhj->bhi', S, r_t)

    S, ys = lax.scan(step, s0.astype(f32), xs)
    y = jnp.moveaxis(ys, 0, 1)
    mu = jnp.mean(y, -1, keepdims=True)
    var = jnp.mean(jnp.square(y - mu), -1, keepdims=True)
    yn = ((y - mu) * lax.rsqrt(var + GN_EPS)).reshape(b, l, W) * gn_g + gn_b
    bonus = (jnp.sum(heads(r * kt * r_k), -1, keepdims=True) * heads(v)).reshape(b, l, W)
    return ((yn + bonus) * g).astype(pr_s.dtype), S

def _mla_q(pm, q_norm_g, w_qb, cos, sin):
    b, l, _ = pm.shape
    q = jnp.einsum('blr,rc->blc', _rmsnorm(pm[..., :Q_LORA], q_norm_g), w_qb)
    q = q.reshape(b, l, MLA_HEADS, QK_NOPE + QK_ROPE)
    return q[..., :QK_NOPE], _rope(q[..., QK_NOPE:], cos[None, :, None], sin[None, :, None])

def _mla_latent(pm, kv_norm_g, cos, sin):
    c = _rmsnorm(pm[..., Q_LORA:Q_LORA + KV_LORA], kv_norm_g)
    kr = _rope(pm[..., Q_LORA + KV_LORA:], cos[None], sin[None])
    return c, kr

def _mla_expand(c, w_kvb):
    b, l, _ = c.shape
    kv = jnp.einsum('blr,rc->blc', c, w_kvb).reshape(b, l, MLA_HEADS, QK_NOPE + V_HEAD)
    return kv[..., :QK_NOPE], kv[..., QK_NOPE:]

def _mla_attend(q_nope, q_rope, k_nope, k_rope, v, mask):
    s = jnp.einsum('bqhd,bkhd->bhqk', q_nope, k_nope) + jnp.einsum('bqhr,bkr->bhqk', q_rope, k_rope)
    s = s.astype(jnp.float32) * ATTN_SCALE
    if mask is not None:
        s = jnp.where(mask, s, NEG_INF)
    p = jax.nn.softmax(s, axis=-1).astype(v.dtype)
    return jnp.einsum('bhqk,bkhd->bqhd', p, v)

def _mla_prompt_attention(qn, qr, kn, kr, v, cid):
    b, l = qn.shape[0], qn.shape[1]
    seq = l - N_META
    meta_o = _mla_attend(qn[:, :N_META], qr[:, :N_META], kn[:, :N_META], kr[:, :N_META], v[:, :N_META], None)
    n_blk = seq // Q_BLOCK
    blocks = lambda t: jnp.moveaxis(t[:, N_META:].reshape((b, n_blk, Q_BLOCK) + t.shape[2:]), 1, 0)
    cq = cid[N_META:].reshape(n_blk, Q_BLOCK)

    def one_block(args):
        qn_i, qr_i, cq_i = args
        mask = cid[None, :] <= cq_i[:, None]
        return _mla_attend(qn_i, qr_i, kn, kr, v, mask)

    o = lax.map(one_block, (blocks(qn), blocks(qr), cq))
    o = jnp.moveaxis(o, 0, 1).reshape(b, seq, MLA_HEADS, V_HEAD)
    return jnp.concatenate([meta_o, o], axis=1)

def _merge(o_rw, o_at, mla_out_g, w_out):
    b, l = o_rw.shape[0], o_rw.shape[1]
    o_at = _rmsnorm(o_at.reshape(b, l, MLA_WIDTH), mla_out_g).astype(o_rw.dtype)
    return jnp.einsum('blc,cd->bld', jnp.concatenate([o_rw, o_at], axis=-1), w_out)

def _post(x, mix, ln1_g, ln1_b, w_up, w_down, ln2_g, ln2_b):
    h = _layernorm(DEEPNORM_ALPHA * x + mix, ln1_g, ln1_b)
    f = jnp.einsum('blf,fd->bld', jnp.square(jax.nn.relu(jnp.einsum('bld,df->blf', h, w_up))), w_down)
    return _layernorm(DEEPNORM_ALPHA * h + f, ln2_g, ln2_b)

def setup_inputs(seed: int = 0) -> dict:
    key = jax.random.key(seed)
    keys = jax.random.split(key, 40)

    def nrm(i, shape, scale=1.0):
        return scale * jax.random.normal(keys[i], shape, jnp.float32)

    Dp = DEPTH
    return {
        'x_prompt': nrm(0, (BATCH, SEQ, D_MODEL)),
        'x_sample': nrm(1, (DEC_BATCH, DEC_SEQ, D_MODEL)),
        'cache_mla_latent': nrm(2, (Dp, DEC_BATCH, PAST_LEN, KV_LORA)),
        'cache_mla_rope': nrm(3, (Dp, DEC_BATCH, PAST_LEN, QK_ROPE)),
        'state_rwkv': nrm(4, (Dp, DEC_BATCH, RWKV_HEADS, RWKV_HEAD_DIM, RWKV_HEAD_DIM), 0.1),
        'state_shift': nrm(5, (Dp, DEC_BATCH, 1, C_RWKV)),
        'meta_tokens': nrm(6, (N_META, D_MODEL)),
        'ln_in_g': 1.0 + nrm(7, (D_MODEL,), 0.05),
        'ln_in_b': nrm(8, (D_MODEL,), 0.02),
        'w_in': nrm(9, (Dp, D_MODEL, C_IN), D_MODEL ** -0.5),
        'mu_shift': jax.random.uniform(keys[10], (Dp, C_RWKV), jnp.float32),
        'w_decay_up': nrm(11, (Dp, DECAY_LORA, RWKV_WIDTH), DECAY_LORA ** -0.5),
        'decay_base': nrm(12, (Dp, RWKV_WIDTH), 0.5),
        'w_aaa_up': nrm(13, (Dp, AAA_LORA, RWKV_WIDTH), AAA_LORA ** -0.5),
        'aaa_base': nrm(14, (Dp, RWKV_WIDTH), 0.5),
        'w_gate_up': nrm(15, (Dp, GATE_LORA, RWKV_WIDTH), GATE_LORA ** -0.5),
        'k_k': 0.85 + nrm(16, (Dp, RWKV_WIDTH), 0.1),
        'k_a': 1.0 + nrm(17, (Dp, RWKV_WIDTH), 0.1),
        'r_k': nrm(18, (Dp, RWKV_WIDTH), 0.1),
        'gn_g': 1.0 + nrm(19, (Dp, RWKV_WIDTH), 0.05),
        'gn_b': nrm(20, (Dp, RWKV_WIDTH), 0.02),
        'q_norm_g': 1.0 + nrm(21, (Dp, Q_LORA), 0.05),
        'w_qb': nrm(22, (Dp, Q_LORA, MLA_HEADS * (QK_NOPE + QK_ROPE)), Q_LORA ** -0.5),
        'kv_norm_g': 1.0 + nrm(23, (Dp, KV_LORA), 0.05),
        'w_kvb': nrm(24, (Dp, KV_LORA, MLA_HEADS * (QK_NOPE + V_HEAD)), KV_LORA ** -0.5),
        'mla_out_g': 1.0 + nrm(25, (Dp, MLA_WIDTH), 0.05),
        'w_out': nrm(26, (Dp, MIX_WIDTH, D_MODEL), DEEPNORM_BETA * MIX_WIDTH ** -0.5),
        'ln1_g': 1.0 + nrm(27, (Dp, D_MODEL), 0.05),
        'ln1_b': nrm(28, (Dp, D_MODEL), 0.02),
        'w_up': nrm(29, (Dp, D_MODEL, D_FF), D_MODEL ** -0.5),
        'w_down': nrm(30, (Dp, D_FF, D_MODEL), DEEPNORM_BETA * D_FF ** -0.5),
        'ln2_g': 1.0 + nrm(31, (Dp, D_MODEL), 0.05),
        'ln2_b': nrm(32, (Dp, D_MODEL), 0.02),
    }

def reference(x_prompt, x_sample, cache_mla_latent, cache_mla_rope, state_rwkv, state_shift,
              meta_tokens, ln_in_g, ln_in_b, w_in, mu_shift, w_decay_up, decay_base, w_aaa_up,
              aaa_base, w_gate_up, k_k, k_a, r_k, gn_g, gn_b, q_norm_g, w_qb, kv_norm_g, w_kvb,
              mla_out_g, w_out, ln1_g, ln1_b, w_up, w_down, ln2_g, ln2_b):
    b_p, seq = x_prompt.shape[0], x_prompt.shape[1]
    b_s, dec_seq = x_sample.shape[0], x_sample.shape[1]
    meta = jnp.broadcast_to(meta_tokens.astype(x_prompt.dtype)[None], (b_p, N_META, D_MODEL))
    hp = _layernorm(jnp.concatenate([meta, x_prompt], axis=1), ln_in_g, ln_in_b)
    hs = _layernorm(x_sample, ln_in_g, ln_in_b)
    cos_p, sin_p = _rope_tables(jnp.arange(N_META + seq))
    cos_s, sin_s = _rope_tables(PAST_LEN + jnp.arange(dec_seq))
    cid_p = jnp.concatenate([jnp.full((N_META,), -1, jnp.int32), jnp.arange(seq, dtype=jnp.int32) // CHUNK])
    lat_p, rope_p, wkv_p, shift_p = [], [], [], []
    lat_s, rope_s, wkv_s, shift_s = [], [], [], []
    for l in range(DEPTH):
        rw = (w_decay_up[l], decay_base[l], w_aaa_up[l], aaa_base[l], w_gate_up[l],
              k_k[l], k_a[l], r_k[l], gn_g[l], gn_b[l])
        post = (ln1_g[l], ln1_b[l], w_up[l], w_down[l], ln2_g[l], ln2_b[l])
        pr, pm, last = _project(hp, jnp.zeros((b_p, 1, C_RWKV), hp.dtype), w_in[l], mu_shift[l])
        o_rw, s_fin = _rwkv7(pr, jnp.zeros((b_p, RWKV_HEADS, RWKV_HEAD_DIM, RWKV_HEAD_DIM), jnp.float32), *rw)
        qn, qr = _mla_q(pm, q_norm_g[l], w_qb[l], cos_p, sin_p)
        c_p, kr_p = _mla_latent(pm, kv_norm_g[l], cos_p, sin_p)
        kn, vv = _mla_expand(c_p, w_kvb[l])
        o_at = _mla_prompt_attention(qn, qr, kn, kr_p, vv, cid_p)
        hp = _post(hp, _merge(o_rw, o_at, mla_out_g[l], w_out[l]), *post)
        lat_p.append(c_p)
        rope_p.append(kr_p)
        wkv_p.append(s_fin.astype(x_prompt.dtype))
        shift_p.append(last)
        pr, pm, last = _project(hs, state_shift[l], w_in[l], mu_shift[l])
        o_rw, s_fin = _rwkv7(pr, state_rwkv[l], *rw)
        qn, qr = _mla_q(pm, q_norm_g[l], w_qb[l], cos_s, sin_s)
        c_s, kr_s = _mla_latent(pm, kv_norm_g[l], cos_s, sin_s)
        c_all = jnp.concatenate([cache_mla_latent[l].astype(c_s.dtype), c_s], axis=1)
        kr_all = jnp.concatenate([cache_mla_rope[l].astype(kr_s.dtype), kr_s], axis=1)
        kn, vv = _mla_expand(c_all, w_kvb[l])
        o_at = _mla_attend(qn, qr, kn, kr_all, vv, None)
        hs = _post(hs, _merge(o_rw, o_at, mla_out_g[l], w_out[l]), *post)
        lat_s.append(c_s)
        rope_s.append(kr_s)
        wkv_s.append(s_fin.astype(state_rwkv.dtype))
        shift_s.append(last)
    y_prompt = hp[:, N_META:]
    y_sample = hs
    return (y_prompt, y_sample,
            jnp.stack(lat_p), jnp.stack(rope_p), jnp.stack(wkv_p), jnp.stack(shift_p),
            jnp.stack(lat_s), jnp.stack(rope_s), jnp.stack(wkv_s), jnp.stack(shift_s))


_drawn_inputs = setup_inputs


def setup_inputs(seed=0):
    import zlib

    import numpy as np

    out = dict(_drawn_inputs(seed))
    spreads = {}
    factors = {'gn_g': 6.479, 'gn_b': 28.356, 'q_norm_g': 3.456, 'mla_out_g': 3.258, 'ln2_b': 2.747}
    for name, (base, spread) in spreads.items():
        noise = np.random.default_rng([zlib.crc32(name.encode()), seed]).standard_normal(out[name].shape)
        drawn = base * np.exp(spread * noise) if base else spread * noise
        out[name] = jnp.asarray(drawn.astype(out[name].dtype))
    for name, factor in factors.items():
        out[name] = (out[name] * factor).astype(out[name].dtype)
    return out
```

```python
from contextlib import ExitStack

import numpy as np

import concourse.bass as bass
from concourse import mybir

F32 = mybir.dt.float32
F32R = mybir.dt.float32r
I32 = mybir.dt.int32
ALU = mybir.AluOpType
ACT = mybir.ActivationFunctionType
X = mybir.AxisListType.X

P = 128
D = 1024
KD = D // P
META = 16
SEQ = 1024
DEC_B, DEC_T = 8, 16
PAST = 256
SAMPLE = DEC_B * DEC_T
PROMPT = META + SEQ
TOKENS = PROMPT + SAMPLE
HEADS, HD = 8, 64
W = HEADS * HD
PAIRS = HEADS // 2
LORA = 64
C_RWKV = 3 * W + 2 * LORA + P
Q_LORA, KV_LORA, ROPE, NOPE = 384, 256, 32, 64
C_IN = C_RWKV + Q_LORA + KV_LORA + ROPE
QH = NOPE + ROPE
D_FF = 4 * D
ALPHA = 2.0 ** 0.25
LN_EPS, RMS_EPS, GN_EPS = 1e-5, 1e-6, 64e-5
DECAY = 0.6065306597126334
SCALE = QH ** -0.5
RSQRT_SEED = 0x5F3759DF

TILES = [(0, META)] + [(META + P * i, P) for i in range(SEQ // P + 1)]
LAST = len(TILES) - 1


class Semaphores:

    def __init__(self, nc, all_, prefix):
        self.nc, self.all, self.prefix, self.known = nc, all_, prefix, {}

    def __call__(self, name):
        if name not in self.known:
            self.known[name] = self.nc.alloc_semaphore(name=self.prefix + name)
            self.all.append(self.known[name])
        return self.known[name]


class Steps:

    def __init__(self, eng, sem):
        self.eng, self.sem, self.n = eng, sem, 0

    def __call__(self, ins):
        self.n += 1
        ins.then_inc(self.sem, 1)
        self.eng.wait_ge(self.sem, self.n)


def rsqrt(dve, step, y, x, t):
    step(dve.tensor_scalar(t.bitcast(I32), x.bitcast(I32), 1, None, ALU.arith_shift_right))
    step(dve.tensor_scalar(y.bitcast(I32), t.bitcast(I32), -1.0, float(RSQRT_SEED), ALU.mult, ALU.add))
    for _ in range(3):
        step(dve.tensor_tensor(t, y, y, ALU.mult))
        step(dve.scalar_tensor_tensor(t, t, -0.5, x, ALU.mult, ALU.mult))
        step(dve.scalar_tensor_tensor(y, t, 1.5, y, ALU.add, ALU.mult))


def layer_norm_stats(dve, step, x, st, mv, rs, t, n):
    step(dve.bn_stats(st[0:n, 0:6], x[:, 0:512]))
    step(dve.bn_stats(st[0:n, 6:12], x[:, 512:1024]))
    step(dve.bn_aggr(mv[0:n, 0:2], st[0:n, 0:12]))
    step(dve.tensor_scalar(mv[0:n, 1:2], mv[0:n, 1:2], LN_EPS, None, ALU.add))
    rsqrt(dve, step, rs[0:n, 0:1], mv[0:n, 1:2], t[0:n, 0:1])


def bcast(row, n=P):
    return row.rearrange("(a n) -> a n", a=1).broadcast_to([n, row.shape[-1]])


CH = C_IN // 8
N_CH = C_IN // CH
WINDOWS = [(P * w, 0) for w in range(TOKENS // P)] + [(TOKENS - P, P - TOKENS % P)]
NW = len(WINDOWS)


def phase_project(nc, io):
    with ExitStack() as ctx:
        def sb(name, shape, dt=F32):
            return ctx.enter_context(nc.sbuf_tensor(name, shape, dt))

        S = Semaphores(nc, io["semaphores"], "a_")
        x = [sb(f"a_x{i}", [P, D]) for i in range(2)]
        hn = [sb(f"a_hn{i}", [P, D]) for i in range(2)]
        g_row, b_row = sb("a_g", [P, D]), sb("a_b", [P, D])
        ident = sb("a_ident", [P, P])
        stats, mean, rstd, tmp = sb("a_st", [P, 12]), sb("a_mv", [P, 2]), sb("a_rs", [P, 1]), sb("a_t", [P, 1])
        hT = [sb("a_hT_hi", [P, KD, TOKENS], F32R), sb("a_hT_lo", [P, KD, TOKENS], F32R)]
        w_raw = [sb(f"a_w{i}", [P, KD, CH]) for i in range(2)]
        w_hi = [sb(f"a_wh{i}", [P, KD, CH], F32R) for i in range(2)]
        w_lo = [sb(f"a_wl{i}", [P, KD, CH], F32R) for i in range(2)]
        out = [sb(f"a_o{i}", [P, CH]) for i in range(4)]
        zero = sb("a_zero", [1, C_IN])
        pT = [ctx.enter_context(nc.psum_tensor(f"a_pT{i}", [P, 4, P], F32)) for i in range(2)]
        pO = [ctx.enter_context(nc.psum_tensor(f"a_pO{i}", [P, 512], F32)) for i in range(4)]
        w_in = io["w_in"][0].rearrange("(k p) n -> p k n", p=P)
        block = ctx.enter_context(nc.Block())

        def x_rows(i):
            if i == 0:
                return io["meta_tokens"]
            if i == LAST:
                return io["x_sample"].rearrange("b t d -> (b t) d")
            return io["x_prompt"][0, P * (i - 1):P * i, :]

        @block.sync
        def _(sp):
            def load_w(c, slot):
                sp.dma_start(w_raw[slot][:, :, :], w_in[:, :, bass.ds(c * CH, CH)]).then_inc(S(f"w_landed{slot}"), 16)

            def store_p(c, half, w):
                (r0, skip), slot = WINDOWS[w], (NW * half + w) % 4
                sp.wait_ge(S("p_drained"), c * NW + w + 1)
                sp.dma_start(io["p"][1 + r0 + skip:1 + r0 + P, bass.ds(c * CH, CH)],
                             out[slot][skip:P, :]).then_inc(S(f"p_stored{slot}"), 16)

            def pair(c, more):
                for half in range(2):
                    if more:
                        sp.wait_ge(S("w_lo"), c + half + 1)
                        load_w(c + half + 2, half)
                    for w in range(NW):
                        store_p(c + half, half, w)

            sp.dma_start(ident[:, :], io["ident"]).then_inc(S("ident_landed"), 16)
            for i, (t0, n) in enumerate(TILES):
                if i >= 2:
                    sp.wait_ge(S("h_normed"), i - 1)
                sp.dma_start(x[i % 2][0:n, :], x_rows(i)).then_inc(S(f"x_landed{i % 2}"), 16)
                if i == 0:
                    sp.dma_start(g_row[:, :], bcast(io["ln_in_g"])).then_inc(S("gb_landed"), 16)
                    sp.dma_start(b_row[:, :], bcast(io["ln_in_b"])).then_inc(S("gb_landed"), 16)
                    load_w(0, 0)
                    load_w(1, 1)
            sp.wait_ge(S("zero_set"), 1)
            sp.dma_start(io["p"][0:1, :], zero[:, :]).then_inc(S("zero_stored"), 16)
            pair(0, True)
            with sp.Fori(1, N_CH // 2 - 1) as j:
                pair(2 * j, True)
            pair(N_CH - 2, False)
            sp.wait_ge(S("zero_stored"), 16)
            for slot in range(4):
                sp.wait_ge(S(f"p_stored{slot}"), 16 * (NW * N_CH // 4))
            rows = io["p"][1 + PROMPT:1 + TOKENS, 0:C_RWKV].rearrange("(b t) c -> b t c", b=DEC_B)
            prev = io["prev"].rearrange("(b t) c -> b t c", b=DEC_B)
            sp.dma_start(prev[:, 1:DEC_T, :], rows[:, 0:DEC_T - 1, :]).then_inc(S("shift_copied"), 16)
            sp.dma_start(prev[:, 0, :], io["state_shift"][0, :, 0, :]).then_inc(S("shift_copied"), 16)
            sp.dma_start(io["o_shift_s"][0, :, 0, :], rows[:, DEC_T - 1, :]).then_inc(S("shift_copied"), 16)
            sp.dma_start(io["o_shift_p"][0, 0], io["p"][PROMPT:PROMPT + 1, 0:C_RWKV]).then_inc(S("shift_copied"), 16)
            sp.wait_ge(S("shift_copied"), 64)

        @block.gpsimd
        def _(pool):
            pool.memset(zero[:, :], 0.0).then_inc(S("zero_set"), 1)
            for i, (t0, n) in enumerate(TILES):
                pool.wait_ge(S("h_normed"), i + 1)
                if i == 0:
                    pool.wait_ge(S("gb_landed"), 32)
                h = hn[i % 2][0:n, :]
                pool.tensor_tensor(h, h, g_row[0:n, :], ALU.mult).then_inc(S("h_scaled"), 1)
                pool.wait_ge(S("h_scaled"), i + 1)
                pool.tensor_tensor(h, h, b_row[0:n, :], ALU.add).then_inc(S("h_ready"), 1)
                pool.wait_ge(S("h_ready"), i + 1)
                pool.dma_start(io["h"][t0:t0 + n, :], h).then_inc(S(f"h_stored{i % 2}"), 16)
            for s in range(2):
                pool.wait_ge(S(f"h_stored{s}"), 16 * len(range(s, len(TILES), 2)))

        @block.scalar
        def _(act):
            def w_high(c, slot):
                act.wait_ge(S(f"w_landed{slot}"), (c - slot) * 8 + 16)
                act.activation(w_hi[slot][:, :, :], w_raw[slot][:, :, :], ACT.Copy).then_inc(S("w_hi"), 1)

            def h_high(i):
                t0, n = TILES[i]
                for b in range(2):
                    act.wait_ge(S("h_transposed"), 2 * i + b + 1)
                    act.activation(hT[0][:, 4 * b:4 * b + 4, t0:t0 + n], pT[b][:, :, 0:n], ACT.Copy)\
                       .then_inc(S("h_hi"), 1)

            def drain(c, half, w, store=True):
                u = NW * half + w
                act.wait_ge(S("p_filled"), c * NW + w + 1)
                if store:
                    act.wait_ge(S(f"p_stored{u % 4}"), (c - half) * 4 * NW + 16 * (u // 4))
                act.activation(out[u % 4][:, :], pO[u % 4][:, 0:CH], ACT.Copy).then_inc(S("p_drained"), 1)

            def pair(c, more):
                for half in range(2):
                    for w in range(NW):
                        drain(c + half, half, w)
                        if w == 1 and (half == 0 or more):
                            w_high(c + half + 1, 1 - half)

            w_high(0, 0)
            for i in range(3):
                h_high(i)
            for half in range(2):
                for w in range(NW):
                    if half == 0 and w + 3 <= LAST:
                        h_high(w + 3)
                    drain(half, half, w, store=NW * half + w >= 4)
                    if w == (5 if half == 0 else 1):
                        w_high(half + 1, 1 - half)
            with act.Fori(1, N_CH // 2 - 1) as j:
                pair(2 * j, True)
            pair(N_CH - 2, False)

        @block.vector
        def _(dve):
            step = Steps(dve, S("dve_step"))

            def w_low(c, slot):
                dve.wait_ge(S("w_hi"), c + 1)
                dve.tensor_tensor(w_lo[slot][:, :, :], w_raw[slot][:, :, :], w_hi[slot][:, :, :].bitcast(F32),
                                  ALU.subtract).then_inc(S("w_lo"), 1)

            def norm(i):
                t0, n = TILES[i]
                dve.wait_ge(S(f"x_landed{i % 2}"), 16 * (i // 2 + 1))
                layer_norm_stats(dve, step, x[i % 2][0:n, :], stats, mean, rstd, tmp, n)
                if i >= 2:
                    dve.wait_ge(S("h_transposed"), 2 * i - 2)
                    dve.wait_ge(S(f"h_stored{i % 2}"), 16 * (i // 2))
                dve.tensor_scalar(hn[i % 2][0:n, :], x[i % 2][0:n, :], mean[0:n, 0:1], rstd[0:n, 0:1],
                                  ALU.subtract, ALU.mult).then_inc(S("h_normed"), 1)
                dve.wait_ge(S("h_normed"), i + 1)

            def h_low(i):
                t0, n = TILES[i]
                for b in range(2):
                    dve.wait_ge(S("h_hi"), 2 * i + b + 1)
                    dve.tensor_tensor(hT[1][:, 4 * b:4 * b + 4, t0:t0 + n], pT[b][:, :, 0:n],
                                      hT[0][:, 4 * b:4 * b + 4, t0:t0 + n].bitcast(F32), ALU.subtract)\
                       .then_inc(S("h_lo"), 1)

            norm(0)
            for i in range(len(TILES)):
                if i < LAST:
                    norm(i + 1)
                h_low(i)
                if i == 1:
                    w_low(0, 0)
            w_low(1, 1)
            w_low(2, 0)
            with dve.Fori(1, N_CH // 2 - 1) as j:
                w_low(2 * j + 1, 1)
                w_low(2 * j + 2, 0)
            w_low(N_CH - 1, 1)

        @block.tensor
        def _(pe):
            def turn(i):
                t0, n = TILES[i]
                pe.wait_ge(S("h_ready"), i + 1)
                for b in range(2):
                    if i >= 1:
                        pe.wait_ge(S("h_lo"), 2 * i + b - 1)
                    for k in range(4):
                        last = pe.transpose(pT[b][:, k, 0:n], hn[i % 2][0:n, P * (4 * b + k):P * (4 * b + k + 1)],
                                            ident[0:n, 0:n])
                    last.then_inc(S("h_transposed"), 1)

            def project(c, half, w, first=False):
                r0, slot = WINDOWS[w][0], (NW * half + w) % 4
                if not first:
                    pe.wait_ge(S("p_drained"), c * NW + w - 3)
                parts = [(hT[0], w_hi[half]), (hT[0], w_lo[half]), (hT[1], w_hi[half])]
                for a, (h, wt) in enumerate(parts):
                    for k in range(KD):
                        last = pe.matmul(pO[slot][:, 0:CH], h[:, k, r0:r0 + P], wt[:, k, :],
                                         start=(a == 0 and k == 0), stop=(a == 2 and k == KD - 1))
                last.then_inc(S("p_filled"), 1)

            def pair(c):
                for half in range(2):
                    pe.wait_ge(S("w_lo"), c + half + 1)
                    for w in range(NW):
                        project(c + half, half, w)

            pe.wait_ge(S("ident_landed"), 16)
            for i in range(3):
                turn(i)
            pe.wait_ge(S("w_lo"), 1)
            for w in range(NW):
                pe.wait_ge(S("h_lo"), 2 * (min(w + 1, LAST) + 1))
                project(0, 0, w, first=w < 4)
                if w + 3 <= LAST:
                    turn(w + 3)
            pe.wait_ge(S("w_lo"), 2)
            for w in range(NW):
                project(1, 1, w)
            with pe.Fori(1, N_CH // 2 - 1) as j:
                pair(2 * j)
            pair(N_CH - 2)


BLK = 3
N_BLK = (SEQ + SAMPLE) // (BLK * P)
NT = BLK * P
NF = D_FF // P
ROWS = KD + NF


def phase_mlp(nc, io):
    with ExitStack() as ctx:
        def sb(name, shape, dt=F32):
            return ctx.enter_context(nc.sbuf_tensor(name, shape, dt))

        S = Semaphores(nc, io["semaphores"], "c_")
        ident = sb("c_ident", [P, P])
        rows = {n: sb(f"c_{n}", [P, D]) for n in ("ln1_g", "ln1_b", "ln2_g", "ln2_b")}
        mix = sb("c_mix", [P, BLK, D])
        res = [sb(f"c_res{i}", [P, BLK, D]) for i in range(2)]
        zT = [sb("c_zT_hi", [P, KD, NT], F32R), sb("c_zT_lo", [P, KD, NT], F32R)]
        row_raw = [sb(f"c_rw{i}", [P, D]) for i in range(2)]
        row_hi = [sb(f"c_rh{i}", [P, D], F32R) for i in range(2)]
        row_lo = [sb(f"c_rl{i}", [P, D], F32R) for i in range(2)]
        up_raw = [sb(f"c_uw{i}", [P, KD, P]) for i in range(2)]
        up_hi = [sb(f"c_uh{i}", [P, KD, P], F32R) for i in range(2)]
        up_lo = [sb(f"c_ul{i}", [P, KD, P], F32R) for i in range(2)]
        relu = [sb(f"c_relu{i}", [P, NT]) for i in range(2)]
        hid = [sb(f"c_hid{i}", [P, NT]) for i in range(2)]
        hid_hi = [sb(f"c_hh{i}", [P, NT], F32R) for i in range(2)]
        hid_lo = [sb(f"c_hl{i}", [P, NT], F32R) for i in range(2)]
        zero_raw, zero = sb("c_zero_raw", [P, 512]), sb("c_zero", [P, 512], F32R)
        stats, mean, rstd, tmp = sb("c_st", [P, 12]), sb("c_mv", [P, 2]), sb("c_rs", [P, 1]), sb("c_t", [P, 1])
        pY = [ctx.enter_context(nc.psum_tensor(f"c_pY{i}", [P, 512], F32)) for i in range(2 * BLK)]
        pU = [ctx.enter_context(nc.psum_tensor(f"c_pU{i}", [P, 512], F32)) for i in range(2)]
        w_up = io["w_up"][0].rearrange("(k p) n -> p k n", p=P)
        w_out, w_down = io["w_out"][0], io["w_down"][0]
        block = ctx.enter_context(nc.Block())

        def y_rows(b, t):
            i = BLK * b + t
            if i == SEQ // P:
                return io["o_y_s"].rearrange("b t d -> (b t) d")
            return io["o_y_p"][0, P * i:P * (i + 1), :]

        @block.sync
        def _(sp):
            def load_row(src, r, slot):
                sp.dma_start(row_raw[slot][:, :], src[bass.ds(r, P), :]).then_inc(S(f"row_landed{slot}"), 16)

            def load_up(f, slot):
                sp.dma_start(up_raw[slot][:, :, :], w_up[:, :, bass.ds(f, P)]).then_inc(S(f"up_landed{slot}"), 16)

            def load_tokens(b):
                r0 = P * BLK * b
                sp.dma_start(mix[:, :, :], io["mix"][r0:r0 + NT, :].rearrange("(t p) d -> p t d", p=P))\
                  .then_inc(S("mix_landed"), 16)
                if b >= 2:
                    sp.wait_ge(S("y_stored"), 16 * BLK * (b - 1))
                sp.dma_start(res[b % 2][:, :, :], io["h"][META + r0:META + r0 + NT, :].rearrange("(t p) d -> p t d", p=P))\
                  .then_inc(S("h_landed"), 16)

            sp.dma_start(ident[:, :], io["ident"]).then_inc(S("ident_landed"), 16)
            load_tokens(0)
            load_row(w_out, 0, 0)
            load_row(w_out, P, 1)
            load_up(0, 0)
            load_up(P, 1)
            for n in rows:
                sp.dma_start(rows[n][:, :], bcast(io[n])).then_inc(S("gb_landed"), 16)
            for b in range(N_BLK):
                for k in range(KD):
                    sp.wait_ge(S("row_lo"), ROWS * b + k + 1)
                    if k + 2 < KD:
                        load_row(w_out, P * (k + 2), k % 2)
                    else:
                        load_row(w_down, P * (k + 2 - KD), k % 2)
                if b + 1 < N_BLK:
                    sp.wait_ge(S("turned"), 4 * BLK * b + 2 * BLK)
                    load_tokens(b + 1)

                def step_pair(f):
                    for half in range(2):
                        sp.wait_ge(S("up_lo"), NF * b + f + half + 1)
                        load_up(P * (f + half + 2), half)
                        sp.wait_ge(S("row_lo"), ROWS * b + KD + f + half + 1)
                        load_row(w_down, P * (f + half + 2), half)

                with sp.Fori(0, NF // 2 - 1) as j:
                    step_pair(2 * j)
                if b + 1 < N_BLK:
                    for half in range(2):
                        sp.wait_ge(S("row_lo"), ROWS * b + KD + NF - 2 + half + 1)
                        load_row(w_out, P * half, half)
                        sp.wait_ge(S("up_lo"), NF * b + NF - 2 + half + 1)
                        load_up(P * half, half)

        @block.gpsimd
        def _(pool):
            pool.memset(zero_raw[:, :], 0.0).then_inc(S("zero_set"), 1)
            count = [0]

            def scale_rows(ready, n, buf, b, g, bb):
                for t in range(BLK):
                    pool.wait_ge(S(ready), BLK * b + t + 1)
                    r = buf[:, t, :]
                    count[0] += 1
                    pool.tensor_tensor(r, r, rows[g][:, :], ALU.mult).then_inc(S("scaled"), 1)
                    pool.wait_ge(S("scaled"), count[0])
                    pool.tensor_tensor(r, r, rows[bb][:, :], ALU.add).then_inc(S(n), 1)
                    if n == "y_ready":
                        pool.wait_ge(S(n), BLK * b + t + 1)
                        pool.dma_start(y_rows(b, t), r).then_inc(S("y_stored"), 16)

            def square(b, f, half, first=False):
                u = NF * b + f + half
                pool.wait_ge(S("relu"), u + 1)
                if not first:
                    pool.wait_ge(S("hid_lo"), u - 1)
                pool.tensor_tensor(hid[half][:, :], relu[half][:, :], relu[half][:, :], ALU.mult)\
                    .then_inc(S("squared"), 1)

            pool.wait_ge(S("gb_landed"), 64)
            for b in range(N_BLK):
                if b:
                    scale_rows("y_normed", "y_ready", res[(b - 1) % 2], b - 1, "ln2_g", "ln2_b")
                scale_rows("h1_normed", "h1_ready", res[b % 2], b, "ln1_g", "ln1_b")
                square(b, 0, 0, first=b == 0)
                square(b, 0, 1, first=b == 0)
                with pool.Fori(1, NF // 2) as j:
                    square(b, 2 * j, 0)
                    square(b, 2 * j, 1)
            b = N_BLK - 1
            scale_rows("y_normed", "y_ready", res[b % 2], b, "ln2_g", "ln2_b")
            pool.wait_ge(S("y_stored"), 16 * BLK * N_BLK)

        @block.scalar
        def _(act):
            def row_high(b, r, slot):
                act.wait_ge(S(f"row_landed{slot}"), 8 * (ROWS * b + r - slot) + 16)
                if not (b == 0 and isinstance(r, int) and r < 2):
                    act.wait_ge(S("row_used"), ROWS * b + r - 1)
                act.activation(row_hi[slot][:, :], row_raw[slot][:, :], ACT.Copy).then_inc(S("row_hi"), 1)

            def up_high(b, f, slot):
                act.wait_ge(S(f"up_landed{slot}"), 8 * (NF * b + f - slot) + 16)
                if not (b == 0 and isinstance(f, int) and f < 2):
                    act.wait_ge(S("up_done"), NF * b + f - 1)
                act.activation(up_hi[slot][:, :, :], up_raw[slot][:, :, :], ACT.Copy).then_inc(S("up_hi"), 1)

            def turned_high(b, which):
                for u in range(2 * BLK):
                    t, k4 = u // 2, 4 * (u % 2)
                    act.wait_ge(S("turned"), 4 * BLK * b + 2 * BLK * which + u + 1)
                    act.activation(zT[0][:, k4:k4 + 4, P * t:P * (t + 1)],
                                   pU[u % 2][:, :].rearrange("p (k n) -> p k n", k=4), ACT.Copy)\
                       .then_inc(S("zT_hi"), 1)

            def hidden(b, f, half, more_row=True, more_up=True, first=False):
                u = NF * b + f + half
                act.wait_ge(S("up_done"), u + 1)
                if not first:
                    act.wait_ge(S("squared"), u - 1)
                act.activation(relu[half][:, :], pU[half][:, 0:NT], ACT.Relu).then_inc(S("relu"), 1)
                if more_row:
                    row_high(b, f + half + 1 + KD, (half + 1) % 2)
                act.wait_ge(S("squared"), u + 1)
                act.wait_ge(S("row_used"), ROWS * b + KD + f + half - 1)
                act.activation(hid_hi[half][:, :], hid[half][:, :], ACT.Copy).then_inc(S("hid_hi"), 1)
                if more_up:
                    up_high(b, f + half + 2, half)

            act.wait_ge(S("zero_set"), 1)
            act.activation(zero[:, :], zero_raw[:, :], ACT.Copy).then_inc(S("zero_ready"), 1)
            for b in range(N_BLK):
                turned_high(b, 0)
                for k in range(KD):
                    row_high(b, k, k % 2)
                up_high(b, 0, 0)
                up_high(b, 1, 1)
                row_high(b, KD, 0)
                turned_high(b, 1)
                hidden(b, 0, 0, first=b == 0)
                hidden(b, 0, 1, first=b == 0)
                with act.Fori(1, NF // 2 - 1) as j:
                    hidden(b, 2 * j, 0)
                    hidden(b, 2 * j, 1)
                hidden(b, NF - 2, 0, more_up=False)
                hidden(b, NF - 2, 1, more_row=False, more_up=False)

        @block.vector
        def _(dve):
            step = Steps(dve, S("dve_step"))

            def row_low(b, r, slot):
                dve.wait_ge(S("row_hi"), ROWS * b + r + 1)
                dve.tensor_tensor(row_lo[slot][:, :], row_raw[slot][:, :], row_hi[slot][:, :].bitcast(F32),
                                  ALU.subtract).then_inc(S("row_lo"), 1)

            def up_low(b, f, slot):
                dve.wait_ge(S("up_hi"), NF * b + f + 1)
                dve.tensor_tensor(up_lo[slot][:, :, :], up_raw[slot][:, :, :], up_hi[slot][:, :, :].bitcast(F32),
                                  ALU.subtract).then_inc(S("up_lo"), 1)

            def turned_low(b, which):
                for u in range(2 * BLK):
                    t, k4 = u // 2, 4 * (u % 2)
                    dve.wait_ge(S("zT_hi"), 4 * BLK * b + 2 * BLK * which + u + 1)
                    dve.tensor_tensor(zT[1][:, k4:k4 + 4, P * t:P * (t + 1)],
                                      pU[u % 2][:, :].rearrange("p (k n) -> p k n", k=4),
                                      zT[0][:, k4:k4 + 4, P * t:P * (t + 1)].bitcast(F32), ALU.subtract)\
                       .then_inc(S("zT_lo"), 1)

            def add_residual(b, taken):
                r = res[b % 2]
                for u in range(2 * BLK):
                    x = r[:, u // 2, 512 * (u % 2):512 * (u % 2) + 512]
                    dve.scalar_tensor_tensor(x, x, ALPHA, pY[u][:, :], ALU.mult, ALU.add).then_inc(S(taken), 1)

            def normalise(b, normed, taken):
                r = res[b % 2]
                for t in range(BLK):
                    dve.wait_ge(S(taken), 2 * BLK * b + 2 * t + 2)
                    x = r[:, t, :]
                    layer_norm_stats(dve, step, x, stats, mean, rstd, tmp, P)
                    dve.tensor_scalar(x, x, mean[:, 0:1], rstd[:, 0:1], ALU.subtract, ALU.mult)\
                       .then_inc(S(normed), 1)
                    dve.wait_ge(S(normed), BLK * b + t + 1)

            def hidden_low(b, f, half):
                dve.wait_ge(S("hid_hi"), NF * b + f + half + 1)
                dve.tensor_tensor(hid_lo[half][:, :], hid[half][:, :], hid_hi[half][:, :].bitcast(F32),
                                  ALU.subtract).then_inc(S("hid_lo"), 1)

            for b in range(N_BLK):
                turned_low(b, 0)
                row_low(b, 0, 0)
                row_low(b, 1, 1)
                if b:
                    normalise(b - 1, "y_normed", "y_taken")
                for k in range(2, KD):
                    row_low(b, k, k % 2)
                up_low(b, 0, 0)
                up_low(b, 1, 1)
                row_low(b, KD, 0)
                dve.wait_ge(S("row_used"), ROWS * b + KD)
                if b == 0:
                    dve.wait_ge(S("h_landed"), 16)
                else:
                    dve.wait_ge(S("h_landed"), 16 * b + 16)
                add_residual(b, "z_taken")
                normalise(b, "h1_normed", "z_taken")
                turned_low(b, 1)

                def pair(f, more_row=True, more_up=True):
                    for half in range(2):
                        if more_row or half == 0:
                            row_low(b, f + half + 1 + KD, (half + 1) % 2)
                        hidden_low(b, f, half)
                        if more_up:
                            up_low(b, f + half + 2, half)

                with dve.Fori(0, NF // 2 - 1) as j:
                    pair(2 * j)
                pair(NF - 2, more_row=False, more_up=False)
                dve.wait_ge(S("row_used"), ROWS * (b + 1))
                dve.wait_ge(S("h1_ready"), BLK * (b + 1))
                add_residual(b, "y_taken")
            normalise(N_BLK - 1, "y_normed", "y_taken")

        @block.tensor
        def _(pe):
            def turn(b, which):
                src = mix if which == 0 else res[b % 2]
                for u in range(2 * BLK):
                    t = u // 2
                    if which:
                        pe.wait_ge(S("h1_ready"), BLK * b + t + 1)
                    n = 4 * BLK * b + 2 * BLK * which + u
                    if which == 0 and u < 2:
                        if b:
                            pe.wait_ge(S("relu"), NF * b)
                    else:
                        pe.wait_ge(S("zT_lo"), n - 1)
                    for k in range(4):
                        c = P * (4 * (u % 2) + k)
                        last = pe.transpose(pU[u % 2][:, P * k:P * (k + 1)], src[:, t, c:c + P], ident[:, :])
                    last.then_inc(S("turned"), 1)

            def add_rows(b, r, slot, lhs, first=False, final=False):
                pe.wait_ge(S("row_lo"), ROWS * b + r + 1)
                for t in range(BLK):
                    for half in range(2):
                        out = pY[2 * t + half][:, :]
                        for a, (x, w) in enumerate([(lhs[0], row_hi), (lhs[0], row_lo), (lhs[1], row_hi)]):
                            last = pe.matmul(out, x[:, P * t:P * (t + 1)], w[slot][:, 512 * half:512 * half + 512],
                                             start=first and a == 0, stop=final and a == 2, skip_group_check=True)
                last.then_inc(S("row_used"), 1)

            def up(b, f, slot, first=False):
                pe.wait_ge(S("up_lo"), NF * b + f + 1)
                if not first:
                    pe.wait_ge(S("relu"), NF * b + f - 1)
                parts = [(up_hi, zT[0]), (up_lo, zT[0]), (up_hi, zT[1])]
                for a, (w, x) in enumerate(parts):
                    for k in range(KD):
                        last = pe.matmul(pU[slot][:, 0:NT], w[slot][:, k, :], x[:, k, :],
                                         start=(a == 0 and k == 0), stop=(a == 2 and k == KD - 1))
                last.then_inc(S("up_done"), 1)

            def down(b, f, half, final=False):
                pe.wait_ge(S("hid_lo"), NF * b + f + half + 1)
                add_rows(b, KD + f + half, half, (hid_hi[half], hid_lo[half]), final=final)

            pe.wait_ge(S("ident_landed"), 16)
            pe.wait_ge(S("zero_ready"), 1)
            for b in range(N_BLK):
                pe.wait_ge(S("mix_landed"), 16 * (b + 1))
                turn(b, 0)
                pe.wait_ge(S("zT_lo"), 4 * BLK * b + 2 * BLK)
                if b:
                    pe.wait_ge(S("y_taken"), 2 * BLK * b)
                for k in range(KD):
                    add_rows(b, k, k % 2, (zT[0][:, k, :], zT[1][:, k, :]), first=k == 0, final=k == KD - 1)
                turn(b, 1)
                pe.wait_ge(S("zT_lo"), 4 * BLK * (b + 1))
                for u in range(2 * BLK):
                    pe.matmul(pY[u][:, :], zero[:, 0:P], zero[:, :], start=True, stop=False, skip_group_check=True)
                up(b, 0, 0, first=True)
                up(b, 1, 1, first=True)
                down(b, 0, 0)
                with pe.Fori(1, NF // 2) as j:
                    up(b, 2 * j, 0)
                    down(b, 2 * j - 2, 1)
                    up(b, 2 * j + 1, 1)
                    down(b, 2 * j, 0)
                down(b, NF - 2, 1, final=True)


CHUNK = 64
HALF = -0.5 * DECAY
LEVELS = {META: 3, P: 5}
N_CONST = 5
C_LOWER, C_UPPER, C_UPPER_EQ, C_IDENT, C_TWICE = range(N_CONST)


def heads(ap, width=HD):
    return ap.rearrange("p (h d) -> p h d", d=width)


class Jobs:

    def __init__(self, S, banks, tag):
        self.S, self.banks, self.tag, self.number = S, banks, tag, {}

    def fill(self, pe, name):
        q = len(self.number)
        assert name not in self.number, name
        self.number[name] = q
        if q >= len(self.banks):
            pe.wait_ge(self.S(f"{self.tag}_taken{q % len(self.banks)}"), q // len(self.banks))
        return self.banks[q % len(self.banks)]

    def filled(self, last):
        last.then_inc(self.S(f"{self.tag}_filled"), 1)

    def take(self, eng, name):
        eng.wait_ge(self.S(f"{self.tag}_filled"), self.number[name] + 1)
        return self.banks[self.number[name] % len(self.banks)]

    def taken(self, last, name):
        last.then_inc(self.S(f"{self.tag}_taken{self.number[name] % len(self.banks)}"), 1)
        return self.S(f"{self.tag}_taken{self.number[name] % len(self.banks)}"), self.number[name] // len(self.banks) + 1

    def wait_filled(self, eng, name):
        eng.wait_ge(self.S(f"{self.tag}_filled"), self.number[name] + 1)

    def wait_taken(self, eng, name):
        q = self.number[name]
        eng.wait_ge(self.S(f"{self.tag}_taken{q % len(self.banks)}"), q // len(self.banks) + 1)


def load_mix_weights(nc, io, sb, M):
    S = Semaphores(nc, io["semaphores"], "m_")
    M.update({
        "const": sb("m_const", [P, N_CONST, P]),
        "cvec": sb("m_cvec", [P, 8]),
        "ind": sb("m_ind", [P, 10]),
        "rowpair": sb("m_rowpair", [1, 2, P]),
        "wdec": sb("m_wdec", [LORA + 1, W]),
        "waaa": sb("m_waaa", [LORA + 1, W]),
        "wgate": sb("m_wgate", [P, W]),
        "w_qb": sb("m_wqb", [P, Q_LORA // P, HEADS * QH]),
        "w_kvb": sb("m_wkvb", [P, 2, HEADS * 2 * HD]),
        "mu": sb("m_mu", [P, C_RWKV]),
    })
    for r, width in (("k_k", W), ("k_a", W), ("r_k", W), ("gn_g", W), ("gn_b", W), ("q_norm_g", Q_LORA),
                     ("kv_norm_g", KV_LORA), ("mla_out_g", W)):
        M[r] = sb(f"m_{r}", [P, width])
    with nc.Block() as block:
        @block.sync
        def _(sp):
            loads = [
                (M["const"][:, :, :], io["const"].rearrange("m p n -> p m n")),
                (M["cvec"][:, :], io["cvec"]), (M["ind"][:, :], io["ind"]),
                (M["rowpair"][:, :, :], io["rowpair"].rearrange("(a m) n -> a m n", a=1)),
                (M["wdec"][0:LORA, :], io["w_decay_up"][0]), (M["wdec"][LORA:LORA + 1, :], io["decay_base"]),
                (M["waaa"][0:LORA, :], io["w_aaa_up"][0]), (M["waaa"][LORA:LORA + 1, :], io["aaa_base"]),
                (M["wgate"][:, :], io["w_gate_up"][0]),
                (M["w_qb"][:, :, :], io["w_qb"][0].rearrange("(k p) n -> p k n", p=P)),
                (M["w_kvb"][:, :, :], io["w_kvb"][0].rearrange("(k p) n -> p k n", p=P)),
                (M["mu"][:, :], bcast(io["mu_shift"][0])),
            ] + [(M[r][:, :], bcast(io[r][0])) for r in
                 ("k_k", "k_a", "r_k", "gn_g", "gn_b", "q_norm_g", "kv_norm_g", "mla_out_g")]
            for dst, src in loads:
                sp.dma_start(dst, src).then_inc(S("weights_landed"), 16)
            sp.wait_ge(S("weights_landed"), 16 * len(loads))


def schedule(vector=False):
    prepare = [["shift", "norm"], ["turn_latent", "lora"], ["turn_lora", "key_squares"],
               ["key_norm", "lora_up", "latent_keys"],
               ["keys", "decay", "latent_rest"], ["products"]]
    norm = [[], ["mean"], ["variance"], ["gate_out"], [], ["finish"]]
    count = len(TILES) - 1
    steps = [("shift_diff", 0, None)] + [(s, 0, None) for piece in prepare for s in piece]
    steps += [("turn_sides", 0, None), ("turn", 0, None)]
    for i in range(count):
        beside = [[(s, i - 1, None) for s in (norm[m] if i > 1 else [])]
                  + [(s, i + 1, None) for s in (prepare[m] if i + 1 < count else [])] for m in range(len(prepare))]
        attend = lambda name, v: [(name, i, v)] if i and v >= 0 else []
        steps += attend("score", 0) + [("shift_diff", i + 1, None)] * (i + 1 < count) + [("gram", i, None)]
        levels = LEVELS[TILES[i][1]]
        for v in range(levels):
            late = [step for step in beside[v] if not vector or step[0] == "latent_keys"]
            steps += [("newton_t", i, v)] + [step for step in beside[v] if step not in late]
            steps += attend("weights", v - 1) + [("newton_x", i, v)] + attend("values", v - 1)
            steps += (attend("score", v) if v else []) + late
        v = levels - 1
        for c in range(1 if i == 0 else 2):
            steps += [("scan_z", i, c)] + attend("weights", v) + [("scan_sa", i, c)] + attend("values", v)
            steps += attend("score", v + 1) + [("scan_s", i, c)]
            if c == 0:
                steps += [step for piece in beside[levels:] for step in piece]
            v += 1
        following = i + 1 < count
        steps += [("turn_sides", i + 1, None)] * following + attend("weights", v) + attend("values", v)
        steps += attend("score", v + 1) + [("turn", i + 1, None)] * following
        if i:
            steps += attend("weights", v + 1) + attend("values", v + 1) + [("merge", i, None)]
    return steps + [(s, count - 1, None) for piece in norm for s in piece]


def phase_mix_prompt(nc, io, M):
    with ExitStack() as ctx:
        def sb(name, shape, dt=F32):
            return ctx.enter_context(nc.sbuf_tensor(name, shape, dt))

        def psum(name, shape):
            return ctx.enter_context(nc.psum_tensor(name, shape, F32))

        S = Semaphores(nc, io["semaphores"], "b_")
        pr = [sb(f"b_pr{i}", [P, C_IN]) for i in range(2)]
        prev = sb("b_prev", [P, 4 * W])
        w_inc, w_inv, w_ex, kk = (prev[:, W * m:W * m + W] for m in range(4))
        table = sb("b_table", [P, 2 * ROPE])
        laT, lgT = sb("b_laT", [LORA + 1, 2, P]), sb("b_lgT", [P, P])
        td, tmp = sb("b_td", [P, W]), sb("b_tmp", [P, W])
        la, lg = tmp[:, 0:LORA], tmp[:, LORA:LORA + P]
        a_, kt_, gate_, bonus_ = ([sb(f"b_{n}{i}", [P, W]) for i in range(2)] for n in ("a", "kt", "gate", "bonus"))
        wl_ = [sb(f"b_wl{i}", [P, PAIRS, 2]) for i in range(2)]
        KT, RT = sb("b_KT", [P, PAIRS, P]), sb("b_RT", [P, PAIRS, P])
        khBT = sb("b_khBT", [P, 2 * W])
        khT, BT = (khBT[:, W * m:W * m + W].rearrange("p (k n) -> p k n", k=PAIRS) for m in range(2))
        q = khBT[:, 0:HEADS * QH].rearrange("p (h d) -> p h d", d=QH)
        qt = khBT[:, HEADS * QH:HEADS * (QH + ROPE)].rearrange("p (h d) -> p h d", d=ROPE)
        BTn = td[:, :].rearrange("p (k n) -> p k n", k=PAIRS)
        IA, X0, XA, F, PT = (sb(f"b_{n}", [P, HEADS, P]) for n in ("IA", "X0", "XA", "F", "PT"))
        zr, SA = sb("b_zr", [P, W]), sb("b_SA", [P, W])
        state = sb("b_state", [P, PAIRS, HD])
        mixed = sb("b_mixed", [P, D])
        ssq = sb("b_ssq", [P, 4])
        qn, c, kr, krt = sb("b_qn", [P, Q_LORA]), sb("b_c", [P, KV_LORA]), sb("b_kr", [P, ROPE]), sb("b_krt", [P, ROPE])
        cT = sb("b_cT", [P, 2, P])
        qT = sb("b_qT", [QH, HEADS, P])
        kTall = sb("b_kT", [QH, HEADS, PROMPT])
        vall, vmeta, vbd = sb("b_v", [P, SEQ // P, W]), mixed[0:META, 0:W], sb("b_vbd", [P, W])
        Pb = [sb(f"b_P{i}", [P, SEQ]) for i in range(2)]
        PTb = [sb(f"b_PT{i}", [P, 4, P]) for i in range(2)]
        qnT = sb("b_qnT", [P, 3, P])
        sm, pm = sb("b_sm", [P, HEADS, META]), sb("b_pm", [P, HEADS, META])
        pmT = sm[:, :, :].rearrange("p h m -> p (h m)")
        SC = psum("b_SC", [P, SEQ])
        O, Y, Z = psum("b_O", [P, 512]), psum("b_Y", [P, 512]), psum("b_Z", [P, 512])
        J = Jobs(S, [psum(f"b_R{i}", [P, 512]) for i in range(3)], "b")
        ident = M["const"][:, C_IDENT, :]
        lower, upper, upper_eq, twice = (M["const"][:, m, :] for m in (C_LOWER, C_UPPER, C_UPPER_EQ, C_TWICE))
        NP = len(TILES) - 1
        stat = sb("b_stat", [P, 80])
        n2, rk, t8, bs, mu8, v8, rs8, mm, rs, rsm = (stat[:, 8 * m:8 * m + 8] for m in range(10))
        mxc, nb = sb("b_mx", [P, 8]), sb("b_nb", [P, 8])
        ms, rs2, t2 = sb("b_ms", [P, 4]), sb("b_rs2", [P, 4]), sb("b_t2", [P, 4])
        den = sb("b_den", [P, 8])
        block = ctx.enter_context(nc.Block())

        def bc(ap8, n):
            return ap8[0:n, :].unsqueeze(2).to_broadcast([n, HEADS, HD])

        def bc4(m, n):
            return m[0:n, 0:n].unsqueeze(1).to_broadcast([n, 4, n])

        def four(bank, n, rows=None):
            return bank[0:(n if rows is None else rows), 0:4 * n].rearrange("p (k n) -> p k n", k=4)

        def chunk_no(i, c_):
            return 0 if i == 0 else 2 * i - 1 + c_

        def key_jobs(i):
            return [list(range(j, min(j + 4, i + 1))) for j in range(1, i + 1, 4)]

        def pv_before(i, h):
            return sum(HEADS * len(key_jobs(m)) for m in range(1, i)) + h * len(key_jobs(i))

        @block.tensor
        def _(pe):
            def times_state(i, out, lhs, R, odd, name, m):
                r = slice(HD * odd, HD * odd + HD)
                for k in range(PAIRS):
                    last = pe.matmul(out[R, P * k + HD * odd:P * k + HD * odd + HD], lhs[r, k, R], state[r, k, :],
                                     start=False, stop=True, skip_group_check=True)
                last.then_inc(S(name), 1)
                pe.wait_ge(S(name), m + 1)

            for step, i, v in schedule():
                t0, n = TILES[i]
                p_, V = pr[i % 2], pr[i % 2][0:n, 2 * W:3 * W]
                a, kt = a_[i % 2], kt_[i % 2]

                def turns(name, pieces):
                    bank = J.fill(pe, (i, name))
                    for out, src in pieces(bank):
                        last = pe.transpose(out, src, ident[0:n, 0:n])
                    J.filled(last)

                if step == "turn_latent":
                    pe.wait_ge(S("c_ready"), i + 1)
                    pe.wait_ge(S("kr_ready"), i + 1)
                    bank = J.fill(pe, (i, "cT"))
                    for k in range(2):
                        pe.transpose(bank[:, k * n:k * n + n], c[0:n, P * k:P * k + P], ident[0:n, 0:n])
                    J.filled(pe.matmul(bank[NOPE:QH, 2 * n:3 * n], kr[0:n, :], ident[0:n, 0:n],
                                       start=True, stop=True))
                    if i:
                        pe.wait_ge(S("qn_ready"), i + 1)
                        turns("qnT", lambda b: [(b[:, k * n:k * n + n], qn[0:n, P * k:P * k + P]) for k in range(3)])
                if step == "turn_lora":
                    pe.wait_ge(S("la_ready"), 2 * i + 2)
                    pe.wait_ge(S("shifted"), i + 1)
                    turns("loraT", lambda b: [(b[0:LORA, 0:n], la[0:n, :]),
                                              (b[0:LORA, n:2 * n], p_[0:n, 3 * W + LORA:3 * W + 2 * LORA]),
                                              (b[:, 2 * n:3 * n], lg[0:n, :])])
                if step == "lora_up":
                    pe.wait_ge(S("laT_out"), i + 1)
                    J.wait_taken(pe, (i, "loraT"))
                    if i == 0:
                        pe.wait_ge(S("ones_set"), 1)
                    for name, lhs, rhs in (("dec", laT[:, 0, 0:n], M["wdec"]), ("aaa", laT[:, 1, 0:n], M["waaa"]),
                                           ("gate", lgT[:, 0:n], M["wgate"])):
                        bank = J.fill(pe, (i, name))
                        J.filled(pe.matmul(bank[0:n, :], lhs, rhs[:, :], start=True, stop=True))
                if step == "decay":
                    J.wait_taken(pe, (i, "dec"))
                    for name, tri in (("inc", upper_eq), ("ex", upper)):
                        bank = J.fill(pe, (i, name))
                        J.filled(pe.matmul(bank[0:n, :], tri[0:n, 0:n], td[0:n, :], start=True, stop=True))
                    bank = J.fill(pe, (i, "total"))
                    for g in range(PAIRS):
                        last = pe.matmul(bank[:, 2 * g:2 * g + 2], td[0:n, P * g:P * g + P], M["ind"][0:n, 0:2],
                                         start=True, stop=True)
                    J.filled(last)
                if step == "latent_keys":
                    pe.wait_ge(S("cT_out"), i + 1)
                    for g in range(2):
                        bank = J.fill(pe, (i, "kn", g))
                        for hh in range(4):
                            col = (4 * g + hh) * 2 * HD
                            for k in range(2):
                                last = pe.matmul(bank[0:NOPE, hh * n:hh * n + n], M["w_kvb"][:, k, col:col + NOPE],
                                                 cT[:, k, 0:n], start=k == 0, stop=k == 1)
                        J.filled(last)
                if step == "latent_rest":
                    bank = J.fill(pe, (i, "v"))
                    wv = M["w_kvb"][:, :, :].rearrange("p k (h d) -> p k h d", d=2 * HD)[:, :, :, HD:2 * HD]
                    for k in range(2):
                        last = pe.matmul(heads(bank[0:n, :]), cT[:, k, 0:n], wv[:, k], start=k == 0, stop=k == 1)
                    J.filled(last)
                    if i:
                        J.wait_taken(pe, (i, "qnT"))
                        for g in range(2):
                            bank = J.fill(pe, (i, "q", g))
                            for k in range(3):
                                last = pe.matmul(bank[0:n, 0:4 * QH], qnT[:, k, 0:n],
                                                 M["w_qb"][:, k, 4 * QH * g:4 * QH * (g + 1)],
                                                 start=k == 0, stop=k == 2)
                            J.filled(last)
                if step in ("turn_sides", "turn"):
                    if step == "turn" and i:
                        pe.wait_ge(S("q_ready"), i)
                        for g in range(2):
                            turns(("qT", g), lambda b: [(b[0:QH, k * n:k * n + n], q[0:n, 4 * g + k, :])
                                                        for k in range(4)])
                    for name, src in ((("KT", w_ex), ("RT", w_inc)) if step == "turn_sides" else (("khT", kt), ("BT", a))):
                        if name == "RT" and not i:
                            continue
                        pe.wait_ge(S(f"{name}_src"), i if name == "RT" else i + 1)
                        turns(name, lambda b: [(b[:, k * n:k * n + n], src[0:n, P * k:P * k + P]) for k in range(4)])
                if step == "gram":
                    pairs = [("A", KT, BT), ("AT", BTn, KT), ("C", khT, KT)]
                    if i:
                        pairs += [("Q", khT, RT), ("P", BT, RT)]
                    pe.wait_ge(S("BTp_out"), i + 1)
                    for name in ("KT", "khT", "BT") + (("RT",) if i else ()):
                        J.wait_taken(pe, (i, name))
                    for name, lhs, rhs in pairs:
                        for g in range(2):
                            bank = J.fill(pe, (i, name, g))
                            r = slice(HD * g, HD * g + HD)
                            for k in range(PAIRS):
                                last = pe.matmul(bank[0:n, k * n:k * n + n], lhs[r, k, 0:n], rhs[r, k, 0:n],
                                                 start=True, stop=True)
                            J.filled(last)
                    for g in range(2):
                        J.wait_taken(pe, (i, "C", g))
                    if i:
                        pe.wait_ge(S("zr_ready"), chunk_no(i, 0))
                    for h in range(HEADS):
                        pe.matmul(Z[0:n, HD * h:HD * h + HD], F[0:n, h, 0:n], V[:, HD * h:HD * h + HD],
                                  start=h == 0, stop=False, skip_group_check=True)
                    if i:
                        for g in range(2):
                            J.wait_taken(pe, (i, "Q", g))
                        if i >= 2:
                            pe.wait_ge(S("y_out"), i - 1)
                        for h in range(HEADS):
                            last = pe.matmul(Y[0:n, HD * h:HD * h + HD], XA[0:n, h, 0:n], V[:, HD * h:HD * h + HD],
                                             start=h == 0, stop=False, skip_group_check=True)
                    for g in range(2):
                        J.wait_taken(pe, (i, "A", g))
                        J.wait_taken(pe, (i, "AT", g))
                if step == "newton_t":
                    x = XA if v else X0
                    for g in range(2):
                        if v:
                            J.wait_taken(pe, (i, "X", v - 1, g))
                        bank = J.fill(pe, (i, "T", v, g))
                        for hh in range(4):
                            h = 4 * g + hh
                            last = pe.matmul(bank[0:n, hh * n:hh * n + n], x[0:n, h, 0:n], IA[0:n, h, 0:n],
                                             start=True, stop=True)
                        J.filled(last)
                if step == "newton_x":
                    x = XA if v else X0
                    for g in range(2):
                        J.wait_taken(pe, (i, "T", v, g))
                        bank = J.fill(pe, (i, "X", v, g))
                        for hh in range(4):
                            h = 4 * g + hh
                            last = pe.matmul(bank[0:n, hh * n:hh * n + n], F[0:n, h, 0:n], x[0:n, h, 0:n],
                                             start=True, stop=True)
                        J.filled(last)
                if step in ("scan_z", "scan_sa", "scan_s"):
                    m = chunk_no(i, v)
                    R = slice(CHUNK * v, CHUNK * v + min(n, CHUNK))
                if step == "scan_z":
                    if v == 0:
                        for g in range(2):
                            J.wait_taken(pe, (i, "X", LEVELS[n] - 1, g))
                        if i:
                            for g in range(2):
                                J.wait_taken(pe, (i, "P", g))
                    pe.wait_ge(S("state_ready"), m + 1)
                    times_state(i, Z, KT, R, 0, "z_even", m)
                    times_state(i, Z, KT, R, 1, "z_ready", m)
                    if i:
                        times_state(i, Y, RT, R, 1, "y_odd", m - 1)
                        times_state(i, Y, RT, R, 0, "y_even", m - 1)
                if step == "scan_sa":
                    pe.wait_ge(S("zr_ready"), m + 1)
                    bank = J.fill(pe, (i, "SA", v))
                    for h in range(HEADS):
                        last = pe.matmul(bank[R, HD * h:HD * h + HD], XA[R, h, R], zr[R, HD * h:HD * h + HD],
                                         start=True, stop=True)
                    J.filled(last)
                if step == "scan_s":
                    J.wait_taken(pe, (i, "SA", v))
                    bank = J.fill(pe, (i, "S", v))
                    for h in range(HEADS):
                        cols = slice(HD * h, HD * h + HD)
                        out = bank[HD * (h % 2):HD * (h % 2) + HD, HD * (h // 2):HD * (h // 2) + HD]
                        pe.matmul(out, a[R, cols], SA[R, cols], start=True, stop=False)
                        last = pe.matmul(out, kt[R, cols], p_[R, 2 * W + HD * h:2 * W + HD * h + HD],
                                         start=False, stop=True)
                    J.filled(last)
                    if v == 1:
                        for h in range(HEADS):
                            cols = slice(HD * h, HD * h + HD)
                            last = pe.matmul(Y[:, cols], PT[:, h, :], SA[:, cols], start=False, stop=True,
                                             skip_group_check=True)
                        last.then_inc(S("y_ready"), 1)
                if step == "score":
                    if v == 0:
                        for g in range(2):
                            J.wait_taken(pe, (i, ("qT", g)))
                            J.wait_taken(pe, (i, "kn", g))
                        J.wait_taken(pe, (i, "cT"))
                        bank = J.fill(pe, (i, "sm"))
                        for h in range(HEADS):
                            last = pe.matmul(bank[0:n, META * h:META * h + META], qT[:, h, 0:n], kTall[:, h, 0:META],
                                             start=True, stop=True)
                        J.filled(last)
                    m = HEADS * (i - 1) + v
                    if m:
                        pe.wait_ge(S("exp_done"), m)
                    for k0 in range(0, P * i, 512):
                        k1 = min(k0 + 512, P * i)
                        last = pe.matmul(SC[:, k0:k1], qT[:, v, :], kTall[:, v, META + k0:META + k1],
                                         start=True, stop=k1 < P * i, skip_group_check=True)
                    last = pe.matmul(SC[:, P * (i - 1):P * i], M["rowpair"][:, 0, :], M["rowpair"][:, 1, :],
                                     start=False, stop=True, skip_group_check=True)
                    last.then_inc(S("scored"), 1)
                if step == "weights":
                    pe.wait_ge(S("exp_done"), HEADS * (i - 1) + v + 1)
                    for j, group in enumerate(key_jobs(i)):
                        turns(("PT", v, j), lambda b: [(b[:, P * x:P * x + P], Pb[v % 2][:, P * (t - 1):P * t])
                                                       for x, t in enumerate(group)])
                if step == "values":
                    for j, group in enumerate(key_jobs(i)):
                        J.wait_taken(pe, (i, ("PT", v, j)))
                        if v == 0 and j == 0:
                            J.wait_taken(pe, (i, "v"))
                            if i >= 2:
                                pe.wait_ge(S("o_out"), i - 1)
                        slot = (pv_before(i, v) + j) % 2
                        for x, t in enumerate(group):
                            last = pe.matmul(O[:, HD * v:HD * v + HD], PTb[slot][:, x, :],
                                             vall[:, t - 1, HD * v:HD * v + HD],
                                             start=v == 0 and t == 1, stop=False, skip_group_check=True)
                        last.then_inc(S("pv_done"), 1)
                if step == "merge":
                    pe.wait_ge(S("expm_done"), HEADS * i)
                    turns("pmT", lambda b: [(b[:, 0:n], pm[:, :, :].rearrange("p h m -> p (h m)"))])
                    J.wait_taken(pe, (i, "pmT"))
                    if i == 1:
                        pe.wait_ge(S("vbd_ready"), 16 * HEADS)
                    pe.matmul(O[:, :], pmT[:, :], vbd[:, :], start=False, stop=True, skip_group_check=True)\
                      .then_inc(S("o_ready"), 1)

        @block.sync
        def _(sp):
            def load(i):
                t0, n = TILES[i]
                if i >= 2:
                    sp.wait_ge(S("state_ready"), chunk_no(i - 1, 0) + 1)
                    sp.wait_ge(S("bonus_ready"), i - 1)
                sp.dma_start(pr[i % 2][0:n, :], io["p"][1 + t0:1 + t0 + n, :]).then_inc(S(f"pr_landed{i % 2}"), 16)
                if i:
                    for name in ("KT", "RT", "khT", "BT"):
                        if (i - 1, name) in J.number:
                            J.wait_filled(sp, (i - 1, name))
                    sp.wait_ge(S("kr_ready"), i)
                    if i >= 2:
                        sp.wait_ge(S("q_ready"), i - 1)
                sp.dma_start(prev[0:n, 0:C_RWKV], io["p"][t0:t0 + n, 0:C_RWKV]).then_inc(S("prev_landed"), 16)
                sp.dma_start(table[0:n, :], io["table"][t0:t0 + n, :]).then_inc(S("table_landed"), 16)

            def store_mix(i):
                t0, n = TILES[i]
                sp.wait_ge(S("rw_out"), i)
                sp.wait_ge(S("at_out"), i)
                sp.dma_start(io["mix"][t0 - META:t0 - META + n, :], mixed[:, :]).then_inc(S("mix_stored"), 16)

            load(0)
            for i in range(NP):
                t0, n = TILES[i]
                sp.wait_ge(S("c_ready"), i + 1)
                sp.dma_start(io["o_lat_p"][0, 0, t0:t0 + n, :], c[0:n, :]).then_inc(S("c_stored"), 16)
                sp.wait_ge(S("kr_ready"), i + 1)
                sp.dma_start(io["o_rope_p"][0, 0, t0:t0 + n, :], kr[0:n, :]).then_inc(S("kr_stored"), 16)
                if i + 1 < NP:
                    load(i + 1)
                if i == 0:
                    sp.wait_ge(S("vbd_zero"), 1)
                    J.wait_taken(sp, (0, "v"))
                    for h in range(HEADS):
                        sp.dma_start(vbd[META * h:META * h + META, HD * h:HD * h + HD], vmeta[:, HD * h:HD * h + HD])\
                          .then_inc(S("vbd_ready"), 16)
                if i >= 2:
                    store_mix(i - 1)
            store_mix(NP - 1)
            sp.wait_ge(S("state_ready"), chunk_no(NP - 1, 1) + 2)
            sp.dma_start(io["o_state_p"].rearrange("(g p) v -> p g v", p=P), state[:, :, :]).then_inc(S("state_stored"), 16)
            sp.wait_ge(S("state_stored"), 16)
            sp.wait_ge(S("c_stored"), 16 * NP)
            sp.wait_ge(S("kr_stored"), 16 * NP)
            sp.wait_ge(S("mix_stored"), 16 * (NP - 1))

        @block.gpsimd
        def _(pool):
            step = Steps(pool, S("pool_step"))
            pool.memset(vbd[:, :], 0.0).then_inc(S("vbd_zero"), 1)
            for s, i, v in schedule():
                t0, n = TILES[i]
                p_ = pr[i % 2]
                r_, k_, v_ = (p_[0:n, W * m:W * m + W] for m in range(3))
                a, kt, gate, bonus, wl = a_[i % 2], kt_[i % 2], gate_[i % 2], bonus_[i % 2], wl_[i % 2]
                if s == "shift_diff":
                    pool.wait_ge(S("sh_diff"), i + 1)
                    pool.tensor_tensor(prev[0:n, 0:C_RWKV], prev[0:n, 0:C_RWKV], M["mu"][0:n, :], ALU.mult).then_inc(S("sh_mu"), 1)
                if s == "norm":
                    pool.wait_ge(S("table_landed"), 16 * (i + 1))
                    pool.wait_ge(S(f"pr_landed{i % 2}"), 16 * (i // 2 + 1))
                    if i:
                        pool.wait_ge(S("kr_stored"), 16 * i)
                        J.wait_taken(pool, (i - 1, "cT"))
                    x = p_[0:n, C_IN - ROPE:C_IN]
                    cos, sin = table[0:n, 0:ROPE], table[0:n, ROPE:2 * ROPE]
                    step(pool.tensor_tensor(krt[0:n, 0:16], x[:, 16:32], sin[:, 0:16], ALU.mult))
                    step(pool.tensor_tensor(krt[0:n, 16:32], x[:, 0:16], sin[:, 16:32], ALU.mult))
                    step(pool.tensor_tensor(kr[0:n, :], x, cos, ALU.mult))
                    pool.tensor_tensor(kr[0:n, :], kr[0:n, :], krt[0:n, :], ALU.add).then_inc(S("kr_ready"), 1)
                if s == "lora_up":
                    J.wait_taken(pool, (i, "aaa"))
                    pool.tensor_scalar(a[0:n, :], a[0:n, :], 0.5, 0.5, ALU.mult, ALU.add).then_inc(S("a_ready"), 1)
                if s == "key_squares":
                    pool.wait_ge(S("shifted"), i + 1)
                    pool.tensor_tensor(kk[0:n, :], k_, M["k_k"][0:n, :], ALU.mult).then_inc(S("kk0_ready"), 1)
                if s == "keys":
                    pool.wait_ge(S("kt_ready"), i + 1)
                    if i >= 3:
                        pool.wait_ge(S("rw_out"), i - 2)
                    step(pool.tensor_tensor(bonus[0:n, :], r_, kt[0:n, :], ALU.mult))
                    pool.tensor_tensor(bonus[0:n, :], bonus[0:n, :], M["r_k"][0:n, :], ALU.mult).then_inc(S("rb_ready"), 1)
                if s == "products":
                    pool.wait_ge(S("kk_ready"), i + 1)
                    pool.tensor_tensor(a[0:n, :], kk[0:n, :], a[0:n, :], ALU.mult).then_inc(S("b_ready"), 1)
                    pool.wait_ge(S("bs_ready"), i + 1)
                    step(pool.tensor_tensor(heads(bonus[0:n, :]), heads(v_), bc(bs, n), ALU.mult))
                    pool.tensor_tensor(bonus[0:n, :], bonus[0:n, :], M["gn_b"][0:n, :], ALU.add).then_inc(S("bonus_ready"), 1)
                if s == "latent_rest" and i:
                    J.wait_taken(pool, (i, "q", 0))
                    J.wait_taken(pool, (i, "q", 1))
                    cos = table[:, 0:ROPE].unsqueeze(1).to_broadcast([P, HEADS, ROPE])
                    sa = table[:, ROPE:ROPE + 16].unsqueeze(1).to_broadcast([P, HEADS, 16])
                    sb_ = table[:, ROPE + 16:2 * ROPE].unsqueeze(1).to_broadcast([P, HEADS, 16])
                    step(pool.tensor_tensor(qt[:, :, 0:16], q[:, :, NOPE + 16:QH], sa, ALU.mult))
                    step(pool.tensor_tensor(qt[:, :, 16:32], q[:, :, NOPE:NOPE + 16], sb_, ALU.mult))
                    step(pool.tensor_tensor(q[:, :, NOPE:QH], q[:, :, NOPE:QH], cos, ALU.mult))
                    pool.tensor_tensor(q[:, :, NOPE:QH], q[:, :, NOPE:QH], qt, ALU.add).then_inc(S("q_ready"), 1)
                if s == "variance":
                    pool.wait_ge(S("yn_ready"), i)
                    pool.tensor_tensor(zr[:, :], zr[:, :], M["gn_g"][:, :], ALU.mult).then_inc(S("yg_ready"), 1)

        @block.scalar
        def _(act):
            for s, i, v in schedule():
                t0, n = TILES[i]
                p_ = pr[i % 2]
                a, kt, gate, bonus, wl = a_[i % 2], kt_[i % 2], gate_[i % 2], bonus_[i % 2], wl_[i % 2]
                if s == "norm":
                    act.wait_ge(S(f"pr_landed{i % 2}"), 16 * (i // 2 + 1))
                    if i:
                        act.wait_ge(S("sq_read"), i)
                        act.wait_ge(S("kk_ready"), i)
                    for m, (c0, width) in enumerate(((C_RWKV, Q_LORA), (C_RWKV + Q_LORA, KV_LORA))):
                        act.activation(tmp[0:n, 0:width], p_[0:n, c0:c0 + width], ACT.Square,
                                       accum_out=ssq[0:n, m:m + 1]).then_inc(S("ssq_ready"), 1)
                        act.wait_ge(S("ssq_ready"), 2 * i + m + 1)
                if s == "turn_latent":
                    bank = J.take(act, (i, "cT"))
                    act.activation(cT[:, :, 0:n], bank[:, 0:2 * n].rearrange("p (k n) -> p k n", k=2), ACT.Copy)\
                       .then_inc(S("cT_out"), 1)
                    src = bank[NOPE:QH, 2 * n:3 * n].unsqueeze(1).to_broadcast([ROPE, HEADS, n])
                    J.taken(act.activation(kTall[NOPE:QH, :, t0:t0 + n], src, ACT.Copy), (i, "cT"))
                    if i:
                        bank = J.take(act, (i, "qnT"))
                        J.taken(act.activation(qnT[:, :, :], bank[:, 0:3 * n].rearrange("p (k n) -> p k n", k=3),
                                               ACT.Copy), (i, "qnT"))
                        J.wait_taken(act, (i, "cT"))
                if s == "lora":
                    act.wait_ge(S("shifted"), i + 1)
                    act.activation(la[0:n, :], p_[0:n, 3 * W:3 * W + LORA], ACT.Tanh).then_inc(S("la_ready"), 1)
                    act.activation(lg[0:n, :], p_[0:n, 3 * W + 2 * LORA:C_RWKV], ACT.Tanh, scale=0.5)\
                       .then_inc(S("lg_tanh"), 1)
                    act.wait_ge(S("lg_tanh"), i + 1)
                    act.activation(lg[0:n, :], lg[0:n, :], ACT.Copy, scale=0.5, bias=0.5).then_inc(S("la_ready"), 1)
                if s == "turn_lora":
                    bank = J.take(act, (i, "loraT"))
                    act.activation(laT[0:LORA, :, 0:n], bank[0:LORA, 0:2 * n].rearrange("p (k n) -> p k n", k=2),
                                   ACT.Copy).then_inc(S("laT_out"), 1)
                    J.taken(act.activation(lgT[:, 0:n], bank[:, 2 * n:3 * n], ACT.Copy), (i, "loraT"))
                if s == "lora_up":
                    if i:
                        J.wait_filled(act, (i - 1, "AT", 1))
                    if i >= 2:
                        act.wait_ge(S("state_ready"), chunk_no(i - 1, 0) + 1)
                    if i >= 3:
                        act.wait_ge(S("rw_out"), i - 2)
                    for name, dst in (("dec", td), ("aaa", a)):
                        bank = J.take(act, (i, name))
                        J.taken(act.activation(dst[0:n, :], bank[0:n, :], ACT.Tanh, scale=0.5), (i, name))
                    bank = J.take(act, (i, "gate"))
                    J.taken(act.activation(gate[0:n, :], bank[0:n, :], ACT.Copy), (i, "gate"))
                if s == "decay":
                    bank = J.take(act, (i, "inc"))
                    act.activation(w_inc[0:n, :], bank[0:n, :], ACT.Exp, scale=HALF, bias=M["cvec"][0:n, 0:1])\
                       .then_inc(S("winc_ready"), 1)
                    J.taken(act.activation(w_inv[0:n, :], bank[0:n, :], ACT.Exp, scale=-HALF,
                                           bias=M["cvec"][0:n, 1:2]), (i, "inc"))
                    bank = J.take(act, (i, "ex"))
                    J.taken(act.activation(w_ex[0:n, :], bank[0:n, :], ACT.Exp, scale=HALF,
                                           bias=M["cvec"][0:n, 2:3]), (i, "ex"))
                    bank = J.take(act, (i, "total"))
                    col = 4 if i == 0 else 3
                    J.taken(act.activation(wl[:, :, :], bank[:, 0:8].rearrange("p (g c) -> p g c", g=PAIRS), ACT.Exp,
                                           scale=HALF, bias=M["cvec"][:, col:col + 1]), (i, "total"))
                if s == "key_squares":
                    act.wait_ge(S("kk0_ready"), i + 1)
                    act.activation(tmp[0:n, :], kk[0:n, :], ACT.Square).then_inc(S("kksq_ready"), 1)
                if s == "latent_rest":
                    bank = J.take(act, (i, "v"))
                    dst = vall[:, i - 1, :] if i else vmeta
                    J.taken(act.activation(dst, bank[0:n, :], ACT.Copy), (i, "v"))
                    if i:
                        for g in range(2):
                            bank = J.take(act, (i, "q", g))
                            J.taken(act.activation(q[:, 4 * g:4 * g + 4, :],
                                                   bank[:, 0:4 * QH].rearrange("p (h d) -> p h d", d=QH), ACT.Copy),
                                    (i, "q", g))
                if s == "turn_sides":
                    bank = J.take(act, (i, "KT"))
                    J.taken(act.activation(KT[:, :, 0:n], four(bank, n, P), ACT.Copy), (i, "KT"))
                if s == "turn":
                    bank = J.take(act, (i, "BT"))
                    act.activation(BT[:, :, 0:n], four(bank, n, P), ACT.Copy).then_inc(S("BTp_out"), 1)
                    J.taken(act.activation(BTn[:, :, 0:n], four(bank, n, P), ACT.Copy, scale=-1.0), (i, "BT"))
                    act.wait_ge(S("BTp_out"), i + 1)
                if s == "newton_x":
                    for g in range(2):
                        bank = J.take(act, (i, "X", v, g))
                        J.taken(act.activation(XA[0:n, 4 * g:4 * g + 4, 0:n], four(bank, n), ACT.Copy), (i, "X", v, g))
                if s == "scan_z":
                    m = chunk_no(i, v)
                    R = slice(CHUNK * v, CHUNK * v + min(n, CHUNK))
                    act.wait_ge(S("z_ready"), m + 1)
                    if v == 0 and i >= 2:
                        act.wait_ge(S("rw_out"), i - 1)
                    act.activation(zr[R, :], Z[R, :], ACT.Copy, scale=-1.0).then_inc(S("zr_ready"), 1)
                if s == "scan_s" and v == 1:
                    act.wait_ge(S("y_ready"), i)
                    act.activation(SA[:, :], Y[:, :], ACT.Copy).then_inc(S("y_out"), 1)
                if s == "mean":
                    act.wait_ge(S("yc_ready"), i)
                    act.activation(SA[:, :], zr[:, :], ACT.Square).then_inc(S("ysq_ready"), 1)
                if s == "score" and v == 0:
                    bank = J.take(act, (i, "sm"))
                    J.taken(act.activation(sm[:, :, :], bank[:, 0:P].rearrange("p (h m) -> p h m", h=HEADS), ACT.Copy),
                            (i, "sm"))
                if s == "score":
                    m = HEADS * (i - 1) + v
                    act.wait_ge(S("nb_ready"), m + 1)
                    if v >= 2:
                        act.wait_ge(S("pv_done"), pv_before(i, v - 1))
                    if v == 0 and i >= 2:
                        act.wait_ge(S("den_ready"), i - 1)
                    act.activation(Pb[v % 2][:, 0:P * i], SC[:, 0:P * i], ACT.Exp, scale=SCALE, bias=nb[:, v:v + 1],
                                   accum_out=rs[:, v:v + 1]).then_inc(S("exp_done"), 1)
                    act.activation(pm[:, v, :], sm[:, v, :], ACT.Exp, scale=SCALE, bias=nb[:, v:v + 1],
                                   accum_out=rsm[:, v:v + 1]).then_inc(S("expm_done"), 1)
                if s == "weights":
                    for j, group in enumerate(key_jobs(i)):
                        m = pv_before(i, v) + j
                        if m >= 2:
                            act.wait_ge(S("pv_done"), m - 1)
                        bank = J.take(act, (i, ("PT", v, j)))
                        w = P * len(group)
                        J.taken(act.activation(PTb[m % 2][:, 0:len(group), :],
                                               bank[:, 0:w].rearrange("p (k n) -> p k n", n=P), ACT.Copy), (i, ("PT", v, j)))
                if s == "merge":
                    bank = J.take(act, (i, "pmT"))
                    J.taken(act.activation(pmT[:, :], bank[:, 0:P], ACT.Copy), (i, "pmT"))
                if s == "finish":
                    act.wait_ge(S("o_out"), i)
                    act.wait_ge(S("kk_ready"), min(i + 3, NP))
                    act.activation(tmp[0:n, :], mixed[:, W:2 * W], ACT.Square, accum_out=ssq[:, 2:3])\
                       .then_inc(S("osq_ready"), 1)
                    act.wait_ge(S("osq_ready"), i)

        @block.vector
        def _(dve):
            step = Steps(dve, S("dve_step"))
            dve.memset(laT[LORA:LORA + 1, :, :], 1.0).then_inc(S("ones_set"), 1)
            for m in (IA, X0):
                step(dve.tensor_copy(m[:, :, :], ident[:, :].unsqueeze(1).to_broadcast([P, HEADS, P])))
            dve.memset(state[:, :, :], 0.0).then_inc(S("state_ready"), 1)
            for s, i, v in schedule(vector=True):
                t0, n = TILES[i]
                p_ = pr[i % 2]
                r_, k_, v_ = (p_[0:n, W * m:W * m + W] for m in range(3))
                a, kt, gate, bonus, wl = a_[i % 2], kt_[i % 2], gate_[i % 2], bonus_[i % 2], wl_[i % 2]
                if s == "shift_diff":
                    dve.wait_ge(S(f"pr_landed{i % 2}"), 16 * (i // 2 + 1))
                    dve.wait_ge(S("prev_landed"), 16 * (i + 1))
                    dve.tensor_tensor(prev[0:n, 0:C_RWKV], prev[0:n, 0:C_RWKV], p_[0:n, 0:C_RWKV], ALU.subtract)\
                       .then_inc(S("sh_diff"), 1)
                if s == "shift":
                    dve.wait_ge(S("sh_mu"), i + 1)
                    dve.tensor_tensor(p_[0:n, 0:C_RWKV], p_[0:n, 0:C_RWKV], prev[0:n, 0:C_RWKV], ALU.add)\
                       .then_inc(S("shifted"), 1)
                    dve.wait_ge(S("shifted"), i + 1)
                if s == "norm":
                    dve.wait_ge(S("ssq_ready"), 2 * i + 2)
                    step(dve.tensor_scalar(ms[0:n, 0:1], ssq[0:n, 0:1], 1.0 / Q_LORA, RMS_EPS, ALU.mult, ALU.add))
                    dve.tensor_scalar(ms[0:n, 1:2], ssq[0:n, 1:2], 1.0 / KV_LORA, RMS_EPS, ALU.mult, ALU.add)\
                       .then_inc(S("sq_read"), 1)
                    dve.wait_ge(S("sq_read"), i + 1)
                    rsqrt(dve, step, rs2[0:n, 0:2], ms[0:n, 0:2], t2[0:n, 0:2])
                    if i:
                        dve.wait_ge(S("c_stored"), 16 * i)
                        J.wait_taken(dve, (i - 1, "cT"))
                    dve.scalar_tensor_tensor(c[0:n, :], p_[0:n, C_RWKV + Q_LORA:C_RWKV + Q_LORA + KV_LORA], rs2[0:n, 1:2],
                                             M["kv_norm_g"][0:n, :], ALU.mult, ALU.mult).then_inc(S("c_ready"), 1)
                    if i >= 2:
                        J.wait_taken(dve, (i - 1, "qnT"))
                    dve.scalar_tensor_tensor(qn[0:n, :], p_[0:n, C_RWKV:C_RWKV + Q_LORA], rs2[0:n, 0:1],
                                             M["q_norm_g"][0:n, :], ALU.mult, ALU.mult).then_inc(S("qn_ready"), 1)
                if s == "keys":
                    dve.wait_ge(S("a_ready"), i + 1)
                    step(dve.scalar_tensor_tensor(kt[0:n, :], a[0:n, :], -1.0, M["k_a"][0:n, :], ALU.add, ALU.mult))
                    dve.scalar_tensor_tensor(kt[0:n, :], kt[0:n, :], 1.0, k_, ALU.add, ALU.mult)\
                       .then_inc(S("kt_ready"), 1)
                if s == "key_norm":
                    dve.wait_ge(S("kksq_ready"), i + 1)
                    step(dve.tensor_reduce(n2[0:n, :], heads(tmp[0:n, :]), X, ALU.add))
                    step(dve.tensor_scalar(n2[0:n, :], n2[0:n, :], 1e-24, None, ALU.max))
                    rsqrt(dve, step, rk[0:n, :], n2[0:n, :], t8[0:n, :])
                    dve.tensor_tensor(heads(kk[0:n, :]), heads(kk[0:n, :]), bc(rk, n), ALU.mult).then_inc(S("kk_ready"), 1)
                if s == "products":
                    dve.wait_ge(S("kt_ready"), i + 1)
                    dve.wait_ge(S("winc_ready"), i + 1)
                    J.wait_taken(dve, (i, "inc"))
                    J.wait_taken(dve, (i, "ex"))
                    if i:
                        dve.tensor_tensor(w_inc[0:n, :], r_, w_inc[0:n, :], ALU.mult).then_inc(S("RT_src"), 1)
                    dve.wait_ge(S("kk_ready"), i + 1)
                    dve.tensor_tensor(w_ex[0:n, :], kk[0:n, :], w_ex[0:n, :], ALU.mult).then_inc(S("KT_src"), 1)
                    dve.wait_ge(S("rb_ready"), i + 1)
                    dve.tensor_reduce(bs[0:n, :], heads(bonus[0:n, :]), X, ALU.add).then_inc(S("bs_ready"), 1)
                    dve.tensor_tensor(kt[0:n, :], kt[0:n, :], w_inv[0:n, :], ALU.mult).then_inc(S("khT_src"), 1)
                    dve.wait_ge(S("b_ready"), i + 1)
                    dve.tensor_tensor(a[0:n, :], a[0:n, :], w_inv[0:n, :], ALU.mult).then_inc(S("BT_src"), 1)
                if s == "latent_keys":
                    for g in range(2):
                        bank = J.take(dve, (i, "kn", g))
                        J.taken(dve.tensor_copy(kTall[0:NOPE, 4 * g:4 * g + 4, t0:t0 + n], four(bank, n, NOPE)),
                                (i, "kn", g))
                if s == "turn_sides" and i:
                    bank = J.take(dve, (i, "RT"))
                    J.taken(dve.tensor_copy(RT[:, :, 0:n], four(bank, n, P)), (i, "RT"))
                if s == "turn":
                    if i:
                        for g in range(2):
                            bank = J.take(dve, (i, ("qT", g)))
                            J.taken(dve.tensor_copy(qT[:, 4 * g:4 * g + 4, :], four(bank, n, QH)), (i, ("qT", g)))
                    bank = J.take(dve, (i, "khT"))
                    J.taken(dve.tensor_copy(khT[:, :, 0:n], four(bank, n, P)), (i, "khT"))
                if s == "gram":
                    for name, dst, mask in (("A", IA, lower), ("AT", X0, upper)):
                        for g in range(2):
                            bank = J.take(dve, (i, name, g))
                            J.taken(dve.copy_predicated(dst[0:n, g:HEADS:2, 0:n], bc4(mask.bitcast(I32), n),
                                                        four(bank, n)), (i, name, g))
                    for name, dst, mask in (("C", F, upper), ("Q", XA, upper_eq), ("P", PT, upper_eq))[0:3 if i else 1]:
                        for g in range(2):
                            bank = J.take(dve, (i, name, g))
                            J.taken(dve.tensor_tensor(dst[0:n, g:HEADS:2, 0:n], four(bank, n), bc4(mask, n),
                                                      ALU.mult), (i, name, g))
                if s == "newton_t":
                    for g in range(2):
                        bank = J.take(dve, (i, "T", v, g))
                        J.taken(dve.scalar_tensor_tensor(F[0:n, 4 * g:4 * g + 4, 0:n], four(bank, n), -1.0,
                                                         bc4(twice, n), ALU.mult, ALU.add), (i, "T", v, g))
                if s == "scan_sa":
                    R = slice(CHUNK * v, CHUNK * v + min(n, CHUNK))
                    bank = J.take(dve, (i, "SA", v))
                    J.taken(dve.tensor_copy(SA[R, :], bank[R, :]), (i, "SA", v))
                if s == "scan_s":
                    m = chunk_no(i, v)
                    if v == 0:
                        J.wait_taken(dve, (i, "total"))
                    bank = J.take(dve, (i, "S", v))
                    J.taken(dve.tensor_tensor(state[:, :, :], state[:, :, :],
                                              bank[:, 0:PAIRS * HD].rearrange("p (g v) -> p g v", g=PAIRS), ALU.add),
                            (i, "S", v))
                    J.wait_taken(dve, (i, "S", v))
                    dve.tensor_tensor(state[:, :, :], state[:, :, :],
                                      wl[:, :, v:v + 1].to_broadcast([P, PAIRS, HD]), ALU.mult)\
                       .then_inc(S("state_ready"), 1)
                    dve.wait_ge(S("state_ready"), m + 2)
                if s == "mean":
                    dve.wait_ge(S("y_out"), i)
                    step(dve.tensor_reduce(mu8[:, :], heads(SA[:, :]), X, ALU.add))
                    step(dve.tensor_scalar(mu8[:, :], mu8[:, :], 1.0 / HD, None, ALU.mult))
                    dve.tensor_tensor(heads(zr[:, :]), heads(SA[:, :]), bc(mu8, n), ALU.subtract)\
                       .then_inc(S("yc_ready"), 1)
                if s == "variance":
                    dve.wait_ge(S("ysq_ready"), i)
                    step(dve.tensor_reduce(v8[:, :], heads(SA[:, :]), X, ALU.add))
                    step(dve.tensor_scalar(v8[:, :], v8[:, :], 1.0 / HD, GN_EPS, ALU.mult, ALU.add))
                    rsqrt(dve, step, rs8[:, :], v8[:, :], t8[:, :])
                    dve.tensor_tensor(heads(zr[:, :]), heads(zr[:, :]), bc(rs8, n), ALU.mult).then_inc(S("yn_ready"), 1)
                if s == "gate_out":
                    dve.wait_ge(S("yg_ready"), i)
                    dve.wait_ge(S("bonus_ready"), i + 1)
                    step(dve.tensor_tensor(zr[:, :], zr[:, :], bonus[:, :], ALU.add))
                    if i == 1:
                        dve.wait_ge(S("vbd_ready"), 16 * HEADS)
                    else:
                        dve.wait_ge(S("mix_stored"), 16 * (i - 1))
                    J.wait_taken(dve, (i, "gate"))
                    dve.tensor_tensor(mixed[:, 0:W], zr[:, :], gate[:, :], ALU.mult).then_inc(S("rw_out"), 1)
                if s == "score":
                    m = HEADS * (i - 1) + v
                    if v == 0:
                        J.wait_taken(dve, (i, "sm"))
                        step(dve.tensor_reduce(mm[:, :], sm[:, :, :], X, ALU.max))
                    dve.wait_ge(S("scored"), m + 1)
                    step(dve.tensor_reduce(mxc[:, v:v + 1], SC[:, 0:P * i], X, ALU.max))
                    dve.tensor_scalar(nb[:, v:v + 1], mxc[:, v:v + 1], mm[:, v:v + 1], -SCALE, ALU.max, ALU.mult)\
                       .then_inc(S("nb_ready"), 1)
                if s == "merge":
                    dve.wait_ge(S("expm_done"), HEADS * i)
                    dve.tensor_tensor(den[:, :], rs[:, :], rsm[:, :], ALU.add).then_inc(S("den_ready"), 1)
                    dve.wait_ge(S("den_ready"), i)
                    step(dve.reciprocal(den[:, :], den[:, :]))
                    dve.wait_ge(S("o_ready"), i)
                    if i >= 2:
                        dve.wait_ge(S("mix_stored"), 16 * (i - 1))
                    dve.tensor_tensor(heads(mixed[:, W:2 * W]), heads(O[:, :]), bc(den, P), ALU.mult)\
                       .then_inc(S("o_out"), 1)
                if s == "finish":
                    dve.wait_ge(S("osq_ready"), i)
                    step(dve.tensor_scalar(ms[:, 2:3], ssq[:, 2:3], 1.0 / W, RMS_EPS, ALU.mult, ALU.add))
                    rsqrt(dve, step, rs2[:, 2:3], ms[:, 2:3], t2[:, 2:3])
                    dve.scalar_tensor_tensor(mixed[:, W:2 * W], mixed[:, W:2 * W], rs2[:, 2:3], M["mla_out_g"][:, :],
                                             ALU.mult, ALU.mult).then_inc(S("at_out"), 1)


KEYS = PAST + DEC_T
LEVELS_S = 3


def phase_mix_sample(nc, io, M):
    with ExitStack() as ctx:
        def sb(name, shape, dt=F32):
            return ctx.enter_context(nc.sbuf_tensor(name, shape, dt))

        def psum(name, shape):
            return ctx.enter_context(nc.psum_tensor(name, shape, F32))

        S = Semaphores(nc, io["semaphores"], "s_")
        B, T = DEC_B, DEC_T
        pr, table = sb("s_pr", [P, C_IN]), sb("s_table", [P, 2 * ROPE])
        prev = sb("s_prev", [P, 2 * HEADS * P])
        ctxT = prev[:, :].rearrange("p (k h b t) -> p k h b t", k=2, h=HEADS, b=B)
        la, lg = sb("s_la", [P, LORA]), sb("s_lg", [P, P])
        laT, lgT = sb("s_laT", [LORA + 1, 2, P]), sb("s_lgT", [P, P])
        td, a, gate, w_inc, w_inv, w_ex = (sb(f"s_{n}", [P, W]) for n in ("td", "a", "gate", "winc", "winv", "wex"))
        kk, kt, bonus, tmp = (sb(f"s_{n}", [P, W]) for n in ("kk", "kt", "bonus", "tmp"))
        wl = sb("s_wl", [P, PAIRS, B])
        KT, BT, khT, RT = (sb(f"s_{n}T", [P, PAIRS, P]) for n in ("K", "B", "kh", "R"))
        BTn = td[:, :].rearrange("p (k n) -> p k n", k=PAIRS)
        IA, X0, XA, F, PT = (sb(f"s_{n}", [P, HEADS, P]) for n in ("IA", "X0", "XA", "F", "PT"))
        zs, ys, SA = w_ex, w_inc, w_inv
        picked = [X0[:, 4 * i:4 * i + 4, :].rearrange("p h n -> p (h n)").rearrange("p (b v) -> p b v", b=B) for i in range(2)]
        spread = [F[:, 4 * i:4 * i + 4, :].rearrange("p h n -> p (h n)").rearrange("p (b v) -> p b v", b=B) for i in range(2)]
        state = sb("s_state", [P, PAIRS, B, HD])
        mixed, ssq = sb("s_mixed", [P, D]), sb("s_ssq", [P, 4])
        qn, c, kr, krt = sb("s_qn", [P, Q_LORA]), sb("s_c", [P, KV_LORA]), sb("s_kr", [P, ROPE]), sb("s_krt", [P, ROPE])
        q, qt = sb("s_q", [P, HEADS, QH]), sb("s_qt", [P, HEADS, ROPE])
        qnT = sb("s_qnT", [P, 3, P])
        both = sb("s_both", [QH, B * KEYS])
        wkT = both[0:NOPE, 0:HEADS * KV_LORA].rearrange("p (h l) -> p h l", h=HEADS)
        ropeT = both[NOPE:QH, :].rearrange("p (b n) -> p b n", b=B)
        qT = sb("s_qT", [QH, HEADS * P])
        qnopeT = qT[0:NOPE, :].rearrange("p (h n) -> p h n", h=HEADS)
        qropeT = qT[NOPE:QH, :].rearrange("p (b h t) -> p b h t", b=B, h=HEADS)
        qabsT = sb("s_qabsT", [P, 2, B, HEADS, T])
        latT = sb("s_latT", [P, 2, B, KEYS])
        lat, lat_new = sb("s_lat", [P, 2, B, KV_LORA]), sb("s_latnew", [T, B, KV_LORA])
        Pb = [sb(f"s_P{i}", [P, KEYS]) for i in range(2)]
        PTb = [sb(f"s_PTb{i}", [P, 3, P]) for i in range(2)]
        stat = sb("s_stat", [P, 64])
        n2, rk, t8, bs, mu8, v8, rs8, _ = (stat[:, 8 * m:8 * m + 8] for m in range(8))
        nb, rs = sb("s_nb", [P, B]), sb("s_rs", [P, B])
        ms, rs2, t2 = sb("s_ms", [P, 4]), sb("s_rs2", [P, 4]), sb("s_t2", [P, 4])
        O, Y, Z = psum("s_O", [P, 512]), psum("s_Y", [P, 512]), psum("s_Z", [P, 512])
        J = Jobs(S, [psum(f"s_R{i}", [P, 512]) for i in range(5)], "s")
        ident, twice = M["const"][:, C_IDENT, :], M["const"][:, C_TWICE, :]
        masks = sb("s_masks", [P, 3, P])
        lower, upper, upper_eq = (masks[:, m, :] for m in (C_LOWER, C_UPPER, C_UPPER_EQ))
        batch_of = M["ind"][:, 2:10].unsqueeze(2).to_broadcast([P, B, HD])
        r_, k_, v_ = (pr[:, W * m:W * m + W] for m in range(3))
        t0 = PROMPT
        block = ctx.enter_context(nc.Block())

        steps = ["shift", "norm", "lora", "latent", "decay", "keys", "turn", "absorb", "gram"]
        steps = [(s, None) for s in steps] + [("score", 0), ("newton", 0), ("attend", 0), ("score", 1), ("newton", 1),
                                              ("attend", 1), ("score", 2), ("newton", 2), ("attend", 2)]
        for v, rest in ((3, [("pick", 0)]), (4, [("scan", None)]), (5, [("update", 0)]), (6, [("update", 1)]), (7, [])):
            steps += [("score", v)] + rest + [("attend", v)]
        steps += [("group_norm", None), ("values", None)]

        def bc(ap8):
            return ap8.unsqueeze(2).to_broadcast([P, HEADS, HD])

        def bc4(m):
            return m.unsqueeze(1).to_broadcast([P, 4, P])

        def four(bank, rows=P):
            return bank[0:rows, 0:4 * P].rearrange("p (k n) -> p k n", k=4)

        def state_banks():
            return [(x, odd, g) for odd in range(2) for x in range(2) for g in range(PAIRS)]

        def used(eng, h):
            if (h - 1) % 2 == 0:
                eng.wait_ge(S("V_used"), (h - 1) // 2 + 1)
            else:
                eng.wait_ge(S("s_filled"), J.number[("S", (h - 1) // 2)] + 1)

        @block.tensor
        def _(pe):
            def turns(name, pieces, rows=P):
                bank = J.fill(pe, name)
                for out, src in pieces(bank):
                    last = pe.transpose(out, src, ident[0:rows, 0:rows])
                J.filled(last)

            for step, v in steps:
                if step == "norm":
                    pe.wait_ge(S("c_ready"), 1)
                    pe.wait_ge(S("kr_ready"), 1)
                    bank = J.fill(pe, "cT")
                    for k in range(2):
                        pe.transpose(bank[:, k * P:k * P + P], c[:, P * k:P * k + P], ident)
                    J.filled(pe.matmul(bank[NOPE:QH, 2 * P:3 * P], kr[:, :], ident, start=True, stop=True))
                    pe.wait_ge(S("qn_ready"), 1)
                    turns("qnT", lambda b: [(b[:, k * P:k * P + P], qn[:, P * k:P * k + P]) for k in range(3)])
                if step == "lora":
                    pe.wait_ge(S("la_ready"), 2)
                    pe.wait_ge(S("shifted"), 1)
                    turns("loraT", lambda b: [(b[0:LORA, 0:P], la[:, :]),
                                              (b[0:LORA, P:2 * P], pr[:, 3 * W + LORA:3 * W + 2 * LORA]),
                                              (b[:, 2 * P:3 * P], lg[:, :])])
                    pe.wait_ge(S("laT_out"), 1)
                    J.wait_taken(pe, "loraT")
                    pe.wait_ge(S("ones_set"), 1)
                    for name, lhs, rhs in (("dec", laT[:, 0, :], M["wdec"]), ("aaa", laT[:, 1, :], M["waaa"]),
                                           ("gate", lgT[:, :], M["wgate"])):
                        bank = J.fill(pe, name)
                        J.filled(pe.matmul(bank[:, :], lhs, rhs[:, :], start=True, stop=True))
                if step == "latent":
                    J.wait_taken(pe, "qnT")
                    for g in range(2):
                        bank = J.fill(pe, ("q", g))
                        for k in range(3):
                            last = pe.matmul(bank[:, 0:4 * QH], qnT[:, k, :], M["w_qb"][:, k, 4 * QH * g:4 * QH * (g + 1)],
                                             start=k == 0, stop=k == 2)
                        J.filled(last)
                if step == "decay":
                    pe.wait_ge(S("masks_landed"), 16)
                    J.wait_taken(pe, "dec")
                    for name, tri in (("inc", upper_eq), ("ex", upper)):
                        bank = J.fill(pe, name)
                        J.filled(pe.matmul(bank[:, :], tri, td[:, :], start=True, stop=True))
                    bank = J.fill(pe, "total")
                    for g in range(PAIRS):
                        last = pe.matmul(bank[:, B * g:B * g + B], td[:, P * g:P * g + P], M["ind"][:, 2:10],
                                         start=True, stop=True)
                    J.filled(last)
                if step == "turn":
                    for name, src in (("KT", w_ex), ("RT", w_inc), ("khT", kt), ("BT", a)):
                        pe.wait_ge(S(f"{name}_src"), 1)
                        turns(name, lambda b: [(b[:, k * P:k * P + P], src[:, P * k:P * k + P]) for k in range(4)])
                    pe.wait_ge(S("q_ready"), 1)
                    for g in range(2):
                        turns(("qT", g), lambda b: [(b[0:QH, k * P:k * P + P], q[:, 4 * g + k, :]) for k in range(4)])
                if step == "absorb":
                    pe.wait_ge(S("wkT_landed"), 16)
                    pe.wait_ge(S("qnope_out"), 2)
                    for k in range(2):
                        for g in range(2):
                            bank = J.fill(pe, ("abs", k, g))
                            for hh in range(4):
                                h = 4 * g + hh
                                last = pe.matmul(bank[:, P * hh:P * hh + P], wkT[:, h, P * k:P * k + P], qnopeT[:, h, :],
                                                 start=True, stop=True)
                            J.filled(last)
                if step == "gram":
                    pe.wait_ge(S("BTp_out"), 1)
                    for name in ("KT", "khT", "BT", "RT"):
                        J.wait_taken(pe, name)
                    for name, lhs, rhs in (("A", KT, BT), ("AT", BTn, KT), ("C", khT, KT), ("Q", khT, RT), ("P", BT, RT)):
                        for g in range(2):
                            bank = J.fill(pe, (name, g))
                            r = slice(HD * g, HD * g + HD)
                            for k in range(PAIRS):
                                last = pe.matmul(bank[:, k * P:k * P + P], lhs[r, k, :], rhs[r, k, :], start=True, stop=True)
                            J.filled(last)
                    for out, w, name in ((Z, F, "C"), (Y, XA, "Q")):
                        for g in range(2):
                            J.wait_taken(pe, (name, g))
                        for h in range(HEADS):
                            last = pe.matmul(out[:, HD * h:HD * h + HD], w[:, h, :], pr[:, 2 * W + HD * h:2 * W + HD * h + HD],
                                             start=h == 0, stop=name == "C", skip_group_check=True)
                        if name == "C":
                            last.then_inc(S("cv_done"), 1)
                    for g in range(2):
                        J.wait_taken(pe, ("A", g))
                        J.wait_taken(pe, ("AT", g))
                if step == "newton":
                    x = XA if v else X0
                    for g in range(2):
                        if v:
                            J.wait_taken(pe, ("X", v - 1, g))
                        bank = J.fill(pe, ("T", v, g))
                        for hh in range(4):
                            last = pe.matmul(bank[:, hh * P:hh * P + P], x[:, 4 * g + hh, :], IA[:, 4 * g + hh, :],
                                             start=True, stop=True)
                        J.filled(last)
                    for g in range(2):
                        J.wait_taken(pe, ("T", v, g))
                        bank = J.fill(pe, ("X", v, g))
                        for hh in range(4):
                            last = pe.matmul(bank[:, hh * P:hh * P + P], F[:, 4 * g + hh, :], x[:, 4 * g + hh, :],
                                             start=True, stop=True)
                        J.filled(last)
                if step == "score":
                    if v == 0:
                        for k in range(2):
                            for g in range(2):
                                J.wait_taken(pe, ("abs", k, g))
                        for g in range(2):
                            J.wait_taken(pe, ("qT", g))
                        pe.wait_ge(S("latT_out"), 1)
                        J.wait_taken(pe, "cT")
                        pe.wait_ge(S("latT_landed"), 16 * 2)
                        pe.wait_ge(S("ropeT_landed"), 16)
                    bank = J.fill(pe, ("SC", v))
                    for k in range(2):
                        pe.matmul(bank[:, 0:KEYS], qabsT[:, k, v].rearrange("p h t -> p (h t)"), latT[:, k, v, :],
                                  start=k == 0, stop=False)
                    J.filled(pe.matmul(bank[:, 0:KEYS], qropeT[:, v].rearrange("p h t -> p (h t)"), ropeT[:, v, :],
                                       start=False, stop=True))
                if step == "pick":
                    pe.wait_ge(S("state_landed"), 16 * PAIRS)
                    for x, odd, g in state_banks():
                        bank = J.fill(pe, ("pick", x, odd, g))
                        r = slice(HD * odd, HD * odd + HD)
                        J.filled(pe.matmul(bank[:, :], (KT, RT)[x][r, g, :],
                                           state[r, g].rearrange("p b v -> p (b v)"), start=True, stop=True))
                if step == "scan":
                    for g in range(2):
                        J.wait_taken(pe, ("X", LEVELS_S - 1, g))
                        J.wait_taken(pe, ("P", g))
                    pe.wait_ge(S("zr_ready"), 1)
                    bank = J.fill(pe, "SA")
                    for h in range(HEADS):
                        last = pe.matmul(bank[:, HD * h:HD * h + HD], XA[:, h, :], zs[:, HD * h:HD * h + HD],
                                         start=True, stop=True)
                    J.filled(last)
                    J.wait_taken(pe, "SA")
                    for h in range(HEADS):
                        cols = slice(HD * h, HD * h + HD)
                        last = pe.matmul(Y[:, cols], PT[:, h, :], SA[:, cols], start=False, stop=True, skip_group_check=True)
                    last.then_inc(S("y_ready"), 1)
                if step == "update":
                    for g in (0, 1) if v == 0 else (2, 3):
                        bank = J.fill(pe, ("S", g))
                        for odd in range(2):
                            h = 2 * g + odd
                            out, cols = bank[HD * odd:HD * odd + HD, :], slice(HD * h, HD * h + HD)
                            for m, (lhs, name) in enumerate(((a, "SA_spread"), (kt, "V_spread"))):
                                pe.wait_ge(S(name), h + 1)
                                last = pe.matmul(out, lhs[:, cols], spread[m][:, :, :].rearrange("p b v -> p (b v)"),
                                                 start=m == 0, stop=m == 1)
                                if m == 0:
                                    last.then_inc(S("SA_used"), 1)
                            if odd == 0:
                                last.then_inc(S("V_used"), 1)
                        J.filled(last)
                if step == "attend":
                    pe.wait_ge(S("p_normed"), v + 1)
                    bank = J.fill(pe, ("PT", v))
                    for k in range(2):
                        pe.transpose(bank[:, P * k:P * k + P], Pb[v % 2][:, P * k:P * k + P], ident)
                    J.filled(pe.transpose(bank[0:T, 2 * P:3 * P], Pb[v % 2][:, PAST:KEYS], ident))
                    J.wait_taken(pe, ("PT", v))
                    pe.wait_ge(S("lat_landed"), 32)
                    pe.wait_ge(S("latnew_landed"), 16 * B)
                    bank = J.fill(pe, ("ctx", v))
                    for k in range(2):
                        out, cols = bank[:, P * k:P * k + P], slice(P * k, P * k + P)
                        for m in range(2):
                            pe.matmul(out, lat[:, m, v, cols], PTb[v % 2][:, m, :], start=m == 0, stop=False)
                        last = pe.matmul(out, lat_new[:, v, cols], PTb[v % 2][0:T, 2, :], start=False, stop=True)
                    J.filled(last)
                if step == "values":
                    for m in range(B):
                        J.wait_taken(pe, ("ctx", m))
                    for h in range(HEADS):
                        col = 2 * HD * h + NOPE
                        for k in range(2):
                            last = pe.matmul(O[:, HD * h:HD * h + HD], ctxT[:, k, h].rearrange("p b t -> p (b t)"),
                                             M["w_kvb"][:, k, col:col + HD], start=k == 0, stop=k == 1)
                    last.then_inc(S("o_ready"), 1)

        @block.sync
        def _(sp):
            sp.dma_start(pr[:, :], io["p"][1 + t0:1 + t0 + P, :]).then_inc(S("pr_landed"), 16)
            sp.dma_start(masks[:, :, :], io["masks"].rearrange("m p n -> p m n")).then_inc(S("masks_landed"), 16)
            sp.dma_start(prev[:, 0:C_RWKV], io["prev"]).then_inc(S("prev_landed"), 16)
            sp.dma_start(table[:, :], io["table"][t0:t0 + P, :]).then_inc(S("table_landed"), 16)
            sp.dma_start(wkT, io["w_kT"].rearrange("(h n) l -> n h l", n=NOPE)).then_inc(S("wkT_landed"), 16)
            for k in range(2):
                sp.dma_start(latT[:, k, :, 0:PAST], io["cache_latT"][:, P * k:P * k + P, :].rearrange("b l n -> l b n"))\
                  .then_inc(S("latT_landed"), 16)
            sp.dma_start(ropeT[:, :, 0:PAST], io["cache_ropeT"].rearrange("b r n -> r b n")).then_inc(S("ropeT_landed"), 16)
            sp.dma_start(lat[:, 0, :, :],
                         io["cache_lat"][0, :, 0:P, :].rearrange("b n l -> n b l")).then_inc(S("lat_landed"), 16)
            sp.dma_start(lat[:, 1, :, :], io["cache_lat"][0, :, P:PAST, :].rearrange("b n l -> n b l"))\
              .then_inc(S("lat_landed"), 16)
            for g in range(PAIRS):
                sp.dma_start(state[:, g, :, :], io["state"][:, P * g:P * g + P, :].rearrange("b p v -> p b v"))\
                  .then_inc(S("state_landed"), 16)
            sp.wait_ge(S("c_ready"), 1)
            for b in range(B):
                sp.dma_start(lat_new[:, b, :], c[T * b:T * b + T, :]).then_inc(S("latnew_landed"), 16)
            sp.dma_start(io["o_lat_s"][0].rearrange("b t l -> (b t) l"), c[:, :]).then_inc(S("stored"), 16)
            sp.wait_ge(S("kr_ready"), 1)
            sp.dma_start(io["o_rope_s"][0].rearrange("b t r -> (b t) r"), kr[:, :]).then_inc(S("stored"), 16)
            for g in range(PAIRS):
                sp.wait_ge(S("state_new"), g + 1)
                sp.dma_start(io["o_state_s"][:, P * g:P * g + P, :].rearrange("b p v -> p b v"), state[:, g, :, :])\
                  .then_inc(S("stored"), 16)
            sp.wait_ge(S("rw_out"), 1)
            sp.wait_ge(S("at_out"), 1)
            sp.dma_start(io["mix"][SEQ:SEQ + P, :], mixed[:, :]).then_inc(S("stored"), 16)
            sp.wait_ge(S("stored"), 16 * (3 + PAIRS))

        @block.gpsimd
        def _(pool):
            step = Steps(pool, S("pool_step"))
            for s, v in steps:
                if s == "shift":
                    pool.wait_ge(S("sh_diff"), 1)
                    pool.tensor_tensor(prev[:, 0:C_RWKV], prev[:, 0:C_RWKV], M["mu"][:, :], ALU.mult).then_inc(S("sh_mu"), 1)
                if s == "norm":
                    pool.wait_ge(S("table_landed"), 16)
                    pool.wait_ge(S("pr_landed"), 16)
                    x = pr[:, C_IN - ROPE:C_IN]
                    step(pool.tensor_tensor(krt[:, 0:16], x[:, 16:32], table[:, ROPE:ROPE + 16], ALU.mult))
                    step(pool.tensor_tensor(krt[:, 16:32], x[:, 0:16], table[:, ROPE + 16:2 * ROPE], ALU.mult))
                    step(pool.tensor_tensor(kr[:, :], x, table[:, 0:ROPE], ALU.mult))
                    pool.tensor_tensor(kr[:, :], kr[:, :], krt[:, :], ALU.add).then_inc(S("kr_ready"), 1)
                if s == "lora":
                    J.wait_taken(pool, "aaa")
                    pool.tensor_scalar(a[:, :], a[:, :], 0.5, 0.5, ALU.mult, ALU.add).then_inc(S("a_ready"), 1)
                if s == "latent":
                    J.wait_taken(pool, ("q", 0))
                    J.wait_taken(pool, ("q", 1))
                    cos = table[:, 0:ROPE].unsqueeze(1).to_broadcast([P, HEADS, ROPE])
                    sa = table[:, ROPE:ROPE + 16].unsqueeze(1).to_broadcast([P, HEADS, 16])
                    sb_ = table[:, ROPE + 16:2 * ROPE].unsqueeze(1).to_broadcast([P, HEADS, 16])
                    step(pool.tensor_tensor(qt[:, :, 0:16], q[:, :, NOPE + 16:QH], sa, ALU.mult))
                    step(pool.tensor_tensor(qt[:, :, 16:32], q[:, :, NOPE:NOPE + 16], sb_, ALU.mult))
                    step(pool.tensor_tensor(q[:, :, NOPE:QH], q[:, :, NOPE:QH], cos, ALU.mult))
                    pool.tensor_tensor(q[:, :, NOPE:QH], q[:, :, NOPE:QH], qt[:, :, :], ALU.add).then_inc(S("q_ready"), 1)
                if s == "keys":
                    pool.wait_ge(S("shifted"), 1)
                    pool.tensor_tensor(kk[:, :], k_, M["k_k"][:, :], ALU.mult).then_inc(S("kk0_ready"), 1)
                    pool.wait_ge(S("kt_ready"), 1)
                    step(pool.tensor_tensor(bonus[:, :], r_, kt[:, :], ALU.mult))
                    pool.tensor_tensor(bonus[:, :], bonus[:, :], M["r_k"][:, :], ALU.mult).then_inc(S("rb_ready"), 1)
                    pool.wait_ge(S("kk_ready"), 1)
                    pool.tensor_tensor(a[:, :], kk[:, :], a[:, :], ALU.mult).then_inc(S("b_ready"), 1)
                    pool.wait_ge(S("bs_ready"), 1)
                    step(pool.tensor_tensor(heads(bonus[:, :]), heads(v_), bc(bs), ALU.mult))
                    pool.tensor_tensor(bonus[:, :], bonus[:, :], M["gn_b"][:, :], ALU.add).then_inc(S("bonus_ready"), 1)
                if s == "update":
                    for h in range(4 * v, 4 * v + 4):
                        if h:
                            used(pool, h)
                        else:
                            pool.wait_ge(S("s_filled"), J.number[("X", LEVELS_S - 1, 1)] + 1)
                        pool.tensor_tensor(spread[1][:, :, :], pr[:, 2 * W + HD * h:2 * W + HD * h + HD].unsqueeze(1)
                                           .to_broadcast([P, B, HD]), batch_of, ALU.mult).then_inc(S("V_spread"), 1)
                if s == "group_norm":
                    pool.wait_ge(S("yn_ready"), 1)
                    pool.tensor_tensor(td[:, :], td[:, :], M["gn_g"][:, :], ALU.mult).then_inc(S("yg_ready"), 1)

        @block.scalar
        def _(act):
            for s, v in steps:
                if s == "norm":
                    act.wait_ge(S("pr_landed"), 16)
                    for m, (c0, width) in enumerate(((C_RWKV, Q_LORA), (C_RWKV + Q_LORA, KV_LORA))):
                        act.activation(tmp[:, 0:width], pr[:, c0:c0 + width], ACT.Square, accum_out=ssq[:, m:m + 1])\
                           .then_inc(S("ssq_ready"), 1)
                        act.wait_ge(S("ssq_ready"), m + 1)
                    bank = J.take(act, "cT")
                    for k in range(2):
                        last = act.activation(latT[:, k, :, PAST:KEYS],
                                              bank[:, P * k:P * k + P].rearrange("p (b t) -> p b t", b=B), ACT.Copy)
                    last.then_inc(S("latT_out"), 1)
                    J.taken(act.activation(ropeT[:, :, PAST:KEYS],
                                           bank[NOPE:QH, 2 * P:3 * P].rearrange("p (b t) -> p b t", b=B), ACT.Copy), "cT")
                    bank = J.take(act, "qnT")
                    J.taken(act.activation(qnT[:, :, :], bank[:, 0:3 * P].rearrange("p (k n) -> p k n", k=3), ACT.Copy), "qnT")
                if s == "lora":
                    act.wait_ge(S("shifted"), 1)
                    act.activation(la[:, :], pr[:, 3 * W:3 * W + LORA], ACT.Tanh).then_inc(S("la_ready"), 1)
                    act.activation(lg[:, :], pr[:, 3 * W + 2 * LORA:C_RWKV], ACT.Tanh, scale=0.5).then_inc(S("lg_tanh"), 1)
                    act.wait_ge(S("lg_tanh"), 1)
                    act.activation(lg[:, :], lg[:, :], ACT.Copy, scale=0.5, bias=0.5).then_inc(S("la_ready"), 1)
                    bank = J.take(act, "loraT")
                    act.activation(laT[0:LORA, :, :], bank[0:LORA, 0:2 * P].rearrange("p (k n) -> p k n", k=2),
                                   ACT.Copy).then_inc(S("laT_out"), 1)
                    J.taken(act.activation(lgT[:, :], bank[:, 2 * P:3 * P], ACT.Copy), "loraT")
                    for name, dst in (("dec", td), ("aaa", a)):
                        bank = J.take(act, name)
                        J.taken(act.activation(dst[:, :], bank[:, :], ACT.Tanh, scale=0.5), name)
                    bank = J.take(act, "gate")
                    J.taken(act.activation(gate[:, :], bank[:, :], ACT.Copy), "gate")
                if s == "latent":
                    for g in range(2):
                        bank = J.take(act, ("q", g))
                        J.taken(act.activation(q[:, 4 * g:4 * g + 4, :],
                                               bank[:, 0:4 * QH].rearrange("p (h d) -> p h d", d=QH), ACT.Copy), ("q", g))
                if s == "decay":
                    bank = J.take(act, "inc")
                    act.activation(w_inc[:, :], bank[:, :], ACT.Exp, scale=HALF, bias=M["cvec"][:, 5:6])\
                       .then_inc(S("winc_ready"), 1)
                    J.taken(act.activation(w_inv[:, :], bank[:, :], ACT.Exp, scale=-HALF, bias=M["cvec"][:, 6:7]), "inc")
                    bank = J.take(act, "ex")
                    J.taken(act.activation(w_ex[:, :], bank[:, :], ACT.Exp, scale=HALF, bias=M["cvec"][:, 7:8]), "ex")
                    bank = J.take(act, "total")
                    J.taken(act.activation(wl[:, :, :], bank[:, 0:PAIRS * B].rearrange("p (g c) -> p g c", g=PAIRS), ACT.Exp,
                                           scale=HALF, bias=M["cvec"][:, 4:5]), "total")
                if s == "keys":
                    act.wait_ge(S("kk0_ready"), 1)
                    act.activation(tmp[:, :], kk[:, :], ACT.Square).then_inc(S("kksq_ready"), 1)
                if s == "turn":
                    bank = J.take(act, "KT")
                    J.taken(act.activation(KT[:, :, :], four(bank), ACT.Copy), "KT")
                    bank = J.take(act, "BT")
                    act.activation(BT[:, :, :], four(bank), ACT.Copy).then_inc(S("BTp_out"), 1)
                    J.taken(act.activation(BTn, four(bank), ACT.Copy, scale=-1.0), "BT")
                if s == "absorb":
                    for k in range(2):
                        for g in range(2):
                            bank = J.take(act, ("abs", k, g))
                            J.taken(act.activation(qabsT[:, k, :, 4 * g:4 * g + 4, :].rearrange("p b h t -> p h b t"),
                                                   bank[:, :].rearrange("p (h b t) -> p h b t", h=4, b=B), ACT.Copy),
                                    ("abs", k, g))
                if s == "newton":
                    for g in range(2):
                        bank = J.take(act, ("X", v, g))
                        if v == 0 and g == 0:
                            act.wait_ge(S("s_filled"), J.number[("T", 0, 0)] + 1)
                        J.taken(act.activation(XA[:, 4 * g:4 * g + 4, :], four(bank), ACT.Copy), ("X", v, g))
                if s == "score":
                    bank = J.take(act, ("SC", v))
                    act.wait_ge(S("nb_ready"), v + 1)
                    if v >= 2:
                        act.wait_ge(S("s_filled"), J.number[("PT", v - 2)] + 1)
                    J.taken(act.activation(Pb[v % 2][:, :], bank[:, 0:KEYS], ACT.Exp, scale=SCALE, bias=nb[:, v:v + 1],
                                           accum_out=rs[:, v:v + 1]), ("SC", v))
                if s == "attend":
                    bank = J.take(act, ("ctx", v))
                    J.taken(act.activation(ctxT[:, :, :, v, :], bank[:, 0:2 * P].rearrange("p (k h t) -> p k h t", k=2, h=HEADS),
                                           ACT.Copy), ("ctx", v))
                if s == "group_norm":
                    act.wait_ge(S("y_sum"), 1)
                    act.wait_ge(S("yc_ready"), 1)
                    act.activation(tmp[:, :], td[:, :], ACT.Square).then_inc(S("ysq_ready"), 1)
                if s == "values":
                    act.wait_ge(S("o_ready"), 1)
                    act.activation(mixed[:, W:2 * W], O[:, :], ACT.Copy).then_inc(S("o_out"), 1)
                    act.wait_ge(S("ysq_ready"), 1)
                    act.wait_ge(S("yv_read"), 1)
                    act.activation(tmp[:, :], O[:, :], ACT.Square, accum_out=ssq[:, 2:3]).then_inc(S("osq_ready"), 1)

        @block.vector
        def _(dve):
            step = Steps(dve, S("dve_step"))
            dve.memset(laT[LORA:LORA + 1, :, :], 1.0).then_inc(S("ones_set"), 1)
            for m in (IA, X0):
                step(dve.tensor_copy(m[:, :, :], ident.unsqueeze(1).to_broadcast([P, HEADS, P])))
            for s, v in steps:
                if s == "shift":
                    dve.wait_ge(S("pr_landed"), 16)
                    dve.wait_ge(S("prev_landed"), 16)
                    dve.tensor_tensor(prev[:, 0:C_RWKV], prev[:, 0:C_RWKV], pr[:, 0:C_RWKV], ALU.subtract)\
                       .then_inc(S("sh_diff"), 1)
                    dve.wait_ge(S("sh_mu"), 1)
                    dve.tensor_tensor(pr[:, 0:C_RWKV], pr[:, 0:C_RWKV], prev[:, 0:C_RWKV], ALU.add).then_inc(S("shifted"), 1)
                    dve.wait_ge(S("shifted"), 1)
                if s == "norm":
                    dve.wait_ge(S("ssq_ready"), 2)
                    step(dve.tensor_scalar(ms[:, 0:1], ssq[:, 0:1], 1.0 / Q_LORA, RMS_EPS, ALU.mult, ALU.add))
                    step(dve.tensor_scalar(ms[:, 1:2], ssq[:, 1:2], 1.0 / KV_LORA, RMS_EPS, ALU.mult, ALU.add))
                    rsqrt(dve, step, rs2[:, 0:2], ms[:, 0:2], t2[:, 0:2])
                    dve.scalar_tensor_tensor(c[:, :], pr[:, C_RWKV + Q_LORA:C_RWKV + Q_LORA + KV_LORA], rs2[:, 1:2],
                                             M["kv_norm_g"][:, :], ALU.mult, ALU.mult).then_inc(S("c_ready"), 1)
                    dve.scalar_tensor_tensor(qn[:, :], pr[:, C_RWKV:C_RWKV + Q_LORA], rs2[:, 0:1],
                                             M["q_norm_g"][:, :], ALU.mult, ALU.mult).then_inc(S("qn_ready"), 1)
                if s == "keys":
                    dve.wait_ge(S("a_ready"), 1)
                    step(dve.scalar_tensor_tensor(kt[:, :], a[:, :], -1.0, M["k_a"][:, :], ALU.add, ALU.mult))
                    dve.scalar_tensor_tensor(kt[:, :], kt[:, :], 1.0, k_, ALU.add, ALU.mult).then_inc(S("kt_ready"), 1)
                    dve.wait_ge(S("kt_ready"), 1)
                    dve.wait_ge(S("kksq_ready"), 1)
                    step(dve.tensor_reduce(n2, heads(tmp[:, :]), X, ALU.add))
                    step(dve.tensor_scalar(n2, n2, 1e-24, None, ALU.max))
                    rsqrt(dve, step, rk, n2, t8)
                    dve.tensor_tensor(heads(kk[:, :]), heads(kk[:, :]), bc(rk), ALU.mult).then_inc(S("kk_ready"), 1)
                    dve.wait_ge(S("winc_ready"), 1)
                    J.wait_taken(dve, "inc")
                    J.wait_taken(dve, "ex")
                    dve.tensor_tensor(w_inc[:, :], r_, w_inc[:, :], ALU.mult).then_inc(S("RT_src"), 1)
                    dve.wait_ge(S("kk_ready"), 1)
                    dve.tensor_tensor(w_ex[:, :], kk[:, :], w_ex[:, :], ALU.mult).then_inc(S("KT_src"), 1)
                    dve.wait_ge(S("rb_ready"), 1)
                    dve.tensor_reduce(bs, heads(bonus[:, :]), X, ALU.add).then_inc(S("bs_ready"), 1)
                    dve.tensor_tensor(kt[:, :], kt[:, :], w_inv[:, :], ALU.mult).then_inc(S("khT_src"), 1)
                    dve.wait_ge(S("b_ready"), 1)
                    dve.tensor_tensor(a[:, :], a[:, :], w_inv[:, :], ALU.mult).then_inc(S("BT_src"), 1)
                if s == "turn":
                    for name, dst in (("RT", RT), ("khT", khT)):
                        bank = J.take(dve, name)
                        J.taken(dve.tensor_copy(dst[:, :, :], four(bank)), name)
                    for g in range(2):
                        bank = J.take(dve, ("qT", g))
                        dve.tensor_copy(qnopeT[:, 4 * g:4 * g + 4, :], four(bank, NOPE)).then_inc(S("qnope_out"), 1)
                        src = bank[NOPE:QH, :].rearrange("p (h b t) -> p h b t", h=4, b=B)
                        J.taken(dve.tensor_copy(qropeT[:, :, 4 * g:4 * g + 4, :].rearrange("p b h t -> p h b t"), src),
                                ("qT", g))
                if s == "gram":
                    dve.wait_ge(S("masks_landed"), 16)
                    for name, dst, mask in (("A", IA, lower), ("AT", X0, upper)):
                        for g in range(2):
                            bank = J.take(dve, (name, g))
                            J.taken(dve.copy_predicated(dst[:, g:HEADS:2, :], bc4(mask.bitcast(I32)), four(bank)), (name, g))
                    for name, dst, mask in (("C", F, upper), ("Q", XA, upper_eq), ("P", PT, upper_eq)):
                        for g in range(2):
                            bank = J.take(dve, (name, g))
                            J.taken(dve.tensor_tensor(dst[:, g:HEADS:2, :], four(bank), bc4(mask), ALU.mult), (name, g))
                if s == "newton":
                    for g in range(2):
                        bank = J.take(dve, ("T", v, g))
                        J.taken(dve.scalar_tensor_tensor(F[:, 4 * g:4 * g + 4, :], four(bank), -1.0, bc4(twice),
                                                         ALU.mult, ALU.add), ("T", v, g))
                if s == "score":
                    bank = J.take(dve, ("SC", v))
                    step(dve.tensor_reduce(nb[:, v:v + 1], bank[:, 0:KEYS], X, ALU.max))
                    dve.tensor_scalar(nb[:, v:v + 1], nb[:, v:v + 1], -SCALE, None, ALU.mult).then_inc(S("nb_ready"), 1)
                if s == "attend":
                    J.wait_taken(dve, ("SC", v))
                    step(dve.reciprocal(rs[:, v:v + 1], rs[:, v:v + 1]))
                    dve.tensor_scalar(Pb[v % 2][:, :], Pb[v % 2][:, :], rs[:, v:v + 1], None, ALU.mult)\
                       .then_inc(S("p_normed"), 1)
                    bank = J.take(dve, ("PT", v))
                    if v >= 2:
                        dve.wait_ge(S("s_filled"), J.number[("ctx", v - 2)] + 1)
                    step(dve.tensor_copy(PTb[v % 2][:, 0:2, :], bank[:, 0:2 * P].rearrange("p (k n) -> p k n", k=2)))
                    J.taken(dve.tensor_copy(PTb[v % 2][0:T, 2, :], bank[0:T, 2 * P:3 * P]), ("PT", v))
                if s == "pick":
                    for m, (x, odd, g) in enumerate(state_banks()):
                        bank = J.take(dve, ("pick", x, odd, g))
                        J.taken(dve.tensor_tensor(picked[m % 2][:, :, :], bank[:, :].rearrange("p (b v) -> p b v", b=B),
                                                  batch_of, ALU.mult), ("pick", x, odd, g))
                        J.wait_taken(dve, ("pick", x, odd, g))
                        cols = slice(HD * (2 * g + odd), HD * (2 * g + odd) + HD)
                        step(dve.tensor_reduce((zs, ys)[x][:, cols], picked[m % 2][:, :, :].rearrange("p b v -> p v b"),
                                               X, ALU.add))
                    dve.wait_ge(S("cv_done"), 1)
                    dve.scalar_tensor_tensor(zs[:, :], Z[:, :], -1.0, zs[:, :], ALU.mult, ALU.subtract)\
                       .then_inc(S("zr_ready"), 1)
                if s == "scan":
                    bank = J.take(dve, "SA")
                    J.taken(dve.tensor_copy(SA[:, :], bank[:, :]), "SA")
                    J.wait_taken(dve, "SA")
                if s == "update":
                    J.wait_taken(dve, "total")
                    for g in (0, 1) if v == 0 else (2, 3):
                        for odd in range(2):
                            h = 2 * g + odd
                            if h:
                                dve.wait_ge(S("SA_used"), h)
                            dve.tensor_tensor(spread[0][:, :, :], SA[:, HD * h:HD * h + HD].unsqueeze(1)
                                              .to_broadcast([P, B, HD]), batch_of, ALU.mult).then_inc(S("SA_spread"), 1)
                        bank = J.take(dve, ("S", g))
                        J.taken(dve.tensor_tensor(state[:, g], state[:, g], bank[:, :].rearrange("p (b v) -> p b v", b=B),
                                                  ALU.add), ("S", g))
                        J.wait_taken(dve, ("S", g))
                        dve.tensor_tensor(state[:, g], state[:, g], wl[:, g, :].unsqueeze(2).to_broadcast([P, B, HD]),
                                          ALU.mult).then_inc(S("state_new"), 1)
                if s == "group_norm":
                    dve.wait_ge(S("y_ready"), 1)
                    dve.tensor_tensor(ys[:, :], Y[:, :], ys[:, :], ALU.add).then_inc(S("y_sum"), 1)
                    dve.wait_ge(S("y_sum"), 1)
                    step(dve.tensor_reduce(mu8, heads(ys[:, :]), X, ALU.add))
                    step(dve.tensor_scalar(mu8, mu8, 1.0 / HD, None, ALU.mult))
                    dve.tensor_tensor(heads(td[:, :]), heads(ys[:, :]), bc(mu8), ALU.subtract).then_inc(S("yc_ready"), 1)
                    dve.wait_ge(S("ysq_ready"), 1)
                    dve.tensor_reduce(v8, heads(tmp[:, :]), X, ALU.add).then_inc(S("yv_read"), 1)
                    dve.wait_ge(S("yv_read"), 1)
                    step(dve.tensor_scalar(v8, v8, 1.0 / HD, GN_EPS, ALU.mult, ALU.add))
                    rsqrt(dve, step, rs8, v8, t8)
                    dve.tensor_tensor(heads(td[:, :]), heads(td[:, :]), bc(rs8), ALU.mult).then_inc(S("yn_ready"), 1)
                    dve.wait_ge(S("yg_ready"), 1)
                    dve.wait_ge(S("bonus_ready"), 1)
                    step(dve.tensor_tensor(td[:, :], td[:, :], bonus[:, :], ALU.add))
                    J.wait_taken(dve, "gate")
                    dve.tensor_tensor(mixed[:, 0:W], td[:, :], gate[:, :], ALU.mult).then_inc(S("rw_out"), 1)
                if s == "values":
                    dve.wait_ge(S("osq_ready"), 1)
                    dve.wait_ge(S("o_out"), 1)
                    step(dve.tensor_scalar(ms[:, 2:3], ssq[:, 2:3], 1.0 / W, RMS_EPS, ALU.mult, ALU.add))
                    rsqrt(dve, step, rs2[:, 2:3], ms[:, 2:3], t2[:, 2:3])
                    dve.scalar_tensor_tensor(mixed[:, W:2 * W], mixed[:, W:2 * W], rs2[:, 2:3], M["mla_out_g"][:, :],
                                             ALU.mult, ALU.mult).then_inc(S("at_out"), 1)


def constants():
    at = np.arange(P)
    const, masks = np.zeros((N_CONST, P, P), np.float32), np.zeros((3, P, P), np.float32)
    for m, size in ((const, CHUNK), (masks, DEC_T)):
        same = at[:, None] // size == at[None, :] // size
        m[C_LOWER] = same & (at[None, :] < at[:, None])
        m[C_UPPER] = same & (at[:, None] < at[None, :])
        m[C_UPPER_EQ] = same & (at[:, None] <= at[None, :])
    const[C_IDENT] = np.eye(P)
    const[C_TWICE] = 2 * np.eye(P)
    cvec = np.zeros((P, 8), np.float32)
    cvec[:, 0], cvec[:, 2] = HALF * (at % CHUNK + 1), HALF * (at % CHUNK)
    cvec[:, 1] = -cvec[:, 0]
    cvec[:, 3], cvec[:, 4] = HALF * CHUNK, HALF * META
    cvec[:, 5], cvec[:, 7] = HALF * (at % DEC_T + 1), HALF * (at % DEC_T)
    cvec[:, 6] = -cvec[:, 5]
    ind = np.zeros((P, 10), np.float32)
    ind[at, at // CHUNK] = 1
    ind[at, 2 + at // DEC_T] = 1
    rowpair = np.stack([np.where(at < CHUNK, -1e30, 0.0), np.where(at < CHUNK, 0.0, 1.0)]).astype(np.float32)
    pos = np.concatenate([np.arange(PROMPT), np.tile(PAST + np.arange(DEC_T), DEC_B)]).astype(np.float32)
    inv = (10000.0 ** (-np.arange(0, ROPE, 2, dtype=np.float32) / ROPE)).astype(np.float32)
    ang = pos[:, None] * inv[None, :]
    cos, sin = np.cos(ang), np.sin(ang)
    table = np.concatenate([cos, cos, -sin, sin], 1).astype(np.float32)
    return {"const": const, "masks": masks, "cvec": cvec, "ind": ind, "rowpair": rowpair, "table": table,
            "ident": np.eye(P, dtype=np.float32)}



OUTS = {
    "o_y_p": (1, SEQ, D), "o_y_s": (DEC_B, DEC_T, D),
    "o_lat_p": (1, 1, PROMPT, KV_LORA), "o_rope_p": (1, 1, PROMPT, ROPE), "o_state_p": (W, HD),
    "o_shift_p": (1, 1, 1, C_RWKV),
    "o_lat_s": (1, DEC_B, DEC_T, KV_LORA), "o_rope_s": (1, DEC_B, DEC_T, ROPE), "o_state_s": (DEC_B, W, HD),
    "o_shift_s": (1, DEC_B, 1, C_RWKV),
}
SCRATCH = {"h": (TOKENS, D), "p": (TOKENS + 1, C_IN), "prev": (SAMPLE, C_RWKV), "mix": (SEQ + SAMPLE, D)}


def build(nc, io):
    def cleared(run, *args):
        io["semaphores"] = []
        run(nc, io, *args)
        nc.clear_and_free_semaphores(io["semaphores"])
        nc.all_engine_barrier()

    cleared(phase_project)
    with ExitStack() as ctx:
        def sb(name, shape, dt=F32):
            return ctx.enter_context(nc.sbuf_tensor(name, shape, dt))

        M = {}
        cleared(load_mix_weights, sb, M)
        cleared(phase_mix_prompt, M)
        cleared(phase_mix_sample, M)
    cleared(phase_mlp)


def kernel(**inputs):
    from concourse import bacc
    from concourse.bass_utils import run_bass_kernel_spmd

    arrays = {n: np.asarray(a) for n, a in inputs.items()}
    state, cache, rope = arrays.pop("state_rwkv"), arrays.pop("cache_mla_latent"), arrays.pop("cache_mla_rope")
    arrays["state"] = state[0].transpose(0, 1, 3, 2).reshape(DEC_B, W, HD)
    arrays["cache_lat"] = cache
    arrays["cache_latT"] = cache[0].transpose(0, 2, 1)
    arrays["cache_ropeT"] = rope[0].transpose(0, 2, 1)
    w_kvb = arrays["w_kvb"][0].reshape(KV_LORA, HEADS, 2 * HD)
    arrays["w_kT"] = w_kvb[:, :, 0:NOPE].transpose(1, 2, 0).reshape(HEADS * NOPE, KV_LORA)
    for n in ("ln1_g", "ln1_b", "ln2_g", "ln2_b"):
        arrays[n] = arrays[n][0]
    arrays.update(constants())
    arrays = {n: np.ascontiguousarray(a) for n, a in arrays.items()}

    nc = bacc.Bacc("TRN2", target_bir_lowering=False, num_devices=1)
    io = {n: nc.dram_tensor(n, a.shape, F32, kind="ExternalInput").ap() for n, a in arrays.items()}
    io.update({n: nc.dram_tensor(n, shape, F32, kind="ExternalOutput").ap() for n, shape in OUTS.items()})
    io.update({n: nc.dram_tensor(f"scratch_{n}", shape, F32, kind="Internal").ap() for n, shape in SCRATCH.items()})
    build(nc, io)
    got = dict(run_bass_kernel_spmd(nc, [arrays], core_ids=[0]).results[0])
    got["o_state_p"] = got["o_state_p"].reshape(1, 1, HEADS, HD, HD).transpose(0, 1, 2, 4, 3)
    got["o_state_s"] = got["o_state_s"].reshape(1, DEC_B, HEADS, HD, HD).transpose(0, 1, 2, 4, 3)
    return tuple(np.ascontiguousarray(got[n]) for n in OUTS)
```

```python
from contextlib import ExitStack

import numpy as np

import concourse.bass as bass
from concourse import mybir

F32 = mybir.dt.float32
F32R = mybir.dt.float32r
I32 = mybir.dt.int32
ALU = mybir.AluOpType
ACT = mybir.ActivationFunctionType
X = mybir.AxisListType.X

P = 128
D = 1024
KD = D // P
META = 16
SEQ = 1024
DEC_B, DEC_T = 8, 16
PAST = 256
SAMPLE = DEC_B * DEC_T
PROMPT = META + SEQ
TOKENS = PROMPT + SAMPLE
HEADS, HD = 8, 64
W = HEADS * HD
PAIRS = HEADS // 2
LORA = 64
C_RWKV = 3 * W + 2 * LORA + P
Q_LORA, KV_LORA, ROPE, NOPE = 384, 256, 32, 64
C_IN = C_RWKV + Q_LORA + KV_LORA + ROPE
QH = NOPE + ROPE
D_FF = 4 * D
ALPHA = 2.0 ** 0.25
LN_EPS, RMS_EPS, GN_EPS = 1e-5, 1e-6, 64e-5
DECAY = 0.6065306597126334
SCALE = QH ** -0.5
RSQRT_SEED = 0x5F3759DF

TILES = [(0, META)] + [(META + P * i, P) for i in range(SEQ // P + 1)]
LAST = len(TILES) - 1


class Semaphores:

    def __init__(self, nc, all_, prefix):
        self.nc, self.all, self.prefix, self.known = nc, all_, prefix, {}

    def __call__(self, name):
        if name not in self.known:
            self.known[name] = self.nc.alloc_semaphore(name=self.prefix + name)
            self.all.append(self.known[name])
        return self.known[name]


class Steps:

    def __init__(self, eng, sem):
        self.eng, self.sem, self.n = eng, sem, 0

    def __call__(self, ins):
        self.n += 1
        ins.then_inc(self.sem, 1)
        self.eng.wait_ge(self.sem, self.n)


def rsqrt(dve, step, y, x, t):
    step(dve.tensor_scalar(t.bitcast(I32), x.bitcast(I32), 1, None, ALU.arith_shift_right))
    step(dve.tensor_scalar(y.bitcast(I32), t.bitcast(I32), -1.0, float(RSQRT_SEED), ALU.mult, ALU.add))
    for _ in range(3):
        step(dve.tensor_tensor(t, y, y, ALU.mult))
        step(dve.scalar_tensor_tensor(t, t, -0.5, x, ALU.mult, ALU.mult))
        step(dve.scalar_tensor_tensor(y, t, 1.5, y, ALU.add, ALU.mult))


def layer_norm_stats(dve, step, x, st, mv, rs, t, n):
    step(dve.bn_stats(st[0:n, 0:6], x[:, 0:512]))
    step(dve.bn_stats(st[0:n, 6:12], x[:, 512:1024]))
    step(dve.bn_aggr(mv[0:n, 0:2], st[0:n, 0:12]))
    step(dve.tensor_scalar(mv[0:n, 1:2], mv[0:n, 1:2], LN_EPS, None, ALU.add))
    rsqrt(dve, step, rs[0:n, 0:1], mv[0:n, 1:2], t[0:n, 0:1])


def bcast(row, n=P):
    return row.rearrange("(a n) -> a n", a=1).broadcast_to([n, row.shape[-1]])


CH = C_IN // 8
N_CH = C_IN // CH
WINDOWS = [(P * w, 0) for w in range(TOKENS // P)] + [(TOKENS - P, P - TOKENS % P)]
NW = len(WINDOWS)


def phase_project(nc, io, M):
    with ExitStack() as ctx:
        def sb(name, shape, dt=F32):
            return ctx.enter_context(nc.sbuf_tensor(name, shape, dt))

        S = Semaphores(nc, io["semaphores"], "a_")
        x = [sb(f"a_x{i}", [P, D]) for i in range(2)]
        hn = [sb(f"a_hn{i}", [P, D]) for i in range(2)]
        g_row, b_row = sb("a_g", [P, D]), sb("a_b", [P, D])
        ident = sb("a_ident", [P, P])
        stats, mean, rstd, tmp = sb("a_st", [P, 12]), sb("a_mv", [P, 2]), sb("a_rs", [P, 1]), sb("a_t", [P, 1])
        hT = [sb("a_hT_hi", [P, KD, TOKENS], F32R), sb("a_hT_lo", [P, KD, TOKENS], F32R)]
        w_raw = [sb(f"a_w{i}", [P, KD, CH]) for i in range(2)]
        w_hi = [sb(f"a_wh{i}", [P, KD, CH], F32R) for i in range(2)]
        w_lo = [sb(f"a_wl{i}", [P, KD, CH], F32R) for i in range(2)]
        out = [sb(f"a_o{i}", [P, CH]) for i in range(4)]
        zero = sb("a_zero", [N_CH, CH])
        pT = [ctx.enter_context(nc.psum_tensor(f"a_pT{i}", [P, 4, P], F32)) for i in range(2)]
        pO = [ctx.enter_context(nc.psum_tensor(f"a_pO{i}", [P, 512], F32)) for i in range(4)]
        w_in = io["w_in"][0].rearrange("(k p) n -> p k n", p=P)
        block = ctx.enter_context(nc.Block())

        def x_rows(i):
            if i == 0:
                return io["meta_tokens"]
            if i == LAST:
                return io["x_sample"].rearrange("b t d -> (b t) d")
            return io["x_prompt"][0, P * (i - 1):P * i, :]

        @block.sync
        def _(sp):
            def load_w(c, slot):
                sp.dma_start(w_raw[slot][:, :, :], w_in[:, :, bass.ds(c * CH, CH)]).then_inc(S(f"w_landed{slot}"), 16)

            def store_p(c, half, w):
                (r0, skip), slot = WINDOWS[w], (NW * half + w) % 4
                sp.wait_ge(S("p_drained"), c * NW + w + 1)
                sp.dma_start(io["p"][1 + r0 + skip:1 + r0 + P, bass.ds(c * CH, CH)],
                             out[slot][skip:P, :]).then_inc(S(f"p_stored{slot}"), 16)

            def pair(c, more):
                for half in range(2):
                    if more:
                        sp.wait_ge(S("w_lo"), c + half + 1)
                        load_w(c + half + 2, half)
                    for w in range(NW):
                        store_p(c + half, half, w)

            sp.dma_start(ident[:, :], io["ident"]).then_inc(S("ident_landed"), 16)
            for i, (t0, n) in enumerate(TILES):
                if i >= 2:
                    sp.wait_ge(S("h_normed"), i - 1)
                sp.dma_start(x[i % 2][0:n, :], x_rows(i)).then_inc(S(f"x_landed{i % 2}"), 16)
                if i == 0:
                    sp.dma_start(g_row[:, :], bcast(io["ln_in_g"])).then_inc(S("gb_landed"), 16)
                    sp.dma_start(b_row[:, :], bcast(io["ln_in_b"])).then_inc(S("gb_landed"), 16)
                    load_w(0, 0)
                    load_w(1, 1)
            sp.wait_ge(S("zero_set"), 1)
            sp.dma_start(io["p"][0].rearrange("(c n) -> c n", n=CH), zero[:, :]).then_inc(S("zero_stored"), 16)
            pair(0, True)
            for dst, src in mix_loads(io, M):
                sp.dma_start(dst, src).then_inc(S("weights_landed"), 16)
            with sp.Fori(1, N_CH // 2 - 1) as j:
                pair(2 * j, True)
            pair(N_CH - 2, False)
            sp.wait_ge(S("zero_stored"), 16)
            sp.wait_ge(S("weights_landed"), 16 * len(mix_loads(io, M)))
            for slot in range(4):
                sp.wait_ge(S(f"p_stored{slot}"), 16 * (NW * N_CH // 4))
            rows = io["p"][1 + PROMPT:1 + TOKENS, 0:C_RWKV].rearrange("(b t) c -> b t c", b=DEC_B)
            prev = io["prev"].rearrange("(b t) c -> b t c", b=DEC_B)
            sp.dma_start(prev[:, 1:DEC_T, :], rows[:, 0:DEC_T - 1, :]).then_inc(S("shift_copied"), 16)
            sp.dma_start(prev[:, 0, :], io["state_shift"][0, :, 0, :]).then_inc(S("shift_copied"), 16)
            sp.dma_start(io["o_shift_s"][0, :, 0, :], rows[:, DEC_T - 1, :]).then_inc(S("shift_copied"), 16)
            sp.dma_start(io["o_shift_p"][0, 0], io["p"][PROMPT:PROMPT + 1, 0:C_RWKV]).then_inc(S("shift_copied"), 16)
            sp.wait_ge(S("shift_copied"), 64)

        @block.gpsimd
        def _(pool):
            pool.memset(zero[:, :], 0.0).then_inc(S("zero_set"), 1)
            for i, (t0, n) in enumerate(TILES):
                pool.wait_ge(S("h_normed"), i + 1)
                if i == 0:
                    pool.wait_ge(S("gb_landed"), 32)
                h = hn[i % 2][0:n, :]
                pool.tensor_tensor(h, h, g_row[0:n, :], ALU.mult).then_inc(S("h_scaled"), 1)
                pool.wait_ge(S("h_scaled"), i + 1)
                pool.tensor_tensor(h, h, b_row[0:n, :], ALU.add).then_inc(S("h_ready"), 1)
                pool.wait_ge(S("h_ready"), i + 1)
                pool.dma_start(io["h"][t0:t0 + n, :], h).then_inc(S(f"h_stored{i % 2}"), 16)
            for s in range(2):
                pool.wait_ge(S(f"h_stored{s}"), 16 * len(range(s, len(TILES), 2)))

        @block.scalar
        def _(act):
            def w_high(c, slot):
                act.wait_ge(S(f"w_landed{slot}"), (c - slot) * 8 + 16)
                act.activation(w_hi[slot][:, :, :], w_raw[slot][:, :, :], ACT.Copy).then_inc(S("w_hi"), 1)

            def h_high(i):
                t0, n = TILES[i]
                for b in range(2):
                    act.wait_ge(S("h_transposed"), 2 * i + b + 1)
                    act.activation(hT[0][:, 4 * b:4 * b + 4, t0:t0 + n], pT[b][:, :, 0:n], ACT.Copy)\
                       .then_inc(S("h_hi"), 1)

            def drain(c, half, w, store=True):
                u = NW * half + w
                act.wait_ge(S("p_filled"), c * NW + w + 1)
                if store:
                    act.wait_ge(S(f"p_stored{u % 4}"), (c - half) * 4 * NW + 16 * (u // 4))
                act.activation(out[u % 4][:, :], pO[u % 4][:, 0:CH], ACT.Copy).then_inc(S("p_drained"), 1)

            def pair(c, more):
                for half in range(2):
                    for w in range(NW):
                        drain(c + half, half, w)
                        if w == 1 and (half == 0 or more):
                            w_high(c + half + 1, 1 - half)

            w_high(0, 0)
            for i in range(3):
                h_high(i)
            for half in range(2):
                for w in range(NW):
                    if half == 0 and w + 3 <= LAST:
                        h_high(w + 3)
                    drain(half, half, w, store=NW * half + w >= 4)
                    if w == (5 if half == 0 else 1):
                        w_high(half + 1, 1 - half)
            with act.Fori(1, N_CH // 2 - 1) as j:
                pair(2 * j, True)
            pair(N_CH - 2, False)

        @block.vector
        def _(dve):
            step = Steps(dve, S("dve_step"))

            def w_low(c, slot):
                dve.wait_ge(S("w_hi"), c + 1)
                dve.tensor_tensor(w_lo[slot][:, :, :], w_raw[slot][:, :, :], w_hi[slot][:, :, :].bitcast(F32),
                                  ALU.subtract).then_inc(S("w_lo"), 1)

            def norm(i):
                t0, n = TILES[i]
                dve.wait_ge(S(f"x_landed{i % 2}"), 16 * (i // 2 + 1))
                layer_norm_stats(dve, step, x[i % 2][0:n, :], stats, mean, rstd, tmp, n)
                if i >= 2:
                    dve.wait_ge(S("h_transposed"), 2 * i - 2)
                    dve.wait_ge(S(f"h_stored{i % 2}"), 16 * (i // 2))
                dve.tensor_scalar(hn[i % 2][0:n, :], x[i % 2][0:n, :], mean[0:n, 0:1], rstd[0:n, 0:1],
                                  ALU.subtract, ALU.mult).then_inc(S("h_normed"), 1)
                dve.wait_ge(S("h_normed"), i + 1)

            def h_low(i):
                t0, n = TILES[i]
                for b in range(2):
                    dve.wait_ge(S("h_hi"), 2 * i + b + 1)
                    dve.tensor_tensor(hT[1][:, 4 * b:4 * b + 4, t0:t0 + n], pT[b][:, :, 0:n],
                                      hT[0][:, 4 * b:4 * b + 4, t0:t0 + n].bitcast(F32), ALU.subtract)\
                       .then_inc(S("h_lo"), 1)

            norm(0)
            for i in range(len(TILES)):
                if i < LAST:
                    norm(i + 1)
                h_low(i)
                if i == 1:
                    w_low(0, 0)
            w_low(1, 1)
            w_low(2, 0)
            with dve.Fori(1, N_CH // 2 - 1) as j:
                w_low(2 * j + 1, 1)
                w_low(2 * j + 2, 0)
            w_low(N_CH - 1, 1)

        @block.tensor
        def _(pe):
            def turn(i):
                t0, n = TILES[i]
                pe.wait_ge(S("h_ready"), i + 1)
                for b in range(2):
                    if i >= 1:
                        pe.wait_ge(S("h_lo"), 2 * i + b - 1)
                    for k in range(4):
                        last = pe.transpose(pT[b][:, k, 0:n], hn[i % 2][0:n, P * (4 * b + k):P * (4 * b + k + 1)],
                                            ident[0:n, 0:n])
                    last.then_inc(S("h_transposed"), 1)

            def project(c, half, w, first=False):
                r0, slot = WINDOWS[w][0], (NW * half + w) % 4
                if not first:
                    pe.wait_ge(S("p_drained"), c * NW + w - 3)
                parts = [(hT[0], w_hi[half]), (hT[0], w_lo[half]), (hT[1], w_hi[half])]
                for a, (h, wt) in enumerate(parts):
                    for k in range(KD):
                        last = pe.matmul(pO[slot][:, 0:CH], h[:, k, r0:r0 + P], wt[:, k, :],
                                         start=(a == 0 and k == 0), stop=(a == 2 and k == KD - 1))
                last.then_inc(S("p_filled"), 1)

            def pair(c):
                for half in range(2):
                    pe.wait_ge(S("w_lo"), c + half + 1)
                    for w in range(NW):
                        project(c + half, half, w)

            pe.wait_ge(S("ident_landed"), 16)
            for i in range(3):
                turn(i)
            pe.wait_ge(S("w_lo"), 1)
            for w in range(NW):
                pe.wait_ge(S("h_lo"), 2 * (min(w + 1, LAST) + 1))
                project(0, 0, w, first=w < 4)
                if w + 3 <= LAST:
                    turn(w + 3)
            pe.wait_ge(S("w_lo"), 2)
            for w in range(NW):
                project(1, 1, w)
            with pe.Fori(1, N_CH // 2 - 1) as j:
                pair(2 * j)
            pair(N_CH - 2)


BLK = 3
N_BLK = (SEQ + SAMPLE) // (BLK * P)
NT = BLK * P
NF = D_FF // P
UNITS = 2 * BLK
FIRST_DOWN = KD * N_BLK


def phase_mlp(nc, io):
    with ExitStack() as ctx:
        def sb(name, shape, dt=F32):
            return ctx.enter_context(nc.sbuf_tensor(name, shape, dt))

        S = Semaphores(nc, io["semaphores"], "c_")
        ident = sb("c_ident", [P, P])
        rows = {n: sb(f"c_{n}", [P, D]) for n in ("ln1_g", "ln1_b", "ln2_g", "ln2_b")}
        mix = sb("c_mix", [P, BLK, D])
        res = [sb(f"c_res{b}", [P, BLK, D]) for b in range(N_BLK)]
        zT_hi = [sb(f"c_zT_hi{i}", [P, KD, NT], F32R) for i in range(2)]
        zT_lo = [sb(f"c_zT_lo{i}", [P, KD, NT], F32R) for i in range(2)]
        row_raw = [sb(f"c_rw{i}", [P, D]) for i in range(2)]
        row_hi = [sb(f"c_rh{i}", [P, D], F32R) for i in range(2)]
        row_lo = [sb(f"c_rl{i}", [P, D], F32R) for i in range(2)]
        up_raw = [sb(f"c_uw{i}", [P, KD, P]) for i in range(2)]
        up_hi = [sb(f"c_uh{i}", [P, KD, P], F32R) for i in range(2)]
        up_lo = [sb(f"c_ul{i}", [P, KD, P], F32R) for i in range(2)]
        relu = [sb(f"c_relu{i}", [P, NT]) for i in range(2)]
        hid = [sb(f"c_hid{i}", [P, NT]) for i in range(2)]
        hid_hi = [sb(f"c_hh{i}", [P, NT], F32R) for i in range(2)]
        hid_lo = [sb(f"c_hl{i}", [P, NT], F32R) for i in range(2)]
        zero_raw, zero = sb("c_zero_raw", [P, 512]), sb("c_zero", [P, 512], F32R)
        stats, mean, rstd, tmp = sb("c_st", [P, 12]), sb("c_mv", [P, 2]), sb("c_rs", [P, 1]), sb("c_t", [P, 1])
        pY = [ctx.enter_context(nc.psum_tensor(f"c_pY{i}", [P, 512], F32)) for i in range(UNITS)]
        pU = [ctx.enter_context(nc.psum_tensor(f"c_pU{i}", [P, 512], F32)) for i in range(2)]
        w_up = io["w_up"][0].rearrange("(k p) n -> p k n", p=P)
        w_out, w_down = io["w_out"][0], io["w_down"][0]
        block = ctx.enter_context(nc.Block())

        def y_rows(b, t):
            i = BLK * b + t
            if i == SEQ // P:
                return io["o_y_s"].rearrange("b t d -> (b t) d")
            return io["o_y_p"][0, P * i:P * (i + 1), :]

        def down_tile(b, f):
            return FIRST_DOWN + NF * b + f

        def norm_beside(b):
            return (N_BLK - 1, "h1") if b == 0 else (b - 1, "y")

        @block.sync
        def _(sp):
            def load_row(src, r, slot):
                sp.dma_start(row_raw[slot][:, :], src[bass.ds(r, P), :]).then_inc(S(f"row_landed{slot}"), 16)

            def load_up(c, slot):
                sp.dma_start(up_raw[slot][:, :, :], w_up[:, :, bass.ds(c, P)]).then_inc(S(f"up_landed{slot}"), 16)

            def load_mix(b):
                sp.dma_start(mix[:, :, :], io["mix"][NT * b:NT * (b + 1), :].rearrange("(t p) d -> p t d", p=P))\
                  .then_inc(S("mix_landed"), 16)

            sp.dma_start(ident[:, :], io["ident"]).then_inc(S("ident_landed"), 16)
            load_mix(0)
            load_row(w_out, 0, 0)
            load_row(w_out, P, 1)
            def load_h(b):
                r0 = META + NT * b
                sp.dma_start(res[b][:, :, :], io["h"][r0:r0 + NT, :].rearrange("(t p) d -> p t d", p=P))\
                  .then_inc(S(f"h_landed{b}"), 16)

            def load_norm(n):
                sp.dma_start(rows[n][:, :], bcast(io[n])).then_inc(S("gb_landed"), 16)

            others = [(load_h, 0), (load_norm, "ln1_g"), (load_norm, "ln1_b"), (load_h, 1), (load_norm, "ln2_g"),
                      (load_norm, "ln2_b"), (load_up, 0, 0), (load_up, P, 1), (load_h, 2)]
            for b in range(N_BLK):
                if b + 1 < N_BLK:
                    sp.wait_ge(S("turned"), UNITS * (b + 1))
                    load_mix(b + 1)
                for k in range(KD):
                    sp.wait_ge(S("row_lo"), KD * b + k + 1)
                    if k + 2 < KD or b + 1 < N_BLK:
                        load_row(w_out, P * ((k + 2) % KD), k % 2)
                    else:
                        load_row(w_down, P * (k + 2 - KD), k % 2)
                    if k % 2 and others:
                        load, *what = others.pop(0)
                        load(*what)
            for b in range(N_BLK):
                with sp.Fori(0, NF // 2 - 1) as j:
                    for half in range(2):
                        sp.wait_ge(S("up_lo"), NF * b + 2 * j + half + 1)
                        load_up(P * (2 * j + half + 2), half)
                        sp.wait_ge(S("row_lo"), down_tile(b, 0) + 2 * j + half + 1)
                        load_row(w_down, P * (2 * j + half + 2), half)
                if b + 1 < N_BLK:
                    for half in range(2):
                        sp.wait_ge(S("up_lo"), NF * (b + 1) - 2 + half + 1)
                        load_up(P * half, half)
                        sp.wait_ge(S("row_lo"), down_tile(b + 1, 0) - 2 + half + 1)
                        load_row(w_down, P * half, half)

        @block.gpsimd
        def _(pool):
            scaled = [0]

            def scale_rows(b, kind, t):
                g, bb = ("ln1_g", "ln1_b") if kind == "h1" else ("ln2_g", "ln2_b")
                pool.wait_ge(S(f"{kind}_normed"), BLK * b + t + 1)
                r = res[b][:, t, :]
                scaled[0] += 1
                pool.tensor_tensor(r, r, rows[g][:, :], ALU.mult).then_inc(S("scaled"), 1)
                pool.wait_ge(S("scaled"), scaled[0])
                pool.tensor_tensor(r, r, rows[bb][:, :], ALU.add).then_inc(S(f"{kind}_ready"), 1)
                if kind == "y":
                    pool.wait_ge(S("y_ready"), BLK * b + t + 1)
                    pool.dma_start(y_rows(b, t), r).then_inc(S("y_stored"), 16)

            def square(b, f, half, first=False):
                u = NF * b + f + half
                pool.wait_ge(S("relu"), u + 1)
                if not first:
                    pool.wait_ge(S("hid_lo"), u - 1)
                pool.tensor_tensor(hid[half][:, :], relu[half][:, :], relu[half][:, :], ALU.mult)\
                    .then_inc(S("squared"), 1)

            pool.memset(zero_raw[:, :], 0.0).then_inc(S("zero_set"), 1)
            pool.wait_ge(S("gb_landed"), 64)
            for b in range(N_BLK - 1):
                for t in range(BLK):
                    scale_rows(b, "h1", t)
            for b in range(N_BLK):
                for f in range(4):
                    square(b, f - f % 2, f % 2, first=b == 0 and f < 2)
                    if f:
                        scale_rows(*norm_beside(b), f - 1)
                with pool.Fori(2, NF // 2) as j:
                    square(b, 2 * j, 0)
                    square(b, 2 * j, 1)
            scale_rows(N_BLK - 1, "y", 0)
            for t in range(1, BLK):
                pool.wait_ge(S("y_last"), t)
                pool.dma_start(y_rows(N_BLK - 1, t), res[N_BLK - 1][:, t, :]).then_inc(S("y_stored"), 16)
            pool.wait_ge(S("y_stored"), 16 * BLK * N_BLK)

        @block.scalar
        def _(act):
            def row_high(r, slot, first=False):
                act.wait_ge(S(f"row_landed{slot}"), 8 * (r - slot) + 16)
                if not first:
                    act.wait_ge(S("row_used"), r - 1)
                act.activation(row_hi[slot][:, :], row_raw[slot][:, :], ACT.Copy).then_inc(S("row_hi"), 1)

            def up_high(b, f, slot, first=False):
                act.wait_ge(S(f"up_landed{slot}"), 8 * (NF * b + f - slot) + 16)
                if not first:
                    act.wait_ge(S("up_done"), NF * b + f - 1)
                act.activation(up_hi[slot][:, :, :], up_raw[slot][:, :, :], ACT.Copy).then_inc(S("up_hi"), 1)

            def turned_high(n):
                for u in range(UNITS):
                    t, k4 = u // 2, 4 * (u % 2)
                    act.wait_ge(S("turned"), UNITS * n + u + 1)
                    act.activation(zT_hi[n % 2][:, k4:k4 + 4, P * t:P * (t + 1)],
                                   pU[u % 2][:, :].rearrange("p (k n) -> p k n", k=4), ACT.Copy)\
                       .then_inc(S("zT_hi"), 1)

            def hidden(b, f, half, more_row=True, more_up=True, first=False):
                u = NF * b + f + half
                act.wait_ge(S("up_done"), u + 1)
                if not first:
                    act.wait_ge(S("squared"), u - 1)
                act.activation(relu[half][:, :], pU[half][:, 0:NT], ACT.Relu).then_inc(S("relu"), 1)
                if more_row:
                    row_high(down_tile(b, 0) + f + half + 1, 1 - half)
                act.wait_ge(S("squared"), u + 1)
                act.wait_ge(S("row_used"), down_tile(b, 0) + f + half - 1)
                act.activation(hid_hi[half][:, :], hid[half][:, :], ACT.Copy).then_inc(S("hid_hi"), 1)
                if more_up:
                    up_high(b, f + half + 2, half)

            act.wait_ge(S("zero_set"), 1)
            act.activation(zero[:, :], zero_raw[:, :], ACT.Copy).then_inc(S("zero_ready"), 1)
            turned_high(0)
            for b in range(N_BLK):
                for k in range(KD):
                    row_high(KD * b + k, k % 2, first=b == 0 and k < 2)
                    if k == KD // 2:
                        turned_high(b + 1)
            for b in range(N_BLK):
                up_high(b, 0, 0, first=b == 0)
                up_high(b, 1, 1, first=b == 0)
                row_high(down_tile(b, 0), 0)
                hidden(b, 0, 0, first=b == 0)
                hidden(b, 0, 1, first=b == 0)
                with act.Fori(1, NF // 2 - 1) as j:
                    hidden(b, 2 * j, 0)
                    hidden(b, 2 * j, 1)
                hidden(b, NF - 2, 0, more_up=False)
                hidden(b, NF - 2, 1, more_row=False, more_up=False)
                if b + 1 < N_BLK:
                    turned_high(N_BLK + b + 1)

        @block.vector
        def _(dve):
            step = Steps(dve, S("dve_step"))

            def row_low(r, slot):
                dve.wait_ge(S("row_hi"), r + 1)
                dve.tensor_tensor(row_lo[slot][:, :], row_raw[slot][:, :], row_hi[slot][:, :].bitcast(F32),
                                  ALU.subtract).then_inc(S("row_lo"), 1)

            def up_low(b, f, slot):
                dve.wait_ge(S("up_hi"), NF * b + f + 1)
                dve.tensor_tensor(up_lo[slot][:, :, :], up_raw[slot][:, :, :], up_hi[slot][:, :, :].bitcast(F32),
                                  ALU.subtract).then_inc(S("up_lo"), 1)

            def turned_low(n):
                for u in range(UNITS):
                    t, k4 = u // 2, 4 * (u % 2)
                    dve.wait_ge(S("zT_hi"), UNITS * n + u + 1)
                    dve.tensor_tensor(zT_lo[n % 2][:, k4:k4 + 4, P * t:P * (t + 1)],
                                      pU[u % 2][:, :].rearrange("p (k n) -> p k n", k=4),
                                      zT_hi[n % 2][:, k4:k4 + 4, P * t:P * (t + 1)].bitcast(F32), ALU.subtract)\
                       .then_inc(S("zT_lo"), 1)

            def add_residual(b, kind):
                for u in range(UNITS):
                    x = res[b][:, u // 2, 512 * (u % 2):512 * (u % 2) + 512]
                    dve.scalar_tensor_tensor(x, x, ALPHA, pY[u][:, :], ALU.mult, ALU.add)\
                       .then_inc(S(f"{kind}_summed"), 1)

            def normalise(b, kind, t):
                dve.wait_ge(S(f"{kind}_summed"), UNITS * b + 2 * t + 2)
                x = res[b][:, t, :]
                layer_norm_stats(dve, step, x, stats, mean, rstd, tmp, P)
                dve.tensor_scalar(x, x, mean[:, 0:1], rstd[:, 0:1], ALU.subtract, ALU.mult)\
                   .then_inc(S(f"{kind}_normed"), 1)
                dve.wait_ge(S(f"{kind}_normed"), BLK * b + t + 1)

            def hidden_low(b, f, half):
                dve.wait_ge(S("hid_hi"), NF * b + f + half + 1)
                dve.tensor_tensor(hid_lo[half][:, :], hid[half][:, :], hid_hi[half][:, :].bitcast(F32),
                                  ALU.subtract).then_inc(S("hid_lo"), 1)

            def one(b, f, half, more_row=True, more_up=True):
                if more_row:
                    row_low(down_tile(b, 0) + f + half + 1, 1 - half)
                hidden_low(b, f, half)
                if more_up:
                    up_low(b, f + half + 2, half)

            turned_low(0)
            for b in range(N_BLK):
                for k in range(KD):
                    row_low(KD * b + k, k % 2)
                    if k == 1 and b:
                        dve.wait_ge(S("row_used"), KD * b)
                        dve.wait_ge(S(f"h_landed{b - 1}"), 16)
                        add_residual(b - 1, "h1")
                    if k >= 3 and k % 2 and b:
                        normalise(b - 1, "h1", (k - 3) // 2)
                    if k == KD // 2:
                        turned_low(b + 1)
            for b in range(N_BLK):
                up_low(b, 0, 0)
                up_low(b, 1, 1)
                row_low(down_tile(b, 0), 0)
                last, kind = norm_beside(b)
                dve.wait_ge(S("row_used"), down_tile(b, 0))
                if b == 0:
                    dve.wait_ge(S(f"h_landed{last}"), 16)
                add_residual(last, kind)
                for f in range(4):
                    one(b, f - f % 2, f % 2)
                    if f < BLK:
                        normalise(last, kind, f)
                with dve.Fori(2, NF // 2 - 1) as j:
                    one(b, 2 * j, 0)
                    one(b, 2 * j, 1)
                one(b, NF - 2, 0, more_up=False)
                one(b, NF - 2, 1, more_row=False, more_up=False)
                if b + 1 < N_BLK:
                    turned_low(N_BLK + b + 1)
            dve.wait_ge(S("row_used"), down_tile(N_BLK, 0))
            add_residual(N_BLK - 1, "y")
            normalise(N_BLK - 1, "y", 0)
            for t in range(1, BLK):
                dve.wait_ge(S("y_summed"), UNITS * (N_BLK - 1) + 2 * t + 2)
                x = res[N_BLK - 1][:, t, :]
                layer_norm_stats(dve, step, x, stats, mean, rstd, tmp, P)
                step(dve.scalar_tensor_tensor(x, x, mean[:, 0:1], rows["ln2_g"][:, :], ALU.subtract, ALU.mult))
                dve.scalar_tensor_tensor(x, x, rstd[:, 0:1], rows["ln2_b"][:, :], ALU.mult, ALU.add)\
                   .then_inc(S("y_last"), 1)

        @block.tensor
        def _(pe):
            def turn(n, units=range(UNITS)):
                b = n % N_BLK
                for u in units:
                    t = u // 2
                    if n >= N_BLK:
                        pe.wait_ge(S("h1_ready"), BLK * b + t + 1)
                    if n > N_BLK and u < 2:
                        pe.wait_ge(S("relu"), NF * b - 1 + u)
                    elif n or u >= 2:
                        pe.wait_ge(S("zT_lo"), UNITS * n + u - 1)
                    for k in range(4):
                        c = P * (4 * (u % 2) + k)
                        src = mix[:, t, c:c + P] if n < N_BLK else res[b][:, t, c:c + P]
                        last = pe.transpose(pU[u % 2][:, P * k:P * (k + 1)], src, ident[:, :])
                    last.then_inc(S("turned"), 1)

            def add_rows(r, slot, lhs, first=False, final=False):
                pe.wait_ge(S("row_lo"), r + 1)
                for t in range(BLK):
                    for half in range(2):
                        out = pY[2 * t + half][:, :]
                        for a, (x, w) in enumerate([(lhs[0], row_hi), (lhs[0], row_lo), (lhs[1], row_hi)]):
                            last = pe.matmul(out, x[:, P * t:P * (t + 1)], w[slot][:, 512 * half:512 * half + 512],
                                             start=first and a == 0, stop=final and a == 2, skip_group_check=True)
                last.then_inc(S("row_used"), 1)

            def up(b, f, slot, first=False):
                pe.wait_ge(S("up_lo"), NF * b + f + 1)
                if not first:
                    pe.wait_ge(S("relu"), NF * b + f - 1)
                n = (N_BLK + b) % 2
                parts = [(up_hi, zT_hi[n]), (up_lo, zT_hi[n]), (up_hi, zT_lo[n])]
                for a, (w, x) in enumerate(parts):
                    for k in range(KD):
                        last = pe.matmul(pU[slot][:, 0:NT], w[slot][:, k, :], x[:, k, :],
                                         start=(a == 0 and k == 0), stop=(a == 2 and k == KD - 1))
                last.then_inc(S("up_done"), 1)

            def down(b, f, half, final=False):
                pe.wait_ge(S("hid_lo"), NF * b + f + half + 1)
                add_rows(down_tile(b, 0) + f + half, half, (hid_hi[half], hid_lo[half]), final=final)

            pe.wait_ge(S("ident_landed"), 16)
            pe.wait_ge(S("mix_landed"), 16)
            turn(0)
            for b in range(N_BLK):
                pe.wait_ge(S("zT_lo"), UNITS * (b + 1))
                if b:
                    pe.wait_ge(S("h1_summed"), UNITS * b)
                for k in range(KD):
                    add_rows(KD * b + k, k % 2, (zT_hi[b % 2][:, k, :], zT_lo[b % 2][:, k, :]), first=k == 0,
                             final=k == KD - 1)
                    if k == KD // 2:
                        if b + 1 < N_BLK:
                            pe.wait_ge(S("mix_landed"), 16 * (b + 2))
                        turn(b + 1)
            pe.wait_ge(S("zero_ready"), 1)
            for b in range(N_BLK):
                pe.wait_ge(S("zT_lo"), UNITS * (N_BLK + b + 1))
                up(b, 0, 0, first=b == 0)
                up(b, 1, 1, first=b == 0)
                pe.wait_ge(S("h1_summed" if b == 0 else "y_summed"), UNITS * (N_BLK if b == 0 else b))
                for u in range(UNITS):
                    pe.matmul(pY[u][:, :], zero[:, 0:P], zero[:, :], start=True, stop=False, skip_group_check=True)
                down(b, 0, 0)
                with pe.Fori(1, NF // 2) as j:
                    up(b, 2 * j, 0)
                    down(b, 2 * j - 2, 1)
                    up(b, 2 * j + 1, 1)
                    down(b, 2 * j, 0)
                if b + 1 < N_BLK:
                    turn(N_BLK + b + 1, range(2))
                down(b, NF - 2, 1, final=True)
                if b + 1 < N_BLK:
                    turn(N_BLK + b + 1, range(2, UNITS))


CHUNK = 64
HALF = -0.5 * DECAY
LEVELS = {META: 3, P: 5}
N_CONST = 5
C_LOWER, C_UPPER, C_UPPER_EQ, C_IDENT, C_TWICE = range(N_CONST)


def heads(ap, width=HD):
    return ap.rearrange("p (h d) -> p h d", d=width)


class Jobs:

    def __init__(self, S, banks, tag):
        self.S, self.banks, self.tag, self.number = S, banks, tag, {}

    def fill(self, pe, name):
        q = len(self.number)
        assert name not in self.number, name
        self.number[name] = q
        if q >= len(self.banks):
            pe.wait_ge(self.S(f"{self.tag}_taken{q % len(self.banks)}"), q // len(self.banks))
        return self.banks[q % len(self.banks)]

    def filled(self, last):
        last.then_inc(self.S(f"{self.tag}_filled"), 1)

    def take(self, eng, name):
        eng.wait_ge(self.S(f"{self.tag}_filled"), self.number[name] + 1)
        return self.banks[self.number[name] % len(self.banks)]

    def taken(self, last, name):
        last.then_inc(self.S(f"{self.tag}_taken{self.number[name] % len(self.banks)}"), 1)
        return self.S(f"{self.tag}_taken{self.number[name] % len(self.banks)}"), self.number[name] // len(self.banks) + 1

    def wait_filled(self, eng, name):
        eng.wait_ge(self.S(f"{self.tag}_filled"), self.number[name] + 1)

    def wait_taken(self, eng, name):
        q = self.number[name]
        eng.wait_ge(self.S(f"{self.tag}_taken{q % len(self.banks)}"), q // len(self.banks) + 1)


ROWS_EARLY = (("k_k", W), ("k_a", W), ("r_k", W), ("gn_g", W), ("gn_b", W), ("kv_norm_g", KV_LORA), ("mla_out_g", W))


def mix_weights(sb):
    M = {
        "const": sb("m_const", [P, N_CONST, P]),
        "cvec": sb("m_cvec", [P, 8]),
        "ind": sb("m_ind", [P, 10]),
        "wdec": sb("m_wdec", [LORA + 1, W]),
        "waaa": sb("m_waaa", [LORA + 1, W]),
        "wgate": sb("m_wgate", [P, W]),
        "w_qb": sb("m_wqb", [P, Q_LORA // P, HEADS * QH]),
        "w_kvb": sb("m_wkvb", [P, 2, HEADS * 2 * HD]),
        "mu": sb("m_mu", [P, C_RWKV]),
    }
    for r, width in ROWS_EARLY:
        M[r] = sb(f"m_{r}", [P, width])
    return M


def mix_weights_late(sb):
    return {"rowpair": sb("m_rowpair", [1, 2, P]), "q_norm_g": sb("m_q_norm_g", [P, Q_LORA])}


def mix_loads(io, M):
    return [
        (M["const"][:, :, :], io["const"].rearrange("m p n -> p m n")),
        (M["cvec"][:, :], io["cvec"]), (M["ind"][:, :], io["ind"]),
        (M["wdec"][0:LORA, :], io["w_decay_up"][0]), (M["wdec"][LORA:LORA + 1, :], io["decay_base"]),
        (M["waaa"][0:LORA, :], io["w_aaa_up"][0]), (M["waaa"][LORA:LORA + 1, :], io["aaa_base"]),
        (M["wgate"][:, :], io["w_gate_up"][0]),
        (M["w_qb"][:, :, :], io["w_qb"][0].rearrange("(k p) n -> p k n", p=P)),
        (M["w_kvb"][:, :, :], io["w_kvb"][0].rearrange("(k p) n -> p k n", p=P)),
        (M["mu"][:, :], bcast(io["mu_shift"][0])),
    ] + [(M[r][:, :], bcast(io[r][0])) for r, _ in ROWS_EARLY]


def schedule(vector=False):
    prepare = [["shift", "norm"], ["turn_latent", "lora"], ["turn_lora", "key_squares"],
               ["key_norm", "lora_up", "decay"], ["keys", "latent_keys"], ["products", "latent_rest"]]
    norm = [[], ["mean"], ["variance"], ["gate_out"], [], ["finish"]]
    count = len(TILES) - 1
    steps = [("shift_diff", 0, None), ("squares", 0, None)] + [(s, 0, None) for piece in prepare for s in piece]
    steps += [("turn_sides", 0, None), ("turn", 0, None)]
    for i in range(count):
        beside = [[(s, i - 1, None) for s in (norm[m] if i > 1 else [])]
                  + [(s, i + 1, None) for s in (prepare[m] if i + 1 < count else [])] for m in range(len(prepare))]
        attend = lambda name, v: [(name, i, v)] if i and v < HEADS else []
        outputs = [[("outer_q", i, None)], [("outer_qv", i, None)], [("outer_p", i, None)], [], []] if i else [[]] * 5
        steps += attend("score", 0) + [("shift_diff", i + 1, None), ("squares", i + 1, None)] * (i + 1 < count) + [("outer_a", i, None)]
        steps += attend("weights", 0) + attend("values", 0) + attend("score", 1) + [("outer_c", i, None)]
        levels = LEVELS[TILES[i][1]]
        for v in range(levels):
            late = [step for step in beside[v] if not vector or step[0] == "latent_keys"]
            steps += [("newton_t", i, v)] + [step for step in beside[v] if step not in late]
            steps += attend("weights", v + 1) + [("newton_x", i, v)] + attend("values", v + 1)
            steps += attend("score", v + 2) + outputs[v] + late
        v = levels + 1
        for c in range(1 if i == 0 else 2):
            steps += [("scan_z", i, c)] + attend("weights", v) + [("scan_sa", i, c)] + attend("values", v)
            steps += attend("score", v + 1) + [("scan_s", i, c)]
            if c == 0:
                steps += [step for piece in beside[levels:] for step in piece]
            v += 1
        if i + 1 < count:
            steps += [("turn_sides", i + 1, None), ("turn", i + 1, None)]
        if i:
            steps.append(("merge", i, None))
    return steps + [(s, count - 1, None) for piece in norm for s in piece]


def phase_mix_prompt(nc, io, M):
    with ExitStack() as ctx:
        def sb(name, shape, dt=F32):
            return ctx.enter_context(nc.sbuf_tensor(name, shape, dt))

        def psum(name, shape):
            return ctx.enter_context(nc.psum_tensor(name, shape, F32))

        S = Semaphores(nc, io["semaphores"], "b_")
        pr = [sb(f"b_pr{i}", [P, C_IN]) for i in range(2)]
        prev = sb("b_prev", [P, 4 * W])
        w_inc, w_inv, w_ex, kk = (prev[:, W * m:W * m + W] for m in range(4))
        table = sb("b_table", [P, 2 * ROPE])
        laT, lgT = sb("b_laT", [LORA + 1, 2, P]), sb("b_lgT", [P, P])
        td, tmp = sb("b_td", [P, W]), sb("b_tmp", [P, W])
        la, lg = tmp[:, 0:LORA], tmp[:, LORA:LORA + P]
        a_, kt_, gate_, bonus_ = ([sb(f"b_{n}{i}", [P, W]) for i in range(2)] for n in ("a", "kt", "gate", "bonus"))
        wl_ = [sb(f"b_wl{i}", [P, PAIRS, 2]) for i in range(2)]
        KT, RT = sb("b_KT", [P, PAIRS, P]), sb("b_RT", [P, PAIRS, P])
        khBT = sb("b_khBT", [P, 2 * W])
        khT, BT = (khBT[:, W * m:W * m + W].rearrange("p (k n) -> p k n", k=PAIRS) for m in range(2))
        q = khBT[:, 0:HEADS * QH].rearrange("p (h d) -> p h d", d=QH)
        qt = khBT[:, HEADS * QH:HEADS * (QH + ROPE)].rearrange("p (h d) -> p h d", d=ROPE)
        BTn = td[:, :].rearrange("p (k n) -> p k n", k=PAIRS)
        IA, X0, XA, F, PT = (sb(f"b_{n}", [P, HEADS, P]) for n in ("IA", "X0", "XA", "F", "PT"))
        zr, SA = sb("b_zr", [P, W]), sb("b_SA", [P, W])
        state = sb("b_state", [P, PAIRS, HD])
        mixed = sb("b_mixed", [P, D])
        ssq = sb("b_ssq", [P, 4])
        qn, c, kr, krt = sb("b_qn", [P, Q_LORA]), sb("b_c", [P, KV_LORA]), sb("b_kr", [P, ROPE]), sb("b_krt", [P, ROPE])
        cT = sb("b_cT", [P, 2, P])
        qT = sb("b_qT", [QH, HEADS, P])
        kTall = sb("b_kT", [QH, HEADS, PROMPT])
        vall, vmeta, vbd = sb("b_v", [P, SEQ // P, W]), mixed[0:META, 0:W], sb("b_vbd", [P, W])
        Pb = [sb(f"b_P{i}", [P, SEQ]) for i in range(2)]
        PTb = [sb(f"b_PT{i}", [P, 4, P]) for i in range(2)]
        qnT = sb("b_qnT", [P, 3, P])
        sm, pm = sb("b_sm", [P, HEADS, META]), sb("b_pm", [P, HEADS, META])
        pmT = sm[:, :, :].rearrange("p h m -> p (h m)")
        SC = psum("b_SC", [P, SEQ])
        O, Y, Z = psum("b_O", [P, 512]), psum("b_Y", [P, 512]), psum("b_Z", [P, 512])
        J = Jobs(S, [psum(f"b_R{i}", [P, 512]) for i in range(3)], "b")
        ident = M["const"][:, C_IDENT, :]
        lower, upper, upper_eq, twice = (M["const"][:, m, :] for m in (C_LOWER, C_UPPER, C_UPPER_EQ, C_TWICE))
        NP = len(TILES) - 1
        stat = sb("b_stat", [P, 80])
        n2, rk, t8, bs, mu8, v8, rs8, mm, rs, rsm = (stat[:, 8 * m:8 * m + 8] for m in range(10))
        mxc, nb = sb("b_mx", [P, 8]), sb("b_nb", [P, 8])
        ms, rs2, t2 = sb("b_ms", [P, 4]), sb("b_rs2", [P, 4]), sb("b_t2", [P, 4])
        den = sb("b_den", [P, 8])
        block = ctx.enter_context(nc.Block())

        def bc(ap8, n):
            return ap8[0:n, :].unsqueeze(2).to_broadcast([n, HEADS, HD])

        def bc4(m, n):
            return m[0:n, 0:n].unsqueeze(1).to_broadcast([n, 4, n])

        def four(bank, n, rows=None):
            return bank[0:(n if rows is None else rows), 0:4 * n].rearrange("p (k n) -> p k n", k=4)

        def chunk_no(i, c_):
            return 0 if i == 0 else 2 * i - 1 + c_

        def key_jobs(i):
            return [list(range(j, min(j + 4, i + 1))) for j in range(1, i + 1, 4)]

        def pv_before(i, h):
            return sum(HEADS * len(key_jobs(m)) for m in range(1, i)) + h * len(key_jobs(i))

        @block.tensor
        def _(pe):
            def times_state(i, out, lhs, R, odd, name, m):
                r = slice(HD * odd, HD * odd + HD)
                for k in range(PAIRS):
                    last = pe.matmul(out[R, P * k + HD * odd:P * k + HD * odd + HD], lhs[r, k, R], state[r, k, :],
                                     start=False, stop=True, skip_group_check=True)
                last.then_inc(S(name), 1)
                pe.wait_ge(S(name), m + 1)

            for step, i, v in schedule():
                t0, n = TILES[i]
                p_, V = pr[i % 2], pr[i % 2][0:n, 2 * W:3 * W]
                a, kt = a_[i % 2], kt_[i % 2]

                def turns(name, pieces):
                    bank = J.fill(pe, (i, name))
                    for out, src in pieces(bank):
                        last = pe.transpose(out, src, ident[0:n, 0:n])
                    J.filled(last)

                if step == "turn_latent":
                    pe.wait_ge(S("c_ready"), i + 1)
                    pe.wait_ge(S("kr_ready"), i + 1)
                    bank = J.fill(pe, (i, "cT"))
                    for k in range(2):
                        pe.transpose(bank[:, k * n:k * n + n], c[0:n, P * k:P * k + P], ident[0:n, 0:n])
                    J.filled(pe.matmul(bank[NOPE:QH, 2 * n:3 * n], kr[0:n, :], ident[0:n, 0:n],
                                       start=True, stop=True))
                    if i:
                        pe.wait_ge(S("qn_ready"), i + 1)
                        turns("qnT", lambda b: [(b[:, k * n:k * n + n], qn[0:n, P * k:P * k + P]) for k in range(3)])
                if step == "turn_lora":
                    pe.wait_ge(S("la_ready"), 2 * i + 2)
                    pe.wait_ge(S("shifted"), i + 1)
                    turns("loraT", lambda b: [(b[0:LORA, 0:n], la[0:n, :]),
                                              (b[0:LORA, n:2 * n], p_[0:n, 3 * W + LORA:3 * W + 2 * LORA]),
                                              (b[:, 2 * n:3 * n], lg[0:n, :])])
                if step == "lora_up":
                    pe.wait_ge(S("laT_out"), i + 1)
                    J.wait_taken(pe, (i, "loraT"))
                    if i == 0:
                        pe.wait_ge(S("ones_set"), 1)
                    for name, lhs, rhs in (("dec", laT[:, 0, 0:n], M["wdec"]), ("aaa", laT[:, 1, 0:n], M["waaa"]),
                                           ("gate", lgT[:, 0:n], M["wgate"])):
                        bank = J.fill(pe, (i, name))
                        J.filled(pe.matmul(bank[0:n, :], lhs, rhs[:, :], start=True, stop=True))
                if step == "decay":
                    J.wait_taken(pe, (i, "dec"))
                    for name, tri in (("inc", upper_eq), ("ex", upper)):
                        bank = J.fill(pe, (i, name))
                        J.filled(pe.matmul(bank[0:n, :], tri[0:n, 0:n], td[0:n, :], start=True, stop=True))
                    bank = J.fill(pe, (i, "total"))
                    for g in range(PAIRS):
                        last = pe.matmul(bank[:, 2 * g:2 * g + 2], td[0:n, P * g:P * g + P], M["ind"][0:n, 0:2],
                                         start=True, stop=True)
                    J.filled(last)
                if step == "latent_keys":
                    pe.wait_ge(S("cT_out"), i + 1)
                    for g in range(2):
                        bank = J.fill(pe, (i, "kn", g))
                        for hh in range(4):
                            col = (4 * g + hh) * 2 * HD
                            for k in range(2):
                                last = pe.matmul(bank[0:NOPE, hh * n:hh * n + n], M["w_kvb"][:, k, col:col + NOPE],
                                                 cT[:, k, 0:n], start=k == 0, stop=k == 1)
                        J.filled(last)
                if step == "latent_rest":
                    bank = J.fill(pe, (i, "v"))
                    wv = M["w_kvb"][:, :, :].rearrange("p k (h d) -> p k h d", d=2 * HD)[:, :, :, HD:2 * HD]
                    for k in range(2):
                        last = pe.matmul(heads(bank[0:n, :]), cT[:, k, 0:n], wv[:, k], start=k == 0, stop=k == 1)
                    J.filled(last)
                    if i:
                        J.wait_taken(pe, (i, "qnT"))
                        for g in range(2):
                            bank = J.fill(pe, (i, "q", g))
                            for k in range(3):
                                last = pe.matmul(bank[0:n, 0:4 * QH], qnT[:, k, 0:n],
                                                 M["w_qb"][:, k, 4 * QH * g:4 * QH * (g + 1)],
                                                 start=k == 0, stop=k == 2)
                            J.filled(last)
                if step in ("turn_sides", "turn"):
                    if step == "turn" and i:
                        pe.wait_ge(S("q_ready"), i)
                        for g in range(2):
                            turns(("qT", g), lambda b: [(b[0:QH, k * n:k * n + n], q[0:n, 4 * g + k, :])
                                                        for k in range(4)])
                    for name, src in ((("KT", w_ex), ("RT", w_inc)) if step == "turn_sides" else (("khT", kt), ("BT", a))):
                        if name == "RT" and not i:
                            continue
                        pe.wait_ge(S(f"{name}_src"), i if name == "RT" else i + 1)
                        turns(name, lambda b: [(b[:, k * n:k * n + n], src[0:n, P * k:P * k + P]) for k in range(4)])
                outer = {"outer_a": [("A", KT, BT), ("AT", BTn, KT)], "outer_c": [("C", khT, KT)],
                         "outer_q": [("Q", khT, RT)], "outer_p": [("P", BT, RT)]}
                if step == "outer_a":
                    pe.wait_ge(S("BTp_out"), i + 1)
                    for name in ("KT", "khT", "BT") + (("RT",) if i else ()):
                        J.wait_taken(pe, (i, name))
                if step in outer:
                    for name, lhs, rhs in outer[step]:
                        for g in range(2):
                            bank = J.fill(pe, (i, name, g))
                            r = slice(HD * g, HD * g + HD)
                            for k in range(PAIRS):
                                last = pe.matmul(bank[0:n, k * n:k * n + n], lhs[r, k, 0:n], rhs[r, k, 0:n],
                                                 start=True, stop=True)
                            J.filled(last)
                if step == "outer_c":
                    for g in range(2):
                        J.wait_taken(pe, (i, "C", g))
                    if i:
                        pe.wait_ge(S("zr_ready"), chunk_no(i, 0))
                    for h in range(HEADS):
                        pe.matmul(Z[0:n, HD * h:HD * h + HD], F[0:n, h, 0:n], V[:, HD * h:HD * h + HD],
                                  start=h == 0, stop=False, skip_group_check=True)
                if step == "outer_qv":
                    for g in range(2):
                        J.wait_taken(pe, (i, "Q", g))
                    if i >= 2:
                        pe.wait_ge(S("y_out"), i - 1)
                    for h in range(HEADS):
                        last = pe.matmul(Y[0:n, HD * h:HD * h + HD], PT[0:n, h, 0:n], V[:, HD * h:HD * h + HD],
                                         start=h == 0, stop=False, skip_group_check=True)
                if step == "newton_t" and v == 0:
                    for g in range(2):
                        J.wait_taken(pe, (i, "A", g))
                        J.wait_taken(pe, (i, "AT", g))
                if step == "newton_t":
                    x = XA if v else X0
                    for g in range(2):
                        if v:
                            J.wait_taken(pe, (i, "X", v - 1, g))
                        bank = J.fill(pe, (i, "T", v, g))
                        for hh in range(4):
                            h = 4 * g + hh
                            last = pe.matmul(bank[0:n, hh * n:hh * n + n], x[0:n, h, 0:n], IA[0:n, h, 0:n],
                                             start=True, stop=True)
                        J.filled(last)
                if step == "newton_x":
                    x = XA if v else X0
                    for g in range(2):
                        J.wait_taken(pe, (i, "T", v, g))
                        bank = J.fill(pe, (i, "X", v, g))
                        for hh in range(4):
                            h = 4 * g + hh
                            last = pe.matmul(bank[0:n, hh * n:hh * n + n], F[0:n, h, 0:n], x[0:n, h, 0:n],
                                             start=True, stop=True)
                        J.filled(last)
                if step in ("scan_z", "scan_sa", "scan_s"):
                    m = chunk_no(i, v)
                    R = slice(CHUNK * v, CHUNK * v + min(n, CHUNK))
                if step == "scan_z":
                    if v == 0:
                        for g in range(2):
                            J.wait_taken(pe, (i, "X", LEVELS[n] - 1, g))
                        if i:
                            for g in range(2):
                                J.wait_taken(pe, (i, "P", g))
                    pe.wait_ge(S("state_ready"), m + 1)
                    times_state(i, Z, KT, R, 0, "z_even", m)
                    times_state(i, Z, KT, R, 1, "z_ready", m)
                    if i:
                        times_state(i, Y, RT, R, 1, "y_odd", m - 1)
                        times_state(i, Y, RT, R, 0, "y_even", m - 1)
                if step == "scan_sa":
                    pe.wait_ge(S("zr_ready"), m + 1)
                    bank = J.fill(pe, (i, "SA", v))
                    for h in range(HEADS):
                        last = pe.matmul(bank[R, HD * h:HD * h + HD], XA[R, h, R], zr[R, HD * h:HD * h + HD],
                                         start=True, stop=True)
                    J.filled(last)
                if step == "scan_s":
                    J.wait_taken(pe, (i, "SA", v))
                    bank = J.fill(pe, (i, "S", v))
                    for h in range(HEADS):
                        cols = slice(HD * h, HD * h + HD)
                        out = bank[HD * (h % 2):HD * (h % 2) + HD, HD * (h // 2):HD * (h // 2) + HD]
                        pe.matmul(out, a[R, cols], SA[R, cols], start=True, stop=False)
                        last = pe.matmul(out, kt[R, cols], p_[R, 2 * W + HD * h:2 * W + HD * h + HD],
                                         start=False, stop=True)
                    J.filled(last)
                    if v == 1:
                        for h in range(HEADS):
                            cols = slice(HD * h, HD * h + HD)
                            last = pe.matmul(Y[:, cols], PT[:, h, :], SA[:, cols], start=False, stop=True,
                                             skip_group_check=True)
                        last.then_inc(S("y_ready"), 1)
                if step == "score":
                    if v == 0:
                        for g in range(2):
                            J.wait_taken(pe, (i, ("qT", g)))
                            J.wait_taken(pe, (i, "kn", g))
                        J.wait_taken(pe, (i, "cT"))
                        bank = J.fill(pe, (i, "sm"))
                        for h in range(HEADS):
                            last = pe.matmul(bank[0:n, META * h:META * h + META], qT[:, h, 0:n], kTall[:, h, 0:META],
                                             start=True, stop=True)
                        J.filled(last)
                    m = HEADS * (i - 1) + v
                    if m:
                        pe.wait_ge(S("exp_done"), m)
                    for k0 in range(0, P * i, 512):
                        k1 = min(k0 + 512, P * i)
                        last = pe.matmul(SC[:, k0:k1], qT[:, v, :], kTall[:, v, META + k0:META + k1],
                                         start=True, stop=k1 < P * i, skip_group_check=True)
                    if i == 1 and v == 0:
                        pe.wait_ge(S("rowpair_landed"), 16)
                    last = pe.matmul(SC[:, P * (i - 1):P * i], M["rowpair"][:, 0, :], M["rowpair"][:, 1, :],
                                     start=False, stop=True, skip_group_check=True)
                    last.then_inc(S("scored"), 1)
                if step == "weights":
                    pe.wait_ge(S("exp_done"), HEADS * (i - 1) + v + 1)
                    for j, group in enumerate(key_jobs(i)):
                        turns(("PT", v, j), lambda b: [(b[:, P * x:P * x + P], Pb[v % 2][:, P * (t - 1):P * t])
                                                       for x, t in enumerate(group)])
                if step == "values":
                    for j, group in enumerate(key_jobs(i)):
                        J.wait_taken(pe, (i, ("PT", v, j)))
                        if v == 0 and j == 0:
                            J.wait_taken(pe, (i, "v"))
                            if i >= 2:
                                pe.wait_ge(S("o_out"), i - 1)
                        slot = (pv_before(i, v) + j) % 2
                        for x, t in enumerate(group):
                            last = pe.matmul(O[:, HD * v:HD * v + HD], PTb[slot][:, x, :],
                                             vall[:, t - 1, HD * v:HD * v + HD],
                                             start=v == 0 and t == 1, stop=False, skip_group_check=True)
                        last.then_inc(S("pv_done"), 1)
                if step == "merge":
                    pe.wait_ge(S("expm_done"), HEADS * i)
                    turns("pmT", lambda b: [(b[:, 0:n], pm[:, :, :].rearrange("p h m -> p (h m)"))])
                    J.wait_taken(pe, (i, "pmT"))
                    if i == 1:
                        pe.wait_ge(S("vbd_ready"), 16 * HEADS)
                    pe.matmul(O[:, :], pmT[:, :], vbd[:, :], start=False, stop=True, skip_group_check=True)\
                      .then_inc(S("o_ready"), 1)

        @block.sync
        def _(sp):
            def load(i):
                t0, n = TILES[i]
                if i >= 2:
                    sp.wait_ge(S("state_ready"), chunk_no(i - 1, 0) + 1)
                    sp.wait_ge(S("bonus_ready"), i - 1)
                sp.dma_start(pr[i % 2][0:n, :], io["p"][1 + t0:1 + t0 + n, :]).then_inc(S(f"pr_landed{i % 2}"), 16)
                if i:
                    for name in ("KT", "RT", "khT", "BT"):
                        if (i - 1, name) in J.number:
                            J.wait_filled(sp, (i - 1, name))
                    sp.wait_ge(S("kr_ready"), i)
                    if i >= 2:
                        sp.wait_ge(S("q_ready"), i - 1)
                sp.dma_start(prev[0:n, 0:C_RWKV], io["p"][t0:t0 + n, 0:C_RWKV]).then_inc(S("prev_landed"), 16)
                sp.dma_start(table[0:n, :], io["table"][t0:t0 + n, :]).then_inc(S("table_landed"), 16)

            def store_mix(i):
                t0, n = TILES[i]
                sp.wait_ge(S("rw_out"), i)
                sp.wait_ge(S("at_out"), i)
                sp.dma_start(io["mix"][t0 - META:t0 - META + n, :], mixed[:, :]).then_inc(S("mix_stored"), 16)

            load(0)
            sp.dma_start(M["q_norm_g"][:, :], bcast(io["q_norm_g"][0])).then_inc(S("q_norm_landed"), 16)
            sp.dma_start(M["rowpair"][:, :, :], io["rowpair"].rearrange("(a m) n -> a m n", a=1))\
              .then_inc(S("rowpair_landed"), 16)
            for i in range(NP):
                t0, n = TILES[i]
                sp.wait_ge(S("c_ready"), i + 1)
                sp.dma_start(io["o_lat_p"][0, 0, t0:t0 + n, :], c[0:n, :]).then_inc(S("c_stored"), 16)
                sp.wait_ge(S("kr_ready"), i + 1)
                sp.dma_start(io["o_rope_p"][0, 0, t0:t0 + n, :], kr[0:n, :]).then_inc(S("kr_stored"), 16)
                if i + 1 < NP:
                    load(i + 1)
                if i == 0:
                    sp.wait_ge(S("vbd_zero"), 1)
                    J.wait_taken(sp, (0, "v"))
                    for h in range(HEADS):
                        sp.dma_start(vbd[META * h:META * h + META, HD * h:HD * h + HD], vmeta[:, HD * h:HD * h + HD])\
                          .then_inc(S("vbd_ready"), 16)
                if i >= 2:
                    store_mix(i - 1)
            store_mix(NP - 1)
            sp.wait_ge(S("state_ready"), chunk_no(NP - 1, 1) + 2)
            sp.dma_start(io["o_state_p"].rearrange("(g p) v -> p g v", p=P), state[:, :, :]).then_inc(S("state_stored"), 16)
            sp.wait_ge(S("state_stored"), 16)
            sp.wait_ge(S("c_stored"), 16 * NP)
            sp.wait_ge(S("kr_stored"), 16 * NP)
            sp.wait_ge(S("mix_stored"), 16 * (NP - 1))

        @block.gpsimd
        def _(pool):
            step = Steps(pool, S("pool_step"))
            pool.memset(vbd[:, :], 0.0).then_inc(S("vbd_zero"), 1)
            for s, i, v in schedule():
                t0, n = TILES[i]
                p_ = pr[i % 2]
                r_, k_, v_ = (p_[0:n, W * m:W * m + W] for m in range(3))
                a, kt, gate, bonus, wl = a_[i % 2], kt_[i % 2], gate_[i % 2], bonus_[i % 2], wl_[i % 2]
                if s == "shift_diff":
                    pool.wait_ge(S("sh_diff"), i + 1)
                    pool.tensor_tensor(prev[0:n, 0:C_RWKV], prev[0:n, 0:C_RWKV], M["mu"][0:n, :], ALU.mult).then_inc(S("sh_mu"), 1)
                if s == "norm":
                    pool.wait_ge(S("table_landed"), 16 * (i + 1))
                    pool.wait_ge(S(f"pr_landed{i % 2}"), 16 * (i // 2 + 1))
                    if i:
                        pool.wait_ge(S("kr_stored"), 16 * i)
                        J.wait_taken(pool, (i - 1, "cT"))
                    x = p_[0:n, C_IN - ROPE:C_IN]
                    cos, sin = table[0:n, 0:ROPE], table[0:n, ROPE:2 * ROPE]
                    step(pool.tensor_tensor(krt[0:n, 0:16], x[:, 16:32], sin[:, 0:16], ALU.mult))
                    step(pool.tensor_tensor(krt[0:n, 16:32], x[:, 0:16], sin[:, 16:32], ALU.mult))
                    step(pool.tensor_tensor(kr[0:n, :], x, cos, ALU.mult))
                    pool.tensor_tensor(kr[0:n, :], kr[0:n, :], krt[0:n, :], ALU.add).then_inc(S("kr_ready"), 1)
                if s == "lora_up":
                    J.wait_taken(pool, (i, "aaa"))
                    pool.tensor_scalar(a[0:n, :], a[0:n, :], 0.5, 0.5, ALU.mult, ALU.add).then_inc(S("a_ready"), 1)
                if s == "key_squares":
                    pool.wait_ge(S("shifted"), i + 1)
                    pool.tensor_tensor(kk[0:n, :], k_, M["k_k"][0:n, :], ALU.mult).then_inc(S("kk0_ready"), 1)
                if s == "keys":
                    pool.wait_ge(S("kt_ready"), i + 1)
                    if i >= 3:
                        pool.wait_ge(S("rw_out"), i - 2)
                    step(pool.tensor_tensor(bonus[0:n, :], r_, kt[0:n, :], ALU.mult))
                    pool.tensor_tensor(bonus[0:n, :], bonus[0:n, :], M["r_k"][0:n, :], ALU.mult).then_inc(S("rb_ready"), 1)
                if s == "products":
                    pool.wait_ge(S("kk_ready"), i + 1)
                    pool.tensor_tensor(a[0:n, :], kk[0:n, :], a[0:n, :], ALU.mult).then_inc(S("b_ready"), 1)
                    pool.wait_ge(S("bs_ready"), i + 1)
                    step(pool.tensor_tensor(heads(bonus[0:n, :]), heads(v_), bc(bs, n), ALU.mult))
                    pool.tensor_tensor(bonus[0:n, :], bonus[0:n, :], M["gn_b"][0:n, :], ALU.add).then_inc(S("bonus_ready"), 1)
                if s == "latent_rest" and i:
                    J.wait_taken(pool, (i, "q", 0))
                    J.wait_taken(pool, (i, "q", 1))
                    cos = table[:, 0:ROPE].unsqueeze(1).to_broadcast([P, HEADS, ROPE])
                    sa = table[:, ROPE:ROPE + 16].unsqueeze(1).to_broadcast([P, HEADS, 16])
                    sb_ = table[:, ROPE + 16:2 * ROPE].unsqueeze(1).to_broadcast([P, HEADS, 16])
                    step(pool.tensor_tensor(qt[:, :, 0:16], q[:, :, NOPE + 16:QH], sa, ALU.mult))
                    step(pool.tensor_tensor(qt[:, :, 16:32], q[:, :, NOPE:NOPE + 16], sb_, ALU.mult))
                    step(pool.tensor_tensor(q[:, :, NOPE:QH], q[:, :, NOPE:QH], cos, ALU.mult))
                    pool.tensor_tensor(q[:, :, NOPE:QH], q[:, :, NOPE:QH], qt, ALU.add).then_inc(S("q_ready"), 1)
                if s == "variance":
                    pool.wait_ge(S("yn_ready"), i)
                    pool.tensor_tensor(zr[:, :], zr[:, :], M["gn_g"][:, :], ALU.mult).then_inc(S("yg_ready"), 1)

        @block.scalar
        def _(act):
            for s, i, v in schedule():
                t0, n = TILES[i]
                p_ = pr[i % 2]
                a, kt, gate, bonus, wl = a_[i % 2], kt_[i % 2], gate_[i % 2], bonus_[i % 2], wl_[i % 2]
                if s == "squares":
                    act.wait_ge(S(f"pr_landed{i % 2}"), 16 * (i // 2 + 1))
                    if i:
                        act.wait_ge(S("sq_read"), i)
                        act.wait_ge(S("kk_ready"), i)
                    for m, (c0, width) in enumerate(((C_RWKV, Q_LORA), (C_RWKV + Q_LORA, KV_LORA))):
                        act.activation(tmp[0:n, 0:width], p_[0:n, c0:c0 + width], ACT.Square,
                                       accum_out=ssq[0:n, m:m + 1]).then_inc(S("ssq_ready"), 1)
                        act.wait_ge(S("ssq_ready"), 2 * i + m + 1)
                if s == "turn_latent":
                    bank = J.take(act, (i, "cT"))
                    act.activation(cT[:, :, 0:n], bank[:, 0:2 * n].rearrange("p (k n) -> p k n", k=2), ACT.Copy)\
                       .then_inc(S("cT_out"), 1)
                    src = bank[NOPE:QH, 2 * n:3 * n].unsqueeze(1).to_broadcast([ROPE, HEADS, n])
                    J.taken(act.activation(kTall[NOPE:QH, :, t0:t0 + n], src, ACT.Copy), (i, "cT"))
                    if i:
                        bank = J.take(act, (i, "qnT"))
                        J.taken(act.activation(qnT[:, :, :], bank[:, 0:3 * n].rearrange("p (k n) -> p k n", k=3),
                                               ACT.Copy), (i, "qnT"))
                        J.wait_taken(act, (i, "cT"))
                if s == "lora":
                    act.wait_ge(S("shifted"), i + 1)
                    act.activation(la[0:n, :], p_[0:n, 3 * W:3 * W + LORA], ACT.Tanh).then_inc(S("la_ready"), 1)
                    act.activation(lg[0:n, :], p_[0:n, 3 * W + 2 * LORA:C_RWKV], ACT.Tanh, scale=0.5)\
                       .then_inc(S("lg_tanh"), 1)
                    act.wait_ge(S("lg_tanh"), i + 1)
                    act.activation(lg[0:n, :], lg[0:n, :], ACT.Copy, scale=0.5, bias=0.5).then_inc(S("la_ready"), 1)
                if s == "turn_lora":
                    bank = J.take(act, (i, "loraT"))
                    act.activation(laT[0:LORA, :, 0:n], bank[0:LORA, 0:2 * n].rearrange("p (k n) -> p k n", k=2),
                                   ACT.Copy).then_inc(S("laT_out"), 1)
                    J.taken(act.activation(lgT[:, 0:n], bank[:, 2 * n:3 * n], ACT.Copy), (i, "loraT"))
                if s == "lora_up":
                    if i:
                        J.wait_filled(act, (i - 1, "AT", 1))
                    if i >= 2:
                        act.wait_ge(S("state_ready"), chunk_no(i - 1, 0) + 1)
                    if i >= 3:
                        act.wait_ge(S("rw_out"), i - 2)
                    for name, dst in (("dec", td), ("aaa", a)):
                        bank = J.take(act, (i, name))
                        J.taken(act.activation(dst[0:n, :], bank[0:n, :], ACT.Tanh, scale=0.5), (i, name))
                    bank = J.take(act, (i, "gate"))
                    J.taken(act.activation(gate[0:n, :], bank[0:n, :], ACT.Copy), (i, "gate"))
                if s == "decay":
                    bank = J.take(act, (i, "inc"))
                    act.activation(w_inc[0:n, :], bank[0:n, :], ACT.Exp, scale=HALF, bias=M["cvec"][0:n, 0:1])\
                       .then_inc(S("winc_ready"), 1)
                    J.taken(act.activation(w_inv[0:n, :], bank[0:n, :], ACT.Exp, scale=-HALF,
                                           bias=M["cvec"][0:n, 1:2]), (i, "inc"))
                    bank = J.take(act, (i, "ex"))
                    J.taken(act.activation(w_ex[0:n, :], bank[0:n, :], ACT.Exp, scale=HALF,
                                           bias=M["cvec"][0:n, 2:3]), (i, "ex"))
                    bank = J.take(act, (i, "total"))
                    col = 4 if i == 0 else 3
                    J.taken(act.activation(wl[:, :, :], bank[:, 0:8].rearrange("p (g c) -> p g c", g=PAIRS), ACT.Exp,
                                           scale=HALF, bias=M["cvec"][:, col:col + 1]), (i, "total"))
                if s == "key_squares":
                    act.wait_ge(S("kk0_ready"), i + 1)
                    act.activation(tmp[0:n, :], kk[0:n, :], ACT.Square).then_inc(S("kksq_ready"), 1)
                if s == "latent_rest":
                    bank = J.take(act, (i, "v"))
                    dst = vall[:, i - 1, :] if i else vmeta
                    J.taken(act.activation(dst, bank[0:n, :], ACT.Copy), (i, "v"))
                    if i:
                        for g in range(2):
                            bank = J.take(act, (i, "q", g))
                            J.taken(act.activation(q[:, 4 * g:4 * g + 4, :],
                                                   bank[:, 0:4 * QH].rearrange("p (h d) -> p h d", d=QH), ACT.Copy),
                                    (i, "q", g))
                if s == "turn_sides":
                    bank = J.take(act, (i, "KT"))
                    J.taken(act.activation(KT[:, :, 0:n], four(bank, n, P), ACT.Copy), (i, "KT"))
                if s == "turn":
                    bank = J.take(act, (i, "BT"))
                    act.activation(BT[:, :, 0:n], four(bank, n, P), ACT.Copy).then_inc(S("BTp_out"), 1)
                    J.taken(act.activation(BTn[:, :, 0:n], four(bank, n, P), ACT.Copy, scale=-1.0), (i, "BT"))
                    act.wait_ge(S("BTp_out"), i + 1)
                if s == "newton_x":
                    for g in range(2):
                        bank = J.take(act, (i, "X", v, g))
                        J.taken(act.activation(XA[0:n, 4 * g:4 * g + 4, 0:n], four(bank, n), ACT.Copy), (i, "X", v, g))
                if s == "scan_z":
                    m = chunk_no(i, v)
                    R = slice(CHUNK * v, CHUNK * v + min(n, CHUNK))
                    act.wait_ge(S("z_ready"), m + 1)
                    if v == 0 and i >= 2:
                        act.wait_ge(S("rw_out"), i - 1)
                    act.activation(zr[R, :], Z[R, :], ACT.Copy, scale=-1.0).then_inc(S("zr_ready"), 1)
                if s == "scan_s" and v == 1:
                    act.wait_ge(S("y_ready"), i)
                    act.activation(SA[:, :], Y[:, :], ACT.Copy).then_inc(S("y_out"), 1)
                if s == "mean":
                    act.wait_ge(S("yc_ready"), i)
                    act.activation(SA[:, :], zr[:, :], ACT.Square).then_inc(S("ysq_ready"), 1)
                if s == "score" and v == 0:
                    bank = J.take(act, (i, "sm"))
                    J.taken(act.activation(sm[:, :, :], bank[:, 0:P].rearrange("p (h m) -> p h m", h=HEADS), ACT.Copy),
                            (i, "sm"))
                if s == "score":
                    m = HEADS * (i - 1) + v
                    act.wait_ge(S("nb_ready"), m + 1)
                    if v >= 2:
                        act.wait_ge(S("pv_done"), pv_before(i, v - 1))
                    if v == 0 and i >= 2:
                        act.wait_ge(S("den_ready"), i - 1)
                    act.activation(Pb[v % 2][:, 0:P * i], SC[:, 0:P * i], ACT.Exp, scale=SCALE, bias=nb[:, v:v + 1],
                                   accum_out=rs[:, v:v + 1]).then_inc(S("exp_done"), 1)
                    act.activation(pm[:, v, :], sm[:, v, :], ACT.Exp, scale=SCALE, bias=nb[:, v:v + 1],
                                   accum_out=rsm[:, v:v + 1]).then_inc(S("expm_done"), 1)
                if s == "weights":
                    for j, group in enumerate(key_jobs(i)):
                        m = pv_before(i, v) + j
                        if m >= 2:
                            act.wait_ge(S("pv_done"), m - 1)
                        bank = J.take(act, (i, ("PT", v, j)))
                        w = P * len(group)
                        J.taken(act.activation(PTb[m % 2][:, 0:len(group), :],
                                               bank[:, 0:w].rearrange("p (k n) -> p k n", n=P), ACT.Copy), (i, ("PT", v, j)))
                if s == "merge":
                    bank = J.take(act, (i, "pmT"))
                    J.taken(act.activation(pmT[:, :], bank[:, 0:P], ACT.Copy), (i, "pmT"))
                if s == "finish":
                    act.wait_ge(S("o_out"), i)
                    act.wait_ge(S("kk_ready"), min(i + 3, NP))
                    act.activation(tmp[0:n, :], mixed[:, W:2 * W], ACT.Square, accum_out=ssq[:, 2:3])\
                       .then_inc(S("osq_ready"), 1)
                    act.wait_ge(S("osq_ready"), i)

        @block.vector
        def _(dve):
            step = Steps(dve, S("dve_step"))
            dve.memset(laT[LORA:LORA + 1, :, :], 1.0).then_inc(S("ones_set"), 1)
            for m in (IA, X0):
                step(dve.tensor_copy(m[:, :, :], ident[:, :].unsqueeze(1).to_broadcast([P, HEADS, P])))
            dve.memset(state[:, :, :], 0.0).then_inc(S("state_ready"), 1)
            for s, i, v in schedule(vector=True):
                t0, n = TILES[i]
                p_ = pr[i % 2]
                r_, k_, v_ = (p_[0:n, W * m:W * m + W] for m in range(3))
                a, kt, gate, bonus, wl = a_[i % 2], kt_[i % 2], gate_[i % 2], bonus_[i % 2], wl_[i % 2]
                if s == "shift_diff":
                    dve.wait_ge(S(f"pr_landed{i % 2}"), 16 * (i // 2 + 1))
                    dve.wait_ge(S("prev_landed"), 16 * (i + 1))
                    dve.tensor_tensor(prev[0:n, 0:C_RWKV], prev[0:n, 0:C_RWKV], p_[0:n, 0:C_RWKV], ALU.subtract)\
                       .then_inc(S("sh_diff"), 1)
                if s == "shift":
                    dve.wait_ge(S("sh_mu"), i + 1)
                    dve.tensor_tensor(p_[0:n, 0:C_RWKV], p_[0:n, 0:C_RWKV], prev[0:n, 0:C_RWKV], ALU.add)\
                       .then_inc(S("shifted"), 1)
                    dve.wait_ge(S("shifted"), i + 1)
                if s == "norm":
                    dve.wait_ge(S("ssq_ready"), 2 * i + 2)
                    step(dve.tensor_scalar(ms[0:n, 0:1], ssq[0:n, 0:1], 1.0 / Q_LORA, RMS_EPS, ALU.mult, ALU.add))
                    dve.tensor_scalar(ms[0:n, 1:2], ssq[0:n, 1:2], 1.0 / KV_LORA, RMS_EPS, ALU.mult, ALU.add)\
                       .then_inc(S("sq_read"), 1)
                    dve.wait_ge(S("sq_read"), i + 1)
                    rsqrt(dve, step, rs2[0:n, 0:2], ms[0:n, 0:2], t2[0:n, 0:2])
                    if i:
                        dve.wait_ge(S("c_stored"), 16 * i)
                        J.wait_taken(dve, (i - 1, "cT"))
                    dve.scalar_tensor_tensor(c[0:n, :], p_[0:n, C_RWKV + Q_LORA:C_RWKV + Q_LORA + KV_LORA], rs2[0:n, 1:2],
                                             M["kv_norm_g"][0:n, :], ALU.mult, ALU.mult).then_inc(S("c_ready"), 1)
                    if i >= 2:
                        J.wait_taken(dve, (i - 1, "qnT"))
                    if i == 0:
                        dve.wait_ge(S("q_norm_landed"), 16)
                    dve.scalar_tensor_tensor(qn[0:n, :], p_[0:n, C_RWKV:C_RWKV + Q_LORA], rs2[0:n, 0:1],
                                             M["q_norm_g"][0:n, :], ALU.mult, ALU.mult).then_inc(S("qn_ready"), 1)
                if s == "keys":
                    dve.wait_ge(S("a_ready"), i + 1)
                    step(dve.scalar_tensor_tensor(kt[0:n, :], a[0:n, :], -1.0, M["k_a"][0:n, :], ALU.add, ALU.mult))
                    dve.scalar_tensor_tensor(kt[0:n, :], kt[0:n, :], 1.0, k_, ALU.add, ALU.mult)\
                       .then_inc(S("kt_ready"), 1)
                if s == "key_norm":
                    dve.wait_ge(S("kksq_ready"), i + 1)
                    step(dve.tensor_reduce(n2[0:n, :], heads(tmp[0:n, :]), X, ALU.add))
                    step(dve.tensor_scalar(n2[0:n, :], n2[0:n, :], 1e-24, None, ALU.max))
                    rsqrt(dve, step, rk[0:n, :], n2[0:n, :], t8[0:n, :])
                    dve.tensor_tensor(heads(kk[0:n, :]), heads(kk[0:n, :]), bc(rk, n), ALU.mult).then_inc(S("kk_ready"), 1)
                if s == "products":
                    dve.wait_ge(S("kt_ready"), i + 1)
                    dve.wait_ge(S("winc_ready"), i + 1)
                    J.wait_taken(dve, (i, "inc"))
                    J.wait_taken(dve, (i, "ex"))
                    if i:
                        dve.tensor_tensor(w_inc[0:n, :], r_, w_inc[0:n, :], ALU.mult).then_inc(S("RT_src"), 1)
                    dve.wait_ge(S("kk_ready"), i + 1)
                    dve.tensor_tensor(w_ex[0:n, :], kk[0:n, :], w_ex[0:n, :], ALU.mult).then_inc(S("KT_src"), 1)
                    dve.wait_ge(S("rb_ready"), i + 1)
                    dve.tensor_reduce(bs[0:n, :], heads(bonus[0:n, :]), X, ALU.add).then_inc(S("bs_ready"), 1)
                    dve.tensor_tensor(kt[0:n, :], kt[0:n, :], w_inv[0:n, :], ALU.mult).then_inc(S("khT_src"), 1)
                    dve.wait_ge(S("b_ready"), i + 1)
                    dve.tensor_tensor(a[0:n, :], a[0:n, :], w_inv[0:n, :], ALU.mult).then_inc(S("BT_src"), 1)
                if s == "latent_keys":
                    for g in range(2):
                        bank = J.take(dve, (i, "kn", g))
                        J.taken(dve.tensor_copy(kTall[0:NOPE, 4 * g:4 * g + 4, t0:t0 + n], four(bank, n, NOPE)),
                                (i, "kn", g))
                if s == "turn_sides" and i:
                    bank = J.take(dve, (i, "RT"))
                    J.taken(dve.tensor_copy(RT[:, :, 0:n], four(bank, n, P)), (i, "RT"))
                if s == "turn":
                    if i:
                        for g in range(2):
                            bank = J.take(dve, (i, ("qT", g)))
                            J.taken(dve.tensor_copy(qT[:, 4 * g:4 * g + 4, :], four(bank, n, QH)), (i, ("qT", g)))
                    bank = J.take(dve, (i, "khT"))
                    J.taken(dve.tensor_copy(khT[:, :, 0:n], four(bank, n, P)), (i, "khT"))
                if s == "outer_a":
                    for name, dst, mask in (("A", IA, lower), ("AT", X0, upper)):
                        for g in range(2):
                            bank = J.take(dve, (i, name, g))
                            J.taken(dve.copy_predicated(dst[0:n, g:HEADS:2, 0:n], bc4(mask.bitcast(I32), n),
                                                        four(bank, n)), (i, name, g))
                masked = {"outer_c": ("C", F, upper), "outer_q": ("Q", PT, upper_eq), "outer_p": ("P", PT, upper_eq)}
                if s in masked:
                    name, dst, mask = masked[s]
                    for g in range(2):
                        bank = J.take(dve, (i, name, g))
                        J.taken(dve.tensor_tensor(dst[0:n, g:HEADS:2, 0:n], four(bank, n), bc4(mask, n),
                                                  ALU.mult), (i, name, g))
                if s == "newton_t":
                    for g in range(2):
                        bank = J.take(dve, (i, "T", v, g))
                        J.taken(dve.scalar_tensor_tensor(F[0:n, 4 * g:4 * g + 4, 0:n], four(bank, n), -1.0,
                                                         bc4(twice, n), ALU.mult, ALU.add), (i, "T", v, g))
                if s == "scan_sa":
                    R = slice(CHUNK * v, CHUNK * v + min(n, CHUNK))
                    bank = J.take(dve, (i, "SA", v))
                    J.taken(dve.tensor_copy(SA[R, :], bank[R, :]), (i, "SA", v))
                if s == "scan_s":
                    m = chunk_no(i, v)
                    if v == 0:
                        J.wait_taken(dve, (i, "total"))
                    bank = J.take(dve, (i, "S", v))
                    J.taken(dve.tensor_tensor(state[:, :, :], state[:, :, :],
                                              bank[:, 0:PAIRS * HD].rearrange("p (g v) -> p g v", g=PAIRS), ALU.add),
                            (i, "S", v))
                    J.wait_taken(dve, (i, "S", v))
                    dve.tensor_tensor(state[:, :, :], state[:, :, :],
                                      wl[:, :, v:v + 1].to_broadcast([P, PAIRS, HD]), ALU.mult)\
                       .then_inc(S("state_ready"), 1)
                    dve.wait_ge(S("state_ready"), m + 2)
                if s == "mean":
                    dve.wait_ge(S("y_out"), i)
                    step(dve.tensor_reduce(mu8[:, :], heads(SA[:, :]), X, ALU.add))
                    step(dve.tensor_scalar(mu8[:, :], mu8[:, :], 1.0 / HD, None, ALU.mult))
                    dve.tensor_tensor(heads(zr[:, :]), heads(SA[:, :]), bc(mu8, n), ALU.subtract)\
                       .then_inc(S("yc_ready"), 1)
                if s == "variance":
                    dve.wait_ge(S("ysq_ready"), i)
                    step(dve.tensor_reduce(v8[:, :], heads(SA[:, :]), X, ALU.add))
                    step(dve.tensor_scalar(v8[:, :], v8[:, :], 1.0 / HD, GN_EPS, ALU.mult, ALU.add))
                    rsqrt(dve, step, rs8[:, :], v8[:, :], t8[:, :])
                    dve.tensor_tensor(heads(zr[:, :]), heads(zr[:, :]), bc(rs8, n), ALU.mult).then_inc(S("yn_ready"), 1)
                if s == "gate_out":
                    dve.wait_ge(S("yg_ready"), i)
                    dve.wait_ge(S("bonus_ready"), i + 1)
                    step(dve.tensor_tensor(zr[:, :], zr[:, :], bonus[:, :], ALU.add))
                    if i == 1:
                        dve.wait_ge(S("vbd_ready"), 16 * HEADS)
                    else:
                        dve.wait_ge(S("mix_stored"), 16 * (i - 1))
                    J.wait_taken(dve, (i, "gate"))
                    dve.tensor_tensor(mixed[:, 0:W], zr[:, :], gate[:, :], ALU.mult).then_inc(S("rw_out"), 1)
                if s == "score":
                    m = HEADS * (i - 1) + v
                    if v == 0:
                        J.wait_taken(dve, (i, "sm"))
                        step(dve.tensor_reduce(mm[:, :], sm[:, :, :], X, ALU.max))
                    dve.wait_ge(S("scored"), m + 1)
                    step(dve.tensor_reduce(mxc[:, v:v + 1], SC[:, 0:P * i], X, ALU.max))
                    dve.tensor_scalar(nb[:, v:v + 1], mxc[:, v:v + 1], mm[:, v:v + 1], -SCALE, ALU.max, ALU.mult)\
                       .then_inc(S("nb_ready"), 1)
                if s == "merge":
                    dve.wait_ge(S("expm_done"), HEADS * i)
                    dve.tensor_tensor(den[:, :], rs[:, :], rsm[:, :], ALU.add).then_inc(S("den_ready"), 1)
                    dve.wait_ge(S("den_ready"), i)
                    step(dve.reciprocal(den[:, :], den[:, :]))
                    dve.wait_ge(S("o_ready"), i)
                    if i >= 2:
                        dve.wait_ge(S("mix_stored"), 16 * (i - 1))
                    dve.tensor_tensor(heads(mixed[:, W:2 * W]), heads(O[:, :]), bc(den, P), ALU.mult)\
                       .then_inc(S("o_out"), 1)
                if s == "finish":
                    dve.wait_ge(S("osq_ready"), i)
                    step(dve.tensor_scalar(ms[:, 2:3], ssq[:, 2:3], 1.0 / W, RMS_EPS, ALU.mult, ALU.add))
                    rsqrt(dve, step, rs2[:, 2:3], ms[:, 2:3], t2[:, 2:3])
                    dve.scalar_tensor_tensor(mixed[:, W:2 * W], mixed[:, W:2 * W], rs2[:, 2:3], M["mla_out_g"][:, :],
                                             ALU.mult, ALU.mult).then_inc(S("at_out"), 1)


KEYS = PAST + DEC_T
LEVELS_S = 3


def sample_steps():
    def plain(*names):
        return [(n, None) for n in names]

    def picks(a, b):
        return [("pick", v) for v in range(a, b)]

    def attend(v):
        return [("weights", v)], [("context", v)] + ([("score", v + 1)] if v + 1 < DEC_B else [])

    steps = plain("shift_diff", "norm", "shift", "turn_latent", "lora", "queries", "turn_lora", "key_squares", "key_norm",
                  "lora_up", "turn_queries", "keys", "decay", "absorb") + [("score", 0)]
    steps += plain("products", "turn") + attend(0)[0] + attend(0)[1]
    steps += picks(0, 2) + plain("gram") + picks(2, 4)
    for level in range(LEVELS_S):
        before, after = attend(level + 1)
        steps += [("newton_t", level)] + before + [("newton_x", level)] + after
        steps += picks(4 + 4 * level, 8 + 4 * level)
    before, after = attend(LEVELS_S + 1)
    steps += plain("pick_end", "scan_sa") + before + [("update", 0)] + after + plain("scan_y")
    for v in range(LEVELS_S + 2, DEC_B):
        before, after = attend(v)
        steps += before + [("update", v - LEVELS_S - 1)] + after + plain(("mean", "variance", "gate_out")[v - LEVELS_S - 2])
    return steps + plain("values")


def phase_mix_sample(nc, io, M):
    with ExitStack() as ctx:
        def sb(name, shape, dt=F32):
            return ctx.enter_context(nc.sbuf_tensor(name, shape, dt))

        def psum(name, shape):
            return ctx.enter_context(nc.psum_tensor(name, shape, F32))

        S = Semaphores(nc, io["semaphores"], "s_")
        B, T = DEC_B, DEC_T
        pr, table = sb("s_pr", [P, C_IN]), sb("s_table", [P, 2 * ROPE])
        prev = sb("s_prev", [P, 2 * HEADS * P])
        ctxT = prev[:, :].rearrange("p (k h b t) -> p k h b t", k=2, h=HEADS, b=B)
        la, lg = sb("s_la", [P, LORA]), sb("s_lg", [P, P])
        laT, lgT = sb("s_laT", [LORA + 1, 2, P]), sb("s_lgT", [P, P])
        td, a, gate, w_inc, w_inv, w_ex = (sb(f"s_{n}", [P, W]) for n in ("td", "a", "gate", "winc", "winv", "wex"))
        kk, kt, bonus, tmp = (sb(f"s_{n}", [P, W]) for n in ("kk", "kt", "bonus", "tmp"))
        wl = sb("s_wl", [P, PAIRS, B])
        KT, BT, khT, RT = (sb(f"s_{n}T", [P, PAIRS, P]) for n in ("K", "B", "kh", "R"))
        BTn = td[:, :].rearrange("p (k n) -> p k n", k=PAIRS)
        IA, X0, XA, F, PT = (sb(f"s_{n}", [P, HEADS, P]) for n in ("IA", "X0", "XA", "F", "PT"))
        zs, ys, SA = w_ex, w_inc, w_inv
        picked = sb("s_picked", [P, B, HD])
        spread = [F[:, 4 * i:4 * i + 4, :].rearrange("p h n -> p (h n)").rearrange("p (b v) -> p b v", b=B) for i in range(2)]
        state = sb("s_state", [P, PAIRS, B, HD])
        mixed, ssq = sb("s_mixed", [P, D]), sb("s_ssq", [P, 4])
        qn, c, kr, krt = sb("s_qn", [P, Q_LORA]), sb("s_c", [P, KV_LORA]), sb("s_kr", [P, ROPE]), sb("s_krt", [P, ROPE])
        q, qt = sb("s_q", [P, HEADS, QH]), sb("s_qt", [P, HEADS, ROPE])
        qnT = sb("s_qnT", [P, 3, P])
        both = sb("s_both", [QH, B * KEYS])
        wkT = both[0:NOPE, 0:HEADS * KV_LORA].rearrange("p (h l) -> p h l", h=HEADS)
        ropeT = both[NOPE:QH, :].rearrange("p (b n) -> p b n", b=B)
        qT = sb("s_qT", [QH, HEADS * P])
        qnopeT = qT[0:NOPE, :].rearrange("p (h n) -> p h n", h=HEADS)
        qropeT = qT[NOPE:QH, :].rearrange("p (b h t) -> p b h t", b=B, h=HEADS)
        qabsT = sb("s_qabsT", [P, 2, B, HEADS, T])
        latT = sb("s_latT", [P, 2, B, KEYS])
        lat, lat_new = sb("s_lat", [P, 2, B, KV_LORA]), sb("s_latnew", [T, B, KV_LORA])
        Pb = [sb(f"s_P{i}", [P, KEYS]) for i in range(2)]
        PTb = [sb(f"s_PTb{i}", [P, 3, P]) for i in range(2)]
        stat = sb("s_stat", [P, 64])
        n2, rk, t8, bs, mu8, v8, rs8, _ = (stat[:, 8 * m:8 * m + 8] for m in range(8))
        nb, rs = sb("s_nb", [P, B]), sb("s_rs", [P, B])
        ms, rs2, t2 = sb("s_ms", [P, 4]), sb("s_rs2", [P, 4]), sb("s_t2", [P, 4])
        O, Y, Z = psum("s_O", [P, 512]), psum("s_Y", [P, 512]), psum("s_Z", [P, 512])
        J = Jobs(S, [psum(f"s_R{i}", [P, 512]) for i in range(5)], "s")
        ident, twice = M["const"][:, C_IDENT, :], M["const"][:, C_TWICE, :]
        masks = sb("s_masks", [P, 3, P])
        lower, upper, upper_eq = (masks[:, m, :] for m in (C_LOWER, C_UPPER, C_UPPER_EQ))
        batch_of = M["ind"][:, 2:10].unsqueeze(2).to_broadcast([P, B, HD])
        r_, k_, v_ = (pr[:, W * m:W * m + W] for m in range(3))
        t0 = PROMPT
        block = ctx.enter_context(nc.Block())

        def bc(ap8):
            return ap8.unsqueeze(2).to_broadcast([P, HEADS, HD])

        def bc4(m):
            return m.unsqueeze(1).to_broadcast([P, 4, P])

        def four(bank, rows=P):
            return bank[0:rows, 0:4 * P].rearrange("p (k n) -> p k n", k=4)

        def state_banks():
            return [(x, odd, g) for x in range(2) for odd in range(2) for g in range(PAIRS)]

        def used(eng, h):
            if (h - 1) % 2 == 0:
                eng.wait_ge(S("SA_used"), (h - 1) // 2 + 1)
            else:
                eng.wait_ge(S("s_filled"), J.number[("S", (h - 1) // 2)] + 1)

        @block.tensor
        def _(pe):
            def turns(name, pieces, rows=P):
                bank = J.fill(pe, name)
                for out, src in pieces(bank):
                    last = pe.transpose(out, src, ident[0:rows, 0:rows])
                J.filled(last)

            for step, v in sample_steps():
                if step == "turn_latent":
                    pe.wait_ge(S("c_ready"), 1)
                    pe.wait_ge(S("kr_ready"), 1)
                    bank = J.fill(pe, "cT")
                    for k in range(2):
                        pe.transpose(bank[:, k * P:k * P + P], c[:, P * k:P * k + P], ident)
                    J.filled(pe.matmul(bank[NOPE:QH, 2 * P:3 * P], kr[:, :], ident, start=True, stop=True))
                    pe.wait_ge(S("qn_ready"), 1)
                    turns("qnT", lambda b: [(b[:, k * P:k * P + P], qn[:, P * k:P * k + P]) for k in range(3)])
                if step == "turn_lora":
                    pe.wait_ge(S("la_ready"), 2)
                    pe.wait_ge(S("shifted"), 1)
                    turns("loraT", lambda b: [(b[0:LORA, 0:P], la[:, :]),
                                              (b[0:LORA, P:2 * P], pr[:, 3 * W + LORA:3 * W + 2 * LORA]),
                                              (b[:, 2 * P:3 * P], lg[:, :])])
                if step == "lora_up":
                    pe.wait_ge(S("laT_out"), 1)
                    J.wait_taken(pe, "loraT")
                    pe.wait_ge(S("ones_set"), 1)
                    for name, lhs, rhs in (("dec", laT[:, 0, :], M["wdec"]), ("aaa", laT[:, 1, :], M["waaa"]),
                                           ("gate", lgT[:, :], M["wgate"])):
                        bank = J.fill(pe, name)
                        J.filled(pe.matmul(bank[:, :], lhs, rhs[:, :], start=True, stop=True))
                if step == "queries":
                    J.wait_taken(pe, "qnT")
                    for g in range(2):
                        bank = J.fill(pe, ("q", g))
                        for k in range(3):
                            last = pe.matmul(bank[:, 0:4 * QH], qnT[:, k, :], M["w_qb"][:, k, 4 * QH * g:4 * QH * (g + 1)],
                                             start=k == 0, stop=k == 2)
                        J.filled(last)
                if step == "decay":
                    pe.wait_ge(S("masks_landed"), 16)
                    J.wait_taken(pe, "dec")
                    for name, tri in (("inc", upper_eq), ("ex", upper)):
                        bank = J.fill(pe, name)
                        J.filled(pe.matmul(bank[:, :], tri, td[:, :], start=True, stop=True))
                    bank = J.fill(pe, "total")
                    for g in range(PAIRS):
                        last = pe.matmul(bank[:, B * g:B * g + B], td[:, P * g:P * g + P], M["ind"][:, 2:10],
                                         start=True, stop=True)
                    J.filled(last)
                if step == "turn":
                    for name, src in (("KT", w_ex), ("RT", w_inc), ("khT", kt), ("BT", a)):
                        pe.wait_ge(S(f"{name}_src"), 1)
                        turns(name, lambda b: [(b[:, k * P:k * P + P], src[:, P * k:P * k + P]) for k in range(4)])
                if step == "turn_queries":
                    pe.wait_ge(S("q_ready"), 1)
                    for g in range(2):
                        turns(("qT", g), lambda b: [(b[0:QH, k * P:k * P + P], q[:, 4 * g + k, :]) for k in range(4)])
                if step == "absorb":
                    pe.wait_ge(S("wkT_landed"), 16)
                    pe.wait_ge(S("qnope_out"), 2)
                    for k in range(2):
                        for g in range(2):
                            bank = J.fill(pe, ("abs", k, g))
                            for hh in range(4):
                                h = 4 * g + hh
                                last = pe.matmul(bank[:, P * hh:P * hh + P], wkT[:, h, P * k:P * k + P], qnopeT[:, h, :],
                                                 start=True, stop=True)
                            J.filled(last)
                if step == "gram":
                    pe.wait_ge(S("BTp_out"), 1)
                    for name in ("KT", "khT", "BT", "RT"):
                        J.wait_taken(pe, name)
                    for name, lhs, rhs in (("A", KT, BT), ("AT", BTn, KT), ("C", khT, KT), ("Q", khT, RT), ("P", BT, RT)):
                        for g in range(2):
                            bank = J.fill(pe, (name, g))
                            r = slice(HD * g, HD * g + HD)
                            for k in range(PAIRS):
                                last = pe.matmul(bank[:, k * P:k * P + P], lhs[r, k, :], rhs[r, k, :], start=True, stop=True)
                            J.filled(last)
                    for out, w, name in ((Z, F, "C"), (Y, XA, "Q")):
                        for g in range(2):
                            J.wait_taken(pe, (name, g))
                        for h in range(HEADS):
                            last = pe.matmul(out[:, HD * h:HD * h + HD], w[:, h, :], pr[:, 2 * W + HD * h:2 * W + HD * h + HD],
                                             start=h == 0, stop=name == "C", skip_group_check=True)
                        if name == "C":
                            last.then_inc(S("cv_done"), 1)
                    for g in range(2):
                        J.wait_taken(pe, ("A", g))
                        J.wait_taken(pe, ("AT", g))
                if step == "newton_t":
                    x = XA if v else X0
                    for g in range(2):
                        if v:
                            J.wait_taken(pe, ("X", v - 1, g))
                        bank = J.fill(pe, ("T", v, g))
                        for hh in range(4):
                            last = pe.matmul(bank[:, hh * P:hh * P + P], x[:, 4 * g + hh, :], IA[:, 4 * g + hh, :],
                                             start=True, stop=True)
                        J.filled(last)
                if step == "newton_x":
                    x = XA if v else X0
                    for g in range(2):
                        J.wait_taken(pe, ("T", v, g))
                        bank = J.fill(pe, ("X", v, g))
                        for hh in range(4):
                            last = pe.matmul(bank[:, hh * P:hh * P + P], F[:, 4 * g + hh, :], x[:, 4 * g + hh, :],
                                             start=True, stop=True)
                        J.filled(last)
                if step == "score":
                    if v == 0:
                        for k in range(2):
                            for g in range(2):
                                J.wait_taken(pe, ("abs", k, g))
                        for g in range(2):
                            J.wait_taken(pe, ("qT", g))
                        pe.wait_ge(S("latT_out"), 1)
                        J.wait_taken(pe, "cT")
                        pe.wait_ge(S("latT_landed"), 16 * 2)
                        pe.wait_ge(S("ropeT_landed"), 16)
                    bank = J.fill(pe, ("SC", v))
                    for k in range(2):
                        pe.matmul(bank[:, 0:KEYS], qabsT[:, k, v].rearrange("p h t -> p (h t)"), latT[:, k, v, :],
                                  start=k == 0, stop=False)
                    J.filled(pe.matmul(bank[:, 0:KEYS], qropeT[:, v].rearrange("p h t -> p (h t)"), ropeT[:, v, :],
                                       start=False, stop=True))
                if step == "pick":
                    x, odd, g = state_banks()[v]
                    if v == 0:
                        J.wait_taken(pe, "KT")
                        J.wait_taken(pe, "RT")
                        pe.wait_ge(S("state_landed"), 16 * PAIRS)
                    bank = J.fill(pe, ("pick", v))
                    r = slice(HD * odd, HD * odd + HD)
                    J.filled(pe.matmul(bank[:, :], (KT, RT)[x][r, g, :],
                                       state[r, g].rearrange("p b v -> p (b v)"), start=True, stop=True))
                if step == "scan_sa":
                    for g in range(2):
                        J.wait_taken(pe, ("X", LEVELS_S - 1, g))
                        J.wait_taken(pe, ("P", g))
                    pe.wait_ge(S("zr_ready"), 1)
                    bank = J.fill(pe, "SA")
                    for h in range(HEADS):
                        last = pe.matmul(bank[:, HD * h:HD * h + HD], XA[:, h, :], zs[:, HD * h:HD * h + HD],
                                         start=True, stop=True)
                    J.filled(last)
                if step == "scan_y":
                    J.wait_taken(pe, "SA")
                    for h in range(HEADS):
                        cols = slice(HD * h, HD * h + HD)
                        last = pe.matmul(Y[:, cols], PT[:, h, :], SA[:, cols], start=False, stop=True, skip_group_check=True)
                    last.then_inc(S("y_ready"), 1)
                if step == "update":
                    bank = J.fill(pe, ("S", v))
                    for odd in range(2):
                        h = 2 * v + odd
                        out, cols = bank[HD * odd:HD * odd + HD, :], slice(HD * h, HD * h + HD)
                        for m, (lhs, name) in enumerate(((kt, "V_spread"), (a, "SA_spread"))):
                            pe.wait_ge(S(name), h + 1)
                            last = pe.matmul(out, lhs[:, cols], spread[m][:, :, :].rearrange("p b v -> p (b v)"),
                                             start=m == 0, stop=m == 1)
                            if m == 0:
                                last.then_inc(S("V_used"), 1)
                        if odd == 0:
                            last.then_inc(S("SA_used"), 1)
                    J.filled(last)
                if step == "weights":
                    pe.wait_ge(S("p_normed"), v + 1)
                    bank = J.fill(pe, ("PT", v))
                    for k in range(2):
                        pe.transpose(bank[:, P * k:P * k + P], Pb[v % 2][:, P * k:P * k + P], ident)
                    J.filled(pe.transpose(bank[0:T, 2 * P:3 * P], Pb[v % 2][:, PAST:KEYS], ident))
                if step == "context":
                    J.wait_taken(pe, ("PT", v))
                    pe.wait_ge(S("lat_landed"), 32)
                    pe.wait_ge(S("latnew_landed"), 16 * B)
                    bank = J.fill(pe, ("ctx", v))
                    for k in range(2):
                        out, cols = bank[:, P * k:P * k + P], slice(P * k, P * k + P)
                        for m in range(2):
                            pe.matmul(out, lat[:, m, v, cols], PTb[v % 2][:, m, :], start=m == 0, stop=False)
                        last = pe.matmul(out, lat_new[:, v, cols], PTb[v % 2][0:T, 2, :], start=False, stop=True)
                    J.filled(last)
                if step == "values":
                    for m in range(B):
                        J.wait_taken(pe, ("ctx", m))
                    for h in range(HEADS):
                        col = 2 * HD * h + NOPE
                        for k in range(2):
                            last = pe.matmul(O[:, HD * h:HD * h + HD], ctxT[:, k, h].rearrange("p b t -> p (b t)"),
                                             M["w_kvb"][:, k, col:col + HD], start=k == 0, stop=k == 1)
                    last.then_inc(S("o_ready"), 1)

        @block.sync
        def _(sp):
            sp.dma_start(pr[:, :], io["p"][1 + t0:1 + t0 + P, :]).then_inc(S("pr_landed"), 16)
            sp.dma_start(prev[:, 0:C_RWKV], io["prev"]).then_inc(S("prev_landed"), 16)
            sp.dma_start(table[:, :], io["table"][t0:t0 + P, :]).then_inc(S("table_landed"), 16)
            sp.dma_start(masks[:, :, :], io["masks"].rearrange("m p n -> p m n")).then_inc(S("masks_landed"), 16)
            sp.dma_start(wkT, io["w_kT"].rearrange("(h n) l -> n h l", n=NOPE)).then_inc(S("wkT_landed"), 16)
            for k in range(2):
                sp.dma_start(latT[:, k, :, 0:PAST], io["cache_latT"][:, P * k:P * k + P, :].rearrange("b l n -> l b n"))\
                  .then_inc(S("latT_landed"), 16)
            sp.dma_start(ropeT[:, :, 0:PAST], io["cache_ropeT"].rearrange("b r n -> r b n")).then_inc(S("ropeT_landed"), 16)
            sp.dma_start(lat[:, 0, :, :],
                         io["cache_lat"][0, :, 0:P, :].rearrange("b n l -> n b l")).then_inc(S("lat_landed"), 16)
            sp.dma_start(lat[:, 1, :, :], io["cache_lat"][0, :, P:PAST, :].rearrange("b n l -> n b l"))\
              .then_inc(S("lat_landed"), 16)
            for g in range(PAIRS):
                sp.dma_start(state[:, g, :, :], io["state"][:, P * g:P * g + P, :].rearrange("b p v -> p b v"))\
                  .then_inc(S("state_landed"), 16)
            sp.wait_ge(S("c_ready"), 1)
            for b in range(B):
                sp.dma_start(lat_new[:, b, :], c[T * b:T * b + T, :]).then_inc(S("latnew_landed"), 16)
            sp.dma_start(io["o_lat_s"][0].rearrange("b t l -> (b t) l"), c[:, :]).then_inc(S("stored"), 16)
            sp.wait_ge(S("kr_ready"), 1)
            sp.dma_start(io["o_rope_s"][0].rearrange("b t r -> (b t) r"), kr[:, :]).then_inc(S("stored"), 16)
            for g in range(PAIRS):
                sp.wait_ge(S("state_new"), g + 1)
                sp.dma_start(io["o_state_s"][:, P * g:P * g + P, :].rearrange("b p v -> p b v"), state[:, g, :, :])\
                  .then_inc(S("stored"), 16)
            sp.wait_ge(S("rw_out"), 1)
            sp.wait_ge(S("at_out"), 1)
            sp.dma_start(io["mix"][SEQ:SEQ + P, :], mixed[:, :]).then_inc(S("stored"), 16)
            sp.wait_ge(S("stored"), 16 * (3 + PAIRS))

        @block.gpsimd
        def _(pool):
            step = Steps(pool, S("pool_step"))
            for s, v in sample_steps():
                if s == "shift_diff":
                    pool.wait_ge(S("sh_diff"), 1)
                    pool.tensor_tensor(prev[:, 0:C_RWKV], prev[:, 0:C_RWKV], M["mu"][:, :], ALU.mult).then_inc(S("sh_mu"), 1)
                if s == "norm":
                    pool.wait_ge(S("table_landed"), 16)
                    pool.wait_ge(S("pr_landed"), 16)
                    x = pr[:, C_IN - ROPE:C_IN]
                    step(pool.tensor_tensor(krt[:, 0:16], x[:, 16:32], table[:, ROPE:ROPE + 16], ALU.mult))
                    step(pool.tensor_tensor(krt[:, 16:32], x[:, 0:16], table[:, ROPE + 16:2 * ROPE], ALU.mult))
                    step(pool.tensor_tensor(kr[:, :], x, table[:, 0:ROPE], ALU.mult))
                    pool.tensor_tensor(kr[:, :], kr[:, :], krt[:, :], ALU.add).then_inc(S("kr_ready"), 1)
                if s == "lora_up":
                    J.wait_taken(pool, "aaa")
                    pool.tensor_scalar(a[:, :], a[:, :], 0.5, 0.5, ALU.mult, ALU.add).then_inc(S("a_ready"), 1)
                if s == "queries":
                    J.wait_taken(pool, ("q", 0))
                    J.wait_taken(pool, ("q", 1))
                    cos = table[:, 0:ROPE].unsqueeze(1).to_broadcast([P, HEADS, ROPE])
                    sa = table[:, ROPE:ROPE + 16].unsqueeze(1).to_broadcast([P, HEADS, 16])
                    sb_ = table[:, ROPE + 16:2 * ROPE].unsqueeze(1).to_broadcast([P, HEADS, 16])
                    step(pool.tensor_tensor(qt[:, :, 0:16], q[:, :, NOPE + 16:QH], sa, ALU.mult))
                    step(pool.tensor_tensor(qt[:, :, 16:32], q[:, :, NOPE:NOPE + 16], sb_, ALU.mult))
                    step(pool.tensor_tensor(q[:, :, NOPE:QH], q[:, :, NOPE:QH], cos, ALU.mult))
                    pool.tensor_tensor(q[:, :, NOPE:QH], q[:, :, NOPE:QH], qt[:, :, :], ALU.add).then_inc(S("q_ready"), 1)
                if s == "key_squares":
                    pool.wait_ge(S("shifted"), 1)
                    pool.tensor_tensor(kk[:, :], k_, M["k_k"][:, :], ALU.mult).then_inc(S("kk0_ready"), 1)
                if s == "keys":
                    pool.wait_ge(S("kt_ready"), 1)
                    step(pool.tensor_tensor(bonus[:, :], r_, kt[:, :], ALU.mult))
                    pool.tensor_tensor(bonus[:, :], bonus[:, :], M["r_k"][:, :], ALU.mult).then_inc(S("rb_ready"), 1)
                if s == "products":
                    pool.wait_ge(S("kk_ready"), 1)
                    pool.tensor_tensor(a[:, :], kk[:, :], a[:, :], ALU.mult).then_inc(S("b_ready"), 1)
                    pool.wait_ge(S("bs_ready"), 1)
                    step(pool.tensor_tensor(heads(bonus[:, :]), heads(v_), bc(bs), ALU.mult))
                    pool.tensor_tensor(bonus[:, :], bonus[:, :], M["gn_b"][:, :], ALU.add).then_inc(S("bonus_ready"), 1)
                if s == "update":
                    for h in range(2 * v, 2 * v + 2):
                        if h:
                            pool.wait_ge(S("V_used"), h)
                        else:
                            pool.wait_ge(S("s_filled"), J.number[("X", LEVELS_S - 1, 1)] + 1)
                        pool.tensor_tensor(spread[0][:, :, :], pr[:, 2 * W + HD * h:2 * W + HD * h + HD].unsqueeze(1)
                                           .to_broadcast([P, B, HD]), batch_of, ALU.mult).then_inc(S("V_spread"), 1)
                if s == "variance":
                    pool.wait_ge(S("yn_ready"), 1)
                    pool.tensor_tensor(td[:, :], td[:, :], M["gn_g"][:, :], ALU.mult).then_inc(S("yg_ready"), 1)

        @block.scalar
        def _(act):
            for s, v in sample_steps():
                if s == "norm":
                    act.wait_ge(S("pr_landed"), 16)
                    for m, (c0, width) in enumerate(((C_RWKV, Q_LORA), (C_RWKV + Q_LORA, KV_LORA))):
                        act.activation(tmp[:, 0:width], pr[:, c0:c0 + width], ACT.Square, accum_out=ssq[:, m:m + 1])\
                           .then_inc(S("ssq_ready"), 1)
                        act.wait_ge(S("ssq_ready"), m + 1)
                if s == "turn_latent":
                    bank = J.take(act, "cT")
                    for k in range(2):
                        last = act.activation(latT[:, k, :, PAST:KEYS],
                                              bank[:, P * k:P * k + P].rearrange("p (b t) -> p b t", b=B), ACT.Copy)
                    last.then_inc(S("latT_out"), 1)
                    J.taken(act.activation(ropeT[:, :, PAST:KEYS],
                                           bank[NOPE:QH, 2 * P:3 * P].rearrange("p (b t) -> p b t", b=B), ACT.Copy), "cT")
                    bank = J.take(act, "qnT")
                    J.taken(act.activation(qnT[:, :, :], bank[:, 0:3 * P].rearrange("p (k n) -> p k n", k=3), ACT.Copy), "qnT")
                if s == "lora":
                    act.wait_ge(S("shifted"), 1)
                    act.activation(la[:, :], pr[:, 3 * W:3 * W + LORA], ACT.Tanh).then_inc(S("la_ready"), 1)
                    act.activation(lg[:, :], pr[:, 3 * W + 2 * LORA:C_RWKV], ACT.Tanh, scale=0.5).then_inc(S("lg_tanh"), 1)
                    act.wait_ge(S("lg_tanh"), 1)
                    act.activation(lg[:, :], lg[:, :], ACT.Copy, scale=0.5, bias=0.5).then_inc(S("la_ready"), 1)
                if s == "turn_lora":
                    bank = J.take(act, "loraT")
                    act.activation(laT[0:LORA, :, :], bank[0:LORA, 0:2 * P].rearrange("p (k n) -> p k n", k=2),
                                   ACT.Copy).then_inc(S("laT_out"), 1)
                    J.taken(act.activation(lgT[:, :], bank[:, 2 * P:3 * P], ACT.Copy), "loraT")
                if s == "lora_up":
                    for name, dst in (("dec", td), ("aaa", a)):
                        bank = J.take(act, name)
                        J.taken(act.activation(dst[:, :], bank[:, :], ACT.Tanh, scale=0.5), name)
                    bank = J.take(act, "gate")
                    J.taken(act.activation(gate[:, :], bank[:, :], ACT.Copy), "gate")
                if s == "queries":
                    for g in range(2):
                        bank = J.take(act, ("q", g))
                        J.taken(act.activation(q[:, 4 * g:4 * g + 4, :],
                                               bank[:, 0:4 * QH].rearrange("p (h d) -> p h d", d=QH), ACT.Copy), ("q", g))
                if s == "decay":
                    bank = J.take(act, "inc")
                    act.activation(w_inc[:, :], bank[:, :], ACT.Exp, scale=HALF, bias=M["cvec"][:, 5:6])\
                       .then_inc(S("winc_ready"), 1)
                    J.taken(act.activation(w_inv[:, :], bank[:, :], ACT.Exp, scale=-HALF, bias=M["cvec"][:, 6:7]), "inc")
                    bank = J.take(act, "ex")
                    J.taken(act.activation(w_ex[:, :], bank[:, :], ACT.Exp, scale=HALF, bias=M["cvec"][:, 7:8]), "ex")
                    bank = J.take(act, "total")
                    J.taken(act.activation(wl[:, :, :], bank[:, 0:PAIRS * B].rearrange("p (g c) -> p g c", g=PAIRS), ACT.Exp,
                                           scale=HALF, bias=M["cvec"][:, 4:5]), "total")
                if s == "key_squares":
                    act.wait_ge(S("kk0_ready"), 1)
                    act.activation(tmp[:, :], kk[:, :], ACT.Square).then_inc(S("kksq_ready"), 1)
                if s == "turn":
                    bank = J.take(act, "KT")
                    J.taken(act.activation(KT[:, :, :], four(bank), ACT.Copy), "KT")
                    bank = J.take(act, "BT")
                    act.activation(BT[:, :, :], four(bank), ACT.Copy).then_inc(S("BTp_out"), 1)
                    J.taken(act.activation(BTn, four(bank), ACT.Copy, scale=-1.0), "BT")
                if s == "absorb":
                    for k in range(2):
                        for g in range(2):
                            bank = J.take(act, ("abs", k, g))
                            J.taken(act.activation(qabsT[:, k, :, 4 * g:4 * g + 4, :].rearrange("p b h t -> p h b t"),
                                                   bank[:, :].rearrange("p (h b t) -> p h b t", h=4, b=B), ACT.Copy),
                                    ("abs", k, g))
                if s == "newton_x":
                    for g in range(2):
                        bank = J.take(act, ("X", v, g))
                        if v == 0 and g == 0:
                            act.wait_ge(S("s_filled"), J.number[("T", 0, 0)] + 1)
                        J.taken(act.activation(XA[:, 4 * g:4 * g + 4, :], four(bank), ACT.Copy), ("X", v, g))
                if s == "score":
                    bank = J.take(act, ("SC", v))
                    act.wait_ge(S("nb_ready"), v + 1)
                    if v >= 2:
                        act.wait_ge(S("s_filled"), J.number[("PT", v - 2)] + 1)
                    J.taken(act.activation(Pb[v % 2][:, :], bank[:, 0:KEYS], ACT.Exp, scale=SCALE, bias=nb[:, v:v + 1],
                                           accum_out=rs[:, v:v + 1]), ("SC", v))
                if s == "context":
                    bank = J.take(act, ("ctx", v))
                    J.taken(act.activation(ctxT[:, :, :, v, :], bank[:, 0:2 * P].rearrange("p (k h t) -> p k h t", k=2, h=HEADS),
                                           ACT.Copy), ("ctx", v))
                if s == "mean":
                    act.wait_ge(S("y_sum"), 1)
                    act.wait_ge(S("yc_ready"), 1)
                    act.activation(tmp[:, :], td[:, :], ACT.Square).then_inc(S("ysq_ready"), 1)
                if s == "values":
                    act.wait_ge(S("o_ready"), 1)
                    act.activation(mixed[:, W:2 * W], O[:, :], ACT.Copy).then_inc(S("o_out"), 1)
                    act.wait_ge(S("ysq_ready"), 1)
                    act.wait_ge(S("yv_read"), 1)
                    act.activation(tmp[:, :], O[:, :], ACT.Square, accum_out=ssq[:, 2:3]).then_inc(S("osq_ready"), 1)

        @block.vector
        def _(dve):
            step = Steps(dve, S("dve_step"))
            dve.memset(laT[LORA:LORA + 1, :, :], 1.0).then_inc(S("ones_set"), 1)
            for m in (IA, X0):
                step(dve.tensor_copy(m[:, :, :], ident.unsqueeze(1).to_broadcast([P, HEADS, P])))
            for s, v in sample_steps():
                if s == "shift_diff":
                    dve.wait_ge(S("pr_landed"), 16)
                    dve.wait_ge(S("prev_landed"), 16)
                    dve.tensor_tensor(prev[:, 0:C_RWKV], prev[:, 0:C_RWKV], pr[:, 0:C_RWKV], ALU.subtract)\
                       .then_inc(S("sh_diff"), 1)
                if s == "shift":
                    dve.wait_ge(S("sh_mu"), 1)
                    dve.tensor_tensor(pr[:, 0:C_RWKV], pr[:, 0:C_RWKV], prev[:, 0:C_RWKV], ALU.add).then_inc(S("shifted"), 1)
                    dve.wait_ge(S("shifted"), 1)
                if s == "norm":
                    dve.wait_ge(S("ssq_ready"), 2)
                    step(dve.tensor_scalar(ms[:, 0:1], ssq[:, 0:1], 1.0 / Q_LORA, RMS_EPS, ALU.mult, ALU.add))
                    step(dve.tensor_scalar(ms[:, 1:2], ssq[:, 1:2], 1.0 / KV_LORA, RMS_EPS, ALU.mult, ALU.add))
                    rsqrt(dve, step, rs2[:, 0:2], ms[:, 0:2], t2[:, 0:2])
                    dve.scalar_tensor_tensor(c[:, :], pr[:, C_RWKV + Q_LORA:C_RWKV + Q_LORA + KV_LORA], rs2[:, 1:2],
                                             M["kv_norm_g"][:, :], ALU.mult, ALU.mult).then_inc(S("c_ready"), 1)
                    dve.scalar_tensor_tensor(qn[:, :], pr[:, C_RWKV:C_RWKV + Q_LORA], rs2[:, 0:1],
                                             M["q_norm_g"][:, :], ALU.mult, ALU.mult).then_inc(S("qn_ready"), 1)
                if s == "keys":
                    dve.wait_ge(S("a_ready"), 1)
                    step(dve.scalar_tensor_tensor(kt[:, :], a[:, :], -1.0, M["k_a"][:, :], ALU.add, ALU.mult))
                    dve.scalar_tensor_tensor(kt[:, :], kt[:, :], 1.0, k_, ALU.add, ALU.mult).then_inc(S("kt_ready"), 1)
                if s == "key_norm":
                    dve.wait_ge(S("kksq_ready"), 1)
                    step(dve.tensor_reduce(n2, heads(tmp[:, :]), X, ALU.add))
                    step(dve.tensor_scalar(n2, n2, 1e-24, None, ALU.max))
                    rsqrt(dve, step, rk, n2, t8)
                    dve.tensor_tensor(heads(kk[:, :]), heads(kk[:, :]), bc(rk), ALU.mult).then_inc(S("kk_ready"), 1)
                if s == "products":
                    dve.wait_ge(S("kt_ready"), 1)
                    dve.wait_ge(S("winc_ready"), 1)
                    J.wait_taken(dve, "inc")
                    J.wait_taken(dve, "ex")
                    dve.tensor_tensor(w_inc[:, :], r_, w_inc[:, :], ALU.mult).then_inc(S("RT_src"), 1)
                    dve.wait_ge(S("kk_ready"), 1)
                    dve.tensor_tensor(w_ex[:, :], kk[:, :], w_ex[:, :], ALU.mult).then_inc(S("KT_src"), 1)
                    dve.wait_ge(S("rb_ready"), 1)
                    dve.tensor_reduce(bs, heads(bonus[:, :]), X, ALU.add).then_inc(S("bs_ready"), 1)
                    dve.tensor_tensor(kt[:, :], kt[:, :], w_inv[:, :], ALU.mult).then_inc(S("khT_src"), 1)
                    dve.wait_ge(S("b_ready"), 1)
                    dve.tensor_tensor(a[:, :], a[:, :], w_inv[:, :], ALU.mult).then_inc(S("BT_src"), 1)
                if s == "turn":
                    for name, dst in (("RT", RT), ("khT", khT)):
                        bank = J.take(dve, name)
                        J.taken(dve.tensor_copy(dst[:, :, :], four(bank)), name)
                if s == "turn_queries":
                    for g in range(2):
                        bank = J.take(dve, ("qT", g))
                        dve.tensor_copy(qnopeT[:, 4 * g:4 * g + 4, :], four(bank, NOPE)).then_inc(S("qnope_out"), 1)
                        src = bank[NOPE:QH, :].rearrange("p (h b t) -> p h b t", h=4, b=B)
                        J.taken(dve.tensor_copy(qropeT[:, :, 4 * g:4 * g + 4, :].rearrange("p b h t -> p h b t"), src),
                                ("qT", g))
                if s == "gram":
                    dve.wait_ge(S("masks_landed"), 16)
                    for name, dst, mask in (("A", IA, lower), ("AT", X0, upper)):
                        for g in range(2):
                            bank = J.take(dve, (name, g))
                            J.taken(dve.copy_predicated(dst[:, g:HEADS:2, :], bc4(mask.bitcast(I32)), four(bank)), (name, g))
                    for name, dst, mask in (("C", F, upper), ("Q", XA, upper_eq), ("P", PT, upper_eq)):
                        for g in range(2):
                            bank = J.take(dve, (name, g))
                            J.taken(dve.tensor_tensor(dst[:, g:HEADS:2, :], four(bank), bc4(mask), ALU.mult), (name, g))
                if s == "newton_t":
                    for g in range(2):
                        bank = J.take(dve, ("T", v, g))
                        J.taken(dve.scalar_tensor_tensor(F[:, 4 * g:4 * g + 4, :], four(bank), -1.0, bc4(twice),
                                                         ALU.mult, ALU.add), ("T", v, g))
                if s == "score":
                    bank = J.take(dve, ("SC", v))
                    step(dve.tensor_reduce(nb[:, v:v + 1], bank[:, 0:KEYS], X, ALU.max))
                    dve.tensor_scalar(nb[:, v:v + 1], nb[:, v:v + 1], -SCALE, None, ALU.mult).then_inc(S("nb_ready"), 1)
                if s == "weights":
                    J.wait_taken(dve, ("SC", v))
                    step(dve.reciprocal(rs[:, v:v + 1], rs[:, v:v + 1]))
                    dve.tensor_scalar(Pb[v % 2][:, :], Pb[v % 2][:, :], rs[:, v:v + 1], None, ALU.mult)\
                       .then_inc(S("p_normed"), 1)
                    bank = J.take(dve, ("PT", v))
                    if v >= 2:
                        dve.wait_ge(S("s_filled"), J.number[("ctx", v - 2)] + 1)
                    step(dve.tensor_copy(PTb[v % 2][:, 0:2, :], bank[:, 0:2 * P].rearrange("p (k n) -> p k n", k=2)))
                    J.taken(dve.tensor_copy(PTb[v % 2][0:T, 2, :], bank[0:T, 2 * P:3 * P]), ("PT", v))
                if s == "pick":
                    x, odd, g = state_banks()[v]
                    bank = J.take(dve, ("pick", v))
                    J.taken(dve.tensor_tensor(picked[:, :, :], bank[:, :].rearrange("p (b v) -> p b v", b=B),
                                              batch_of, ALU.mult), ("pick", v))
                    J.wait_taken(dve, ("pick", v))
                    cols = slice(HD * (2 * g + odd), HD * (2 * g + odd) + HD)
                    step(dve.tensor_reduce((zs, ys)[x][:, cols], picked[:, :, :].rearrange("p b v -> p v b"),
                                           X, ALU.add))
                if s == "pick_end":
                    dve.wait_ge(S("cv_done"), 1)
                    dve.scalar_tensor_tensor(zs[:, :], Z[:, :], -1.0, zs[:, :], ALU.mult, ALU.subtract)\
                       .then_inc(S("zr_ready"), 1)
                if s == "scan_sa":
                    bank = J.take(dve, "SA")
                    J.taken(dve.tensor_copy(SA[:, :], bank[:, :]), "SA")
                    J.wait_taken(dve, "SA")
                if s == "update":
                    g = v
                    J.wait_taken(dve, "total")
                    for h in range(2 * g, 2 * g + 2):
                        if h:
                            used(dve, h)
                        dve.tensor_tensor(spread[1][:, :, :], SA[:, HD * h:HD * h + HD].unsqueeze(1)
                                          .to_broadcast([P, B, HD]), batch_of, ALU.mult).then_inc(S("SA_spread"), 1)
                    bank = J.take(dve, ("S", g))
                    J.taken(dve.tensor_tensor(state[:, g], state[:, g], bank[:, :].rearrange("p (b v) -> p b v", b=B),
                                              ALU.add), ("S", g))
                    J.wait_taken(dve, ("S", g))
                    dve.tensor_tensor(state[:, g], state[:, g], wl[:, g, :].unsqueeze(2).to_broadcast([P, B, HD]),
                                      ALU.mult).then_inc(S("state_new"), 1)
                if s == "mean":
                    dve.wait_ge(S("y_ready"), 1)
                    dve.tensor_tensor(ys[:, :], Y[:, :], ys[:, :], ALU.add).then_inc(S("y_sum"), 1)
                    dve.wait_ge(S("y_sum"), 1)
                    step(dve.tensor_reduce(mu8, heads(ys[:, :]), X, ALU.add))
                    step(dve.tensor_scalar(mu8, mu8, 1.0 / HD, None, ALU.mult))
                    dve.tensor_tensor(heads(td[:, :]), heads(ys[:, :]), bc(mu8), ALU.subtract).then_inc(S("yc_ready"), 1)
                if s == "variance":
                    dve.wait_ge(S("ysq_ready"), 1)
                    dve.tensor_reduce(v8, heads(tmp[:, :]), X, ALU.add).then_inc(S("yv_read"), 1)
                    dve.wait_ge(S("yv_read"), 1)
                    step(dve.tensor_scalar(v8, v8, 1.0 / HD, GN_EPS, ALU.mult, ALU.add))
                    rsqrt(dve, step, rs8, v8, t8)
                    dve.tensor_tensor(heads(td[:, :]), heads(td[:, :]), bc(rs8), ALU.mult).then_inc(S("yn_ready"), 1)
                if s == "gate_out":
                    dve.wait_ge(S("yg_ready"), 1)
                    dve.wait_ge(S("bonus_ready"), 1)
                    step(dve.tensor_tensor(td[:, :], td[:, :], bonus[:, :], ALU.add))
                    J.wait_taken(dve, "gate")
                    dve.tensor_tensor(mixed[:, 0:W], td[:, :], gate[:, :], ALU.mult).then_inc(S("rw_out"), 1)
                if s == "values":
                    dve.wait_ge(S("osq_ready"), 1)
                    dve.wait_ge(S("o_out"), 1)
                    step(dve.tensor_scalar(ms[:, 2:3], ssq[:, 2:3], 1.0 / W, RMS_EPS, ALU.mult, ALU.add))
                    rsqrt(dve, step, rs2[:, 2:3], ms[:, 2:3], t2[:, 2:3])
                    dve.scalar_tensor_tensor(mixed[:, W:2 * W], mixed[:, W:2 * W], rs2[:, 2:3], M["mla_out_g"][:, :],
                                             ALU.mult, ALU.mult).then_inc(S("at_out"), 1)


def constants():
    at = np.arange(P)
    const, masks = np.zeros((N_CONST, P, P), np.float32), np.zeros((3, P, P), np.float32)
    for m, size in ((const, CHUNK), (masks, DEC_T)):
        same = at[:, None] // size == at[None, :] // size
        m[C_LOWER] = same & (at[None, :] < at[:, None])
        m[C_UPPER] = same & (at[:, None] < at[None, :])
        m[C_UPPER_EQ] = same & (at[:, None] <= at[None, :])
    const[C_IDENT] = np.eye(P)
    const[C_TWICE] = 2 * np.eye(P)
    cvec = np.zeros((P, 8), np.float32)
    cvec[:, 0], cvec[:, 2] = HALF * (at % CHUNK + 1), HALF * (at % CHUNK)
    cvec[:, 1] = -cvec[:, 0]
    cvec[:, 3], cvec[:, 4] = HALF * CHUNK, HALF * META
    cvec[:, 5], cvec[:, 7] = HALF * (at % DEC_T + 1), HALF * (at % DEC_T)
    cvec[:, 6] = -cvec[:, 5]
    ind = np.zeros((P, 10), np.float32)
    ind[at, at // CHUNK] = 1
    ind[at, 2 + at // DEC_T] = 1
    rowpair = np.stack([np.where(at < CHUNK, -1e30, 0.0), np.where(at < CHUNK, 0.0, 1.0)]).astype(np.float32)
    pos = np.concatenate([np.arange(PROMPT), np.tile(PAST + np.arange(DEC_T), DEC_B)]).astype(np.float32)
    inv = (10000.0 ** (-np.arange(0, ROPE, 2, dtype=np.float32) / ROPE)).astype(np.float32)
    ang = pos[:, None] * inv[None, :]
    cos, sin = np.cos(ang), np.sin(ang)
    table = np.concatenate([cos, cos, -sin, sin], 1).astype(np.float32)
    return {"const": const, "masks": masks, "cvec": cvec, "ind": ind, "rowpair": rowpair, "table": table,
            "ident": np.eye(P, dtype=np.float32)}



OUTS = {
    "o_y_p": (1, SEQ, D), "o_y_s": (DEC_B, DEC_T, D),
    "o_lat_p": (1, 1, PROMPT, KV_LORA), "o_rope_p": (1, 1, PROMPT, ROPE), "o_state_p": (W, HD),
    "o_shift_p": (1, 1, 1, C_RWKV),
    "o_lat_s": (1, DEC_B, DEC_T, KV_LORA), "o_rope_s": (1, DEC_B, DEC_T, ROPE), "o_state_s": (DEC_B, W, HD),
    "o_shift_s": (1, DEC_B, 1, C_RWKV),
}
SCRATCH = {"h": (TOKENS, D), "p": (TOKENS + 1, C_IN), "prev": (SAMPLE, C_RWKV), "mix": (SEQ + SAMPLE, D)}


def build(nc, io):
    def cleared(run, *args):
        io["semaphores"] = []
        run(nc, io, *args)
        nc.clear_and_free_semaphores(io["semaphores"])
        nc.all_engine_barrier()

    with ExitStack() as ctx:
        def sb(name, shape, dt=F32):
            return ctx.enter_context(nc.sbuf_tensor(name, shape, dt))

        M = mix_weights(sb)
        cleared(phase_project, M)
        M.update(mix_weights_late(sb))
        cleared(phase_mix_prompt, M)
        cleared(phase_mix_sample, M)
    cleared(phase_mlp)


def kernel(**inputs):
    from concourse import bacc
    from concourse.bass_utils import run_bass_kernel_spmd

    arrays = {n: np.asarray(a) for n, a in inputs.items()}
    state, cache, rope = arrays.pop("state_rwkv"), arrays.pop("cache_mla_latent"), arrays.pop("cache_mla_rope")
    arrays["state"] = state[0].transpose(0, 1, 3, 2).reshape(DEC_B, W, HD)
    arrays["cache_lat"] = cache
    arrays["cache_latT"] = cache[0].transpose(0, 2, 1)
    arrays["cache_ropeT"] = rope[0].transpose(0, 2, 1)
    w_kvb = arrays["w_kvb"][0].reshape(KV_LORA, HEADS, 2 * HD)
    arrays["w_kT"] = w_kvb[:, :, 0:NOPE].transpose(1, 2, 0).reshape(HEADS * NOPE, KV_LORA)
    for n in ("ln1_g", "ln1_b", "ln2_g", "ln2_b"):
        arrays[n] = arrays[n][0]
    arrays.update(constants())
    arrays = {n: np.ascontiguousarray(a) for n, a in arrays.items()}

    nc = bacc.Bacc("TRN2", target_bir_lowering=False, num_devices=1)
    io = {n: nc.dram_tensor(n, a.shape, F32, kind="ExternalInput").ap() for n, a in arrays.items()}
    io.update({n: nc.dram_tensor(n, shape, F32, kind="ExternalOutput").ap() for n, shape in OUTS.items()})
    io.update({n: nc.dram_tensor(f"scratch_{n}", shape, F32, kind="Internal").ap() for n, shape in SCRATCH.items()})
    build(nc, io)
    got = dict(run_bass_kernel_spmd(nc, [arrays], core_ids=[0]).results[0])
    got["o_state_p"] = got["o_state_p"].reshape(1, 1, HEADS, HD, HD).transpose(0, 1, 2, 4, 3)
    got["o_state_s"] = got["o_state_s"].reshape(1, DEC_B, HEADS, HD, HD).transpose(0, 1, 2, 4, 3)
    return tuple(np.ascontiguousarray(got[n]) for n in OUTS)
```
